# Optimizing a Trainium2 kernel written in Bass

```python
import math
import jax, jax.numpy as jnp
from jax import lax
import numpy as np

D_MODEL = 1024
BATCH = 1
SEQ = 512
DEPTH = 1

D_MIX = D_MODEL
N_MIXERS = 4
GROUP_W = D_MIX // N_MIXERS
HEAD_DIM = 64
N_HEADS_G = GROUP_W // HEAD_DIM
SSD_STATE = 128
SSD_CONV = 4
SSD_CHUNK = 128
RWKV_DECAY_LORA = 32
RWKV_A_LORA = 32
RWKV_GATE_LORA = 64
RWKV_GN_EPS = 64e-5
GLA_DK = GROUP_W // 2
GLA_HEAD_K = GLA_DK // N_HEADS_G
GLA_GATE_LORA = 16
GLA_GATE_TAU = 16.0
GLA_CHUNK = 64
MLSTM_CONV = 4
MLSTM_CHUNK = 64
N_EXPERTS = 32
TOP_K = 4
D_EXPERT = D_MODEL
SWIGLU_LIMIT = 7.0
SWIGLU_ALPHA = 1.702
EXPERT_BLOCK = 128
PLE_DIM = 256
DEEPNORM_ALPHA = (2 * DEPTH) ** 0.25
DEEPNORM_BETA = (8 * DEPTH) ** -0.25
LN_EPS = 1e-5
NORM_EPS = 1e-5

SSD_SPLITS = (GROUP_W, GROUP_W, SSD_STATE, SSD_STATE, N_HEADS_G)
RWKV_SPLITS = (GROUP_W, GROUP_W, GROUP_W, RWKV_DECAY_LORA, RWKV_A_LORA, RWKV_GATE_LORA)
GLA_SPLITS = (GLA_DK, GLA_DK, GROUP_W, GLA_GATE_LORA, GROUP_W)
MLSTM_SPLITS = (GROUP_W, GROUP_W, GROUP_W, N_HEADS_G, N_HEADS_G, GROUP_W)
SSD_W = sum(SSD_SPLITS)
RWKV_W = sum(RWKV_SPLITS)
GLA_W = sum(GLA_SPLITS)
MLSTM_W = sum(MLSTM_SPLITS)
D_IN_PROJ = SSD_W + RWKV_W + GLA_W + MLSTM_W


def _split(u, sizes):
    idx = np.cumsum(sizes)[:-1].tolist()
    return jnp.split(u, idx, axis=-1)

def _causal_mask(n):
    return jnp.tril(jnp.ones((n, n), dtype=bool))

def _causal_dwconv(u, w, b):
    k, c = w.shape
    y = lax.conv_general_dilated(u, w[:, None, :].astype(u.dtype), window_strides=(1,),
                                 padding=[(k - 1, 0)], dimension_numbers=("NWC", "WIO", "NWC"),
                                 feature_group_count=c)
    return y + b

def _token_shift(u):
    return jnp.pad(u, ((0, 0), (1, 0), (0, 0)))[:, :-1]

def _heads(u, n_heads):
    return u.reshape(*u.shape[:-1], n_heads, u.shape[-1] // n_heads)

def _to_chunks(u, size):
    b, s, h = u.shape[:3]
    u = u.reshape(b, s // size, size, h, *u.shape[3:])
    return jnp.moveaxis(u, 3, 1)

def _from_chunks(y):
    y = jnp.moveaxis(y, 1, 3)
    return y.reshape(y.shape[0], y.shape[1] * y.shape[2], *y.shape[3:])

def _chunk_states(decay, contrib):
    d = jnp.moveaxis(decay, 2, 0)
    u = jnp.moveaxis(contrib, 2, 0)

    def step(s, inp):
        dc, uc = inp
        return dc * s + uc, s

    _, prev = lax.scan(step, jnp.zeros_like(u[0]), (d, u))
    return jnp.moveaxis(prev, 0, 2)

def _layer_norm(x, g, b):
    xf = x.astype(jnp.float32)
    mu = jnp.mean(xf, -1, keepdims=True)
    xc = xf - mu
    var = jnp.mean(xc * xc, -1, keepdims=True)
    return (xc * lax.rsqrt(var + LN_EPS) * g + b).astype(x.dtype)

def _group_norm(y, n_heads, gain, bias, eps, center):
    yf = _heads(y.astype(jnp.float32), n_heads)
    if center:
        yf = yf - jnp.mean(yf, -1, keepdims=True)
    yf = yf * lax.rsqrt(jnp.mean(yf * yf, -1, keepdims=True) + eps)
    yf = yf.reshape(y.shape) * gain
    if bias is not None:
        yf = yf + bias
    return yf

def _ssd_mixer(u, conv_w, conv_b, a_log, dt_bias, d_skip, norm_g):
    bsz, seq, _ = u.shape
    z, xr, bm, cm, dt = _split(u, SSD_SPLITS)
    xbc = jax.nn.silu(_causal_dwconv(jnp.concatenate([xr, bm, cm], -1), conv_w, conv_b))
    xs, bm, cm = _split(xbc, (GROUP_W, SSD_STATE, SSD_STATE))
    xs = _heads(xs, N_HEADS_G)
    dt = jax.nn.softplus(dt + dt_bias)
    nc = seq // SSD_CHUNK
    xc = _to_chunks(xs * dt[..., None], SSD_CHUNK)
    adt = _to_chunks(dt * (-jnp.exp(a_log)), SSD_CHUNK)
    bc = bm.reshape(bsz, nc, SSD_CHUNK, SSD_STATE)
    cc = cm.reshape(bsz, nc, SSD_CHUNK, SSD_STATE)
    acum = jnp.cumsum(adt, axis=-1)
    lmat = jnp.exp(jnp.where(_causal_mask(SSD_CHUNK), acum[..., :, None] - acum[..., None, :], -jnp.inf))
    y_diag = jnp.einsum("bcln,bcsn,bhcls,bhcsp->bhclp", cc, bc, lmat, xc)
    decay_states = jnp.exp(acum[..., -1:] - acum)
    states = jnp.einsum("bcsn,bhcs,bhcsp->bhcpn", bc, decay_states, xc)
    prev = _chunk_states(jnp.exp(acum[..., -1])[..., None, None], states)
    y_off = jnp.einsum("bcln,bhcpn,bhcl->bhclp", cc, prev, jnp.exp(acum))
    y = _from_chunks(y_diag + y_off) + xs * d_skip[:, None]
    y = y.reshape(bsz, seq, GROUP_W) * jax.nn.silu(z)
    return _group_norm(y, 1, norm_g, None, NORM_EPS, center=False)

def _rwkv7_mixer(u, mu, w0, w_up, a0, a_up, g_up, k_k, k_a, r_k, ln_g, ln_b):
    bsz, seq, _ = u.shape
    u = u + (_token_shift(u) - u) * mu
    r, k, v, wd, ad, gd = _split(u, RWKV_SPLITS)
    w = -jax.nn.softplus(-(w0 + jnp.tanh(wd) @ w_up)) - 0.5
    decay = jnp.exp(-jnp.exp(w))
    a = jax.nn.sigmoid(a0 + ad @ a_up)
    g = jax.nn.sigmoid(gd) @ g_up
    kk = _heads(k * k_k, N_HEADS_G)
    kk = kk / jnp.maximum(jnp.linalg.norm(kk, axis=-1, keepdims=True), 1e-12)
    k = k * (1.0 + (a - 1.0) * k_a)
    rh, wh, kh, vh, ah = (_heads(t, N_HEADS_G) for t in (r, decay, k, v, a))
    seq_major = [jnp.moveaxis(t, 1, 0) for t in (rh, wh, kh, vh, -kk, kk * ah)]

    def step(state, inp):
        r_t, w_t, k_t, v_t, a_t, b_t = inp
        sa = jnp.einsum("bhvk,bhk->bhv", state, a_t)
        state = (state * w_t[:, :, None, :] + sa[..., None] * b_t[:, :, None, :]
                 + v_t[..., None] * k_t[:, :, None, :])
        return state, jnp.einsum("bhvk,bhk->bhv", state, r_t)

    s0 = jnp.zeros((bsz, N_HEADS_G, HEAD_DIM, HEAD_DIM), rh.dtype)
    _, o = lax.scan(step, s0, tuple(seq_major))
    o = jnp.moveaxis(o, 0, 1).reshape(bsz, seq, GROUP_W)
    o = _group_norm(o, N_HEADS_G, ln_g, ln_b, RWKV_GN_EPS, center=True)
    bonus = jnp.sum(rh * kh * r_k, -1, keepdims=True) * vh
    return (o + bonus.reshape(bsz, seq, GROUP_W)) * g

def _gla_mixer(u, gate_up, gate_b, norm_g):
    bsz, seq, _ = u.shape
    q, k, v, gd, og = _split(u, GLA_SPLITS)
    log_a = jax.nn.log_sigmoid(gd @ gate_up + gate_b) / GLA_GATE_TAU
    qc = _to_chunks(_heads(q, N_HEADS_G), GLA_CHUNK) * GLA_HEAD_K ** -0.5
    kc = _to_chunks(_heads(k, N_HEADS_G), GLA_CHUNK)
    vc = _to_chunks(_heads(v, N_HEADS_G), GLA_CHUNK)
    bcum = jnp.cumsum(_to_chunks(_heads(log_a, N_HEADS_G), GLA_CHUNK), axis=3)
    q_dec = qc * jnp.exp(bcum)
    k_inv = kc * jnp.exp(-bcum)
    attn = jnp.where(_causal_mask(GLA_CHUNK), jnp.einsum("bhctd,bhcsd->bhcts", q_dec, k_inv), 0.0)
    o_intra = jnp.einsum("bhcts,bhcsv->bhctv", attn, vc)
    b_last = bcum[..., -1, :]
    contrib = jnp.einsum("bhcsd,bhcsv->bhcdv", kc * jnp.exp(b_last[..., None, :] - bcum), vc)
    prev = _chunk_states(jnp.exp(b_last)[..., None], contrib)
    o_inter = jnp.einsum("bhctd,bhcdv->bhctv", q_dec, prev)
    o = _from_chunks(o_intra + o_inter).reshape(bsz, seq, GROUP_W)
    return _group_norm(o, N_HEADS_G, norm_g, None, NORM_EPS, center=False) * jax.nn.silu(og)

def _mlstm_mixer(u, conv_w, conv_b, i_b, f_b, norm_g):
    bsz, seq, _ = u.shape
    q, k, v, ig, fg, og = _split(u, MLSTM_SPLITS)
    q, k = _split(jax.nn.silu(_causal_dwconv(jnp.concatenate([q, k], -1), conv_w, conv_b)), (GROUP_W, GROUP_W))
    qc = _to_chunks(_heads(q, N_HEADS_G), MLSTM_CHUNK) * HEAD_DIM ** -0.5
    kc = _to_chunks(_heads(k, N_HEADS_G), MLSTM_CHUNK)
    vc = _to_chunks(_heads(v, N_HEADS_G), MLSTM_CHUNK)
    i_pre = _to_chunks(ig + i_b, MLSTM_CHUNK)
    b = jnp.cumsum(_to_chunks(jax.nn.log_sigmoid(fg + f_b), MLSTM_CHUNK), axis=-1)
    b_last = b[..., -1]
    dmat = jnp.where(_causal_mask(MLSTM_CHUNK), b[..., :, None] - b[..., None, :] + i_pre[..., None, :], -jnp.inf)
    a_st = b_last[..., None] - b + i_pre
    m_loc = jnp.max(a_st, -1)
    w_st = jnp.exp(a_st - m_loc[..., None])
    c_contrib = jnp.einsum("bhcs,bhcsv,bhcsk->bhcvk", w_st, vc, kc)
    n_contrib = jnp.einsum("bhcs,bhcsk->bhck", w_st, kc)

    def step(carry, inp):
        c_s, n_s, m_s = carry
        bl, ml, cu, nu = inp
        m_new = jnp.maximum(bl + m_s, ml)
        s_old = jnp.exp(bl + m_s - m_new)
        s_new = jnp.exp(ml - m_new)
        c_new = s_old[..., None, None] * c_s + s_new[..., None, None] * cu
        n_new = s_old[..., None] * n_s + s_new[..., None] * nu
        return (c_new, n_new, m_new), (c_s, n_s, m_s)

    init = (jnp.zeros_like(c_contrib[:, :, 0]), jnp.zeros_like(n_contrib[:, :, 0]), jnp.zeros_like(b_last[:, :, 0]))
    xs = tuple(jnp.moveaxis(t, 2, 0) for t in (b_last, m_loc, c_contrib, n_contrib))
    _, (c_prev, n_prev, m_prev) = lax.scan(step, init, xs)
    c_prev, n_prev, m_prev = (jnp.moveaxis(t, 0, 2) for t in (c_prev, n_prev, m_prev))
    m_inter = b + m_prev[..., None]
    m_row = jnp.maximum(m_inter, jnp.max(dmat, -1))
    w_inter = jnp.exp(m_inter - m_row)
    scores = jnp.einsum("bhctk,bhcsk->bhcts", qc, kc) * jnp.exp(dmat - m_row[..., None])
    num = (w_inter[..., None] * jnp.einsum("bhcvk,bhctk->bhctv", c_prev, qc)
           + jnp.einsum("bhcts,bhcsv->bhctv", scores, vc))
    den = w_inter * jnp.einsum("bhck,bhctk->bhct", n_prev, qc) + jnp.sum(scores, -1)
    h = num / jnp.maximum(jnp.abs(den), jnp.exp(-m_row))[..., None]
    h = _from_chunks(h).reshape(bsz, seq, GROUP_W) * jax.nn.sigmoid(og)
    return _group_norm(h, N_HEADS_G, norm_g, None, NORM_EPS, center=True)

def _moe_ffn(x2d, router_w, router_b, w_gu, b_gu, w_down, b_down):
    t, d = x2d.shape
    n_assign = t * TOP_K
    logits = (x2d @ router_w + router_b).astype(jnp.float32)
    top_val, top_idx = lax.top_k(logits, TOP_K)
    gate = jax.nn.softmax(top_val, axis=-1)
    flat_e = top_idx.reshape(-1)
    flat_tok = jnp.arange(n_assign, dtype=jnp.int32) // TOP_K
    order = jnp.argsort(flat_e)
    e_s, tok_s, g_s = flat_e[order], flat_tok[order], gate.reshape(-1)[order]
    counts = jnp.zeros((N_EXPERTS,), jnp.int32).at[flat_e].add(1)
    padded = (counts + EXPERT_BLOCK - 1) // EXPERT_BLOCK * EXPERT_BLOCK
    start = jnp.cumsum(counts) - counts
    pend = jnp.cumsum(padded)
    pstart = pend - padded
    dest = pstart[e_s] + (jnp.arange(n_assign, dtype=jnp.int32) - start[e_s])
    n_blocks = (n_assign + N_EXPERTS * (EXPERT_BLOCK - 1) + EXPERT_BLOCK - 1) // EXPERT_BLOCK
    n_rows = n_blocks * EXPERT_BLOCK
    row_tok = jnp.full((n_rows,), t, jnp.int32).at[dest].set(tok_s)
    row_gate = jnp.zeros((n_rows,), jnp.float32).at[dest].set(g_s)
    block_expert = jnp.minimum(jnp.searchsorted(pend, jnp.arange(n_blocks) * EXPERT_BLOCK, side="right"),
                               N_EXPERTS - 1)
    x_pad = jnp.concatenate([x2d, jnp.zeros((1, d), x2d.dtype)], 0)
    xb = x_pad[row_tok].reshape(n_blocks, EXPERT_BLOCK, d)

    def expert_block(args):
        xblk, e = args
        hg, hl = jnp.split(xblk @ w_gu[e] + b_gu[e], 2, axis=-1)
        hg = jnp.minimum(hg, SWIGLU_LIMIT)
        hl = jnp.clip(hl, -SWIGLU_LIMIT, SWIGLU_LIMIT)
        glu = hg * jax.nn.sigmoid(hg * SWIGLU_ALPHA)
        return ((hl + 1.0) * glu) @ w_down[e] + b_down[e]

    yb = lax.map(expert_block, (xb, block_expert)).reshape(n_rows, d)
    y = (yb * row_gate[:, None]).astype(x2d.dtype)
    return jnp.zeros((t + 1, d), x2d.dtype).at[row_tok].add(y)[:t]

def first_inputs(seed: int = 0) -> dict:
    key = jax.random.key(seed)
    ks = iter(jax.random.split(key, 64))
    f32 = jnp.float32
    L, W, H = DEPTH, GROUP_W, N_HEADS_G

    def nrm(shape, scale):
        return scale * jax.random.normal(next(ks), shape, f32)

    def uni(shape, lo, hi):
        return jax.random.uniform(next(ks), shape, f32, lo, hi)

    dt0 = jnp.exp(uni((L, H), math.log(1e-3), math.log(1e-1)))
    return {
        "x": nrm((BATCH, SEQ, D_MODEL), 1.0),
        "p": nrm((DEPTH, BATCH, SEQ, PLE_DIM), 1.0),
        "w_in": nrm((L, D_MODEL, D_IN_PROJ), D_MODEL ** -0.5),
        "w_out": nrm((L, D_MIX, D_MODEL), DEEPNORM_BETA * D_MIX ** -0.5),
        "ln1_g": 1.0 + nrm((L, D_MODEL), 0.02),
        "ln1_b": nrm((L, D_MODEL), 0.02),
        "ssd_conv_w": nrm((L, SSD_CONV, W + 2 * SSD_STATE), SSD_CONV ** -0.5),
        "ssd_conv_b": nrm((L, W + 2 * SSD_STATE), 0.02),
        "ssd_a_log": jnp.log(uni((L, H), 1.0, 16.0)),
        "ssd_dt_bias": dt0 + jnp.log(-jnp.expm1(-dt0)),
        "ssd_d": 1.0 + nrm((L, H), 0.1),
        "ssd_norm_g": 1.0 + nrm((L, W), 0.02),
        "rwkv_mu": uni((L, RWKV_W), 0.0, 1.0),
        "rwkv_w0": uni((L, W), -6.0, -1.0),
        "rwkv_w_up": nrm((L, RWKV_DECAY_LORA, W), 0.5 * RWKV_DECAY_LORA ** -0.5),
        "rwkv_a0": nrm((L, W), 0.1),
        "rwkv_a_up": nrm((L, RWKV_A_LORA, W), RWKV_A_LORA ** -0.5),
        "rwkv_g_up": nrm((L, RWKV_GATE_LORA, W), RWKV_GATE_LORA ** -0.5),
        "rwkv_k_k": 0.85 + nrm((L, W), 0.02),
        "rwkv_k_a": 1.0 + nrm((L, W), 0.02),
        "rwkv_r_k": nrm((L, H, HEAD_DIM), 0.1),
        "rwkv_ln_g": 1.0 + nrm((L, W), 0.02),
        "rwkv_ln_b": nrm((L, W), 0.02),
        "gla_gate_up": nrm((L, GLA_GATE_LORA, GLA_DK), GLA_GATE_LORA ** -0.5),
        "gla_gate_b": nrm((L, GLA_DK), 0.1),
        "gla_norm_g": 1.0 + nrm((L, W), 0.02),
        "mlstm_conv_w": nrm((L, MLSTM_CONV, 2 * W), MLSTM_CONV ** -0.5),
        "mlstm_conv_b": nrm((L, 2 * W), 0.02),
        "mlstm_i_b": nrm((L, H), 0.1),
        "mlstm_f_b": uni((L, H), 3.0, 6.0),
        "mlstm_norm_g": 1.0 + nrm((L, W), 0.02),
        "router_w": nrm((L, D_MODEL, N_EXPERTS), D_MODEL ** -0.5),
        "router_b": nrm((L, N_EXPERTS), 0.01),
        "exp_w_gu": nrm((L, N_EXPERTS, D_MODEL, 2 * D_EXPERT), D_MODEL ** -0.5),
        "exp_b_gu": nrm((L, N_EXPERTS, 2 * D_EXPERT), 0.01),
        "exp_w_down": nrm((L, N_EXPERTS, D_EXPERT, D_MODEL), DEEPNORM_BETA * D_EXPERT ** -0.5),
        "exp_b_down": nrm((L, N_EXPERTS, D_MODEL), 0.01),
        "ple_gate_w": nrm((L, D_MODEL, D_MODEL), D_MODEL ** -0.5),
        "ple_proj": nrm((L, PLE_DIM, D_MODEL), DEEPNORM_BETA * PLE_DIM ** -0.5),
        "ln2_g": 1.0 + nrm((L, D_MODEL), 0.02),
        "ln2_b": nrm((L, D_MODEL), 0.02),
    }

def first_block(x, p, w_in, w_out, ln1_g, ln1_b,
              ssd_conv_w, ssd_conv_b, ssd_a_log, ssd_dt_bias, ssd_d, ssd_norm_g,
              rwkv_mu, rwkv_w0, rwkv_w_up, rwkv_a0, rwkv_a_up, rwkv_g_up, rwkv_k_k, rwkv_k_a,
              rwkv_r_k, rwkv_ln_g, rwkv_ln_b,
              gla_gate_up, gla_gate_b, gla_norm_g,
              mlstm_conv_w, mlstm_conv_b, mlstm_i_b, mlstm_f_b, mlstm_norm_g,
              router_w, router_b, exp_w_gu, exp_b_gu, exp_w_down, exp_b_down,
              ple_gate_w, ple_proj, ln2_g, ln2_b):
    bsz, seq, d = x.shape
    for i in range(DEPTH):
        u = (x @ w_in[i]).astype(jnp.float32)
        u_ssd, u_rwkv, u_gla, u_mlstm = _split(u, (SSD_W, RWKV_W, GLA_W, MLSTM_W))
        y_ssd = _ssd_mixer(u_ssd, ssd_conv_w[i], ssd_conv_b[i], ssd_a_log[i], ssd_dt_bias[i],
                           ssd_d[i], ssd_norm_g[i])
        y_rwkv = _rwkv7_mixer(u_rwkv, rwkv_mu[i], rwkv_w0[i], rwkv_w_up[i], rwkv_a0[i], rwkv_a_up[i],
                              rwkv_g_up[i], rwkv_k_k[i], rwkv_k_a[i], rwkv_r_k[i], rwkv_ln_g[i], rwkv_ln_b[i])
        y_gla = _gla_mixer(u_gla, gla_gate_up[i], gla_gate_b[i], gla_norm_g[i])
        y_mlstm = _mlstm_mixer(u_mlstm, mlstm_conv_w[i], mlstm_conv_b[i], mlstm_i_b[i], mlstm_f_b[i],
                               mlstm_norm_g[i])
        mix = jnp.concatenate([y_ssd, y_rwkv, y_gla, y_mlstm], -1).astype(x.dtype) @ w_out[i]
        x = _layer_norm(DEEPNORM_ALPHA * x + mix, ln1_g[i], ln1_b[i])
        ffn = _moe_ffn(x.reshape(bsz * seq, d), router_w[i], router_b[i], exp_w_gu[i], exp_b_gu[i],
                       exp_w_down[i], exp_b_down[i]).reshape(bsz, seq, d)
        h = DEEPNORM_ALPHA * x + ffn
        h = h + jax.nn.sigmoid(h @ ple_gate_w[i]) * (p[i] @ ple_proj[i])
        x = _layer_norm(h, ln2_g[i], ln2_b[i])
    return x


_first_inputs = first_inputs


def first_inputs(seed=0):
    import zlib

    import numpy as np

    out = dict(_first_inputs(seed))
    spreads = {}
    factors = {'ssd_conv_b': 4.119,
     'ssd_norm_g': 38.958,
     'rwkv_w_up': 7.026,
     'rwkv_a0': 5.308,
     'rwkv_k_k': 200.0,
     'rwkv_k_a': 74.503,
     'rwkv_ln_g': 84.375,
     'rwkv_ln_b': 101.95,
     'gla_gate_b': 3.936,
     'gla_norm_g': 74.663,
     'mlstm_conv_b': 4.018,
     'mlstm_i_b': 200.0,
     'mlstm_norm_g': 16.851,
     'router_b': 3.315,
     'exp_b_gu': 8.0,
     'exp_b_down': 8.0,
     'ln2_g': 20.412,
     'ln2_b': 19.305}
    for name, (base, spread) in spreads.items():
        noise = np.random.default_rng([zlib.crc32(name.encode()), seed]).standard_normal(out[name].shape)
        drawn = base * np.exp(spread * noise) if base else spread * noise
        out[name] = __import__('jax').numpy.asarray(drawn.astype(out[name].dtype))
    for name, factor in factors.items():
        out[name] = (out[name] * factor).astype(out[name].dtype)
    return out


_narrow_inputs = first_inputs


def first_inputs(seed=0):

    out = dict(_narrow_inputs(seed))
    wider = {'ssd_norm_g': 3.26,
     'rwkv_k_k': 4.65,
     'gla_norm_g': 3.2,
     'mlstm_i_b': 12.0,
     'mlstm_norm_g': 8.43,
     'ln2_g': 3.07,
     'ln2_b': 3.07}
    for name, times in wider.items():
        mean = out[name].mean()
        out[name] = (mean + times * (out[name] - mean)).astype(out[name].dtype)
    return out


DEPTH_2 = 2

N_MEM = 256
DA_HEADS = 4
DA_HEAD_DIM = 64
DA_V_DIM = 2 * DA_HEAD_DIM
DA_WIDTH = DA_HEADS * DA_V_DIM
HG_HEADS = 4
HG_DK = 128
HG_DV = 128
HG_WIDTH = HG_HEADS * HG_DV
HG_CHUNK = 64
HG_MIN_FORGET = 1e-20
MX_HEADS = 4
MX_HEAD_DIM = 128
MX_WIDTH = MX_HEADS * MX_HEAD_DIM
MIX_WIDTH = DA_WIDTH + HG_WIDTH + MX_WIDTH
IN_WIDTHS = (
    DA_HEADS * 2 * DA_HEAD_DIM,
    DA_HEADS * 2 * DA_HEAD_DIM,
    DA_WIDTH,
    HG_HEADS * HG_DK,
    HG_HEADS * HG_DK,
    HG_HEADS * HG_DK,
    HG_WIDTH,
    HG_WIDTH,
    MX_WIDTH,
)
IN_WIDTH = 4608
ROPE_THETA = 500000.0
ROPE_DIM = DA_HEAD_DIM // 4
Q_BLOCK = 128
D_FF = 2816
CONV_W = 3
RMS_EPS = 1e-6
DEEPNORM_ALPHA_2 = (2 * DEPTH_2) ** 0.25
DEEPNORM_BETA_2 = (8 * DEPTH_2) ** -0.25


def layer_norm(x, g, b):
    xf = x.astype(jnp.float32)
    mu = jnp.mean(xf, axis=-1, keepdims=True)
    var = jnp.mean(jnp.square(xf - mu), axis=-1, keepdims=True)
    y = (xf - mu) * lax.rsqrt(var + LN_EPS)
    return (y * g.astype(jnp.float32) + b.astype(jnp.float32)).astype(x.dtype)

def rms_norm(x, g):
    xf = x.astype(jnp.float32)
    y = xf * lax.rsqrt(jnp.mean(jnp.square(xf), axis=-1, keepdims=True) + RMS_EPS)
    return (y * g.astype(jnp.float32)).astype(x.dtype)

def rope_partial(t, cos, sin):
    half = ROPE_DIM // 2
    t1 = t[..., :half]
    t2 = t[..., half:ROPE_DIM]
    return jnp.concatenate([t1 * cos - t2 * sin, t2 * cos + t1 * sin, t[..., ROPE_DIM:]], axis=-1)

def diff_attention(q, k, v, lam):
    B, S, H = q.shape[:3]
    nblk = S // Q_BLOCK
    qb = q.reshape(B, nblk, Q_BLOCK, H, 2, DA_HEAD_DIM).transpose(1, 0, 2, 3, 4, 5)

    def one_block(qi):
        s = jnp.einsum('bqhcd,bkhcd->bhcqk', qi, k).astype(jnp.float32)
        p = jax.nn.softmax(s, axis=-1)
        a = p[:, :, 0] - lam * p[:, :, 1]
        return jnp.einsum('bhqk,bkhv->bqhv', a.astype(v.dtype), v)

    o = lax.map(one_block, qb)
    return o.transpose(1, 0, 2, 3, 4).reshape(B, S, H, DA_V_DIM)

def hgrn2_chunk_scan(q, k, v, g):
    B, S, H, dk = q.shape
    dv = v.shape[-1]
    n = S // HG_CHUNK

    def to_chunks(t):
        return t.reshape(B, n, HG_CHUNK, H, t.shape[-1]).transpose(1, 0, 3, 2, 4)

    qc, kc, vc, gc = to_chunks(q), to_chunks(k), to_chunks(v), to_chunks(g)
    bc = jnp.cumsum(gc, axis=3)
    mask = jnp.tril(jnp.ones((HG_CHUNK, HG_CHUNK), dtype=bool))[:, :, None]

    def step(state, inp):
        qt, kt, vt, bt = inp
        o_inter = jnp.einsum('bhtk,bhkv->bhtv', qt * jnp.exp(bt), state)
        diff = bt[:, :, :, None, :] - bt[:, :, None, :, :]
        dec = jnp.where(mask, jnp.exp(jnp.where(mask, diff, 0.0)), 0.0)
        attn = jnp.einsum('bhtk,bhtsk->bhts', qt, dec * kt[:, :, None, :, :])
        o_intra = jnp.einsum('bhts,bhsv->bhtv', attn, vt)
        b_last = bt[:, :, -1:, :]
        state = jnp.exp(b_last[:, :, 0, :])[..., None] * state + jnp.einsum(
            'bhsk,bhsv->bhkv', kt * jnp.exp(b_last - bt), vt)
        return state, o_inter + o_intra

    s0 = jnp.zeros((B, H, dk, dv), jnp.float32)
    _, o = lax.scan(step, s0, (qc, kc, vc, bc))
    return o.transpose(1, 0, 3, 2, 4).reshape(B, S, H, dv)

def hgrn_lower_bound(lb_logits, layer):
    p = jax.nn.softmax(lb_logits.astype(jnp.float32), axis=0)
    return (jnp.cumsum(p, axis=0) - p[0])[layer]

def hgrn_log_forget(z, lb):
    f = lb + (1.0 - lb) * jax.nn.sigmoid(z)
    return jnp.log(jnp.maximum(f, HG_MIN_FORGET))

def memory_attention(q, mk, mv):
    s = jnp.einsum('bqhd,bmhd->bhqm', q * (MX_HEAD_DIM ** -0.5), mk).astype(jnp.float32)
    p = jax.nn.softmax(s, axis=-1)
    return jnp.einsum('bhqm,bmhd->bqhd', p.astype(mv.dtype), mv)

def depthwise_conv_centred(u, w, b):
    y = lax.conv_general_dilated(
        u, w[:, None, :].astype(u.dtype), window_strides=(1,),
        padding=((CONV_W // 2, CONV_W // 2),),
        dimension_numbers=('NWC', 'WIO', 'NWC'),
        feature_group_count=u.shape[-1])
    return y + b.astype(u.dtype)

def hybrid_layer(x, mem, cos, sin, layer, w_in, da_lambda, da_norm_g, hg_lb_fwd, hg_lb_bwd,
                 hg_norm_g, w_mem_kv, w_out, ln1_g, ln1_b, w_up, conv_w, conv_b, w_down,
                 ln2_g, ln2_b):
    B, S, _ = x.shape
    M = mem.shape[1]
    proj = x @ w_in
    split_idx = [int(i) for i in np.cumsum(IN_WIDTHS)[:-1]]
    da_q, da_k, da_v, hg_q, hg_ff, hg_fb, hg_i, hg_g, mx_q = jnp.split(proj, split_idx, axis=-1)

    dq = rope_partial(da_q.reshape(B, S, DA_HEADS, 2, DA_HEAD_DIM), cos, sin) * (DA_HEAD_DIM ** -0.5)
    dk = rope_partial(da_k.reshape(B, S, DA_HEADS, 2, DA_HEAD_DIM), cos, sin)
    dv = da_v.reshape(B, S, DA_HEADS, DA_V_DIM)
    lam_init = 0.8 - 0.6 * math.exp(-0.3 * layer)
    lf = da_lambda.astype(jnp.float32)
    lam = jnp.exp(jnp.sum(lf[0] * lf[1])) - jnp.exp(jnp.sum(lf[2] * lf[3])) + lam_init
    da_o = diff_attention(dq, dk, dv, lam)
    da_o = (rms_norm(da_o, da_norm_g) * (1.0 - lam_init)).reshape(B, S, DA_WIDTH)

    f32 = jnp.float32
    hq = jax.nn.silu(hg_q.reshape(B, S, HG_HEADS, HG_DK).astype(f32))
    hv = hg_i.reshape(B, S, HG_HEADS, HG_DV).astype(f32)
    lb_f = hgrn_lower_bound(hg_lb_fwd, layer).reshape(HG_HEADS, HG_DK)
    lb_b = hgrn_lower_bound(hg_lb_bwd, layer).reshape(HG_HEADS, HG_DK)
    g_f = hgrn_log_forget(hg_ff.reshape(B, S, HG_HEADS, HG_DK).astype(f32), lb_f)
    g_b = hgrn_log_forget(hg_fb.reshape(B, S, HG_HEADS, HG_DK).astype(f32), lb_b)
    o_fwd = hgrn2_chunk_scan(hq, -jnp.expm1(g_f), hv, g_f)
    o_bwd = jnp.flip(hgrn2_chunk_scan(jnp.flip(hq, 1), jnp.flip(-jnp.expm1(g_b), 1),
                                      jnp.flip(hv, 1), jnp.flip(g_b, 1)), 1)
    hg_o = (o_fwd + o_bwd).astype(x.dtype)
    hg_gate = jax.nn.silu(hg_g.reshape(B, S, HG_HEADS, HG_DV))
    hg_o = (rms_norm(hg_o, hg_norm_g) * hg_gate).reshape(B, S, HG_WIDTH)

    mkv = (mem @ w_mem_kv).reshape(B, M, 2, MX_HEADS, MX_HEAD_DIM)
    mx_o = memory_attention(mx_q.reshape(B, S, MX_HEADS, MX_HEAD_DIM), mkv[:, :, 0], mkv[:, :, 1])
    mx_o = mx_o.reshape(B, S, MX_WIDTH)

    mix = jnp.concatenate([da_o, hg_o, mx_o], axis=-1) @ w_out
    x = layer_norm(DEEPNORM_ALPHA_2 * x + mix, ln1_g, ln1_b)

    u = depthwise_conv_centred(x @ w_up, conv_w, conv_b)
    gate, val = jnp.split(u, 2, axis=-1)
    ffn = (jax.nn.silu(gate) * val) @ w_down
    return layer_norm(DEEPNORM_ALPHA_2 * x + ffn, ln2_g, ln2_b)

def second_inputs(seed: int = 0) -> dict:
    key = jax.random.key(seed)
    ks = jax.random.split(key, 24)
    nrm = jax.random.normal
    D = D_MODEL
    x = nrm(ks[0], (BATCH, SEQ, D), jnp.float32)
    mem = nrm(ks[1], (BATCH, N_MEM, D), jnp.float32)
    offsets = jax.random.randint(ks[2], (BATCH, 1), 0, 1024, dtype=jnp.int32)
    positions = (jnp.arange(SEQ, dtype=jnp.int32)[None, :] + offsets).astype(jnp.int32)
    return {
        "x": x,
        "mem": mem,
        "positions": positions,
        "ln_in_g": 1.0 + 0.02 * nrm(ks[3], (D,), jnp.float32),
        "ln_in_b": 0.02 * nrm(ks[4], (D,), jnp.float32),
        "w_in": nrm(ks[5], (DEPTH_2, D, IN_WIDTH), jnp.float32) * D ** -0.5,
        "da_lambda": 0.1 * nrm(ks[6], (DEPTH_2, 4, DA_HEAD_DIM), jnp.float32),
        "da_norm_g": 1.0 + 0.02 * nrm(ks[7], (DEPTH_2, DA_V_DIM), jnp.float32),
        "hg_lb_fwd": 0.5 * nrm(ks[8], (DEPTH_2, HG_HEADS * HG_DK), jnp.float32),
        "hg_lb_bwd": 0.5 * nrm(ks[9], (DEPTH_2, HG_HEADS * HG_DK), jnp.float32),
        "hg_norm_g": 1.0 + 0.02 * nrm(ks[10], (DEPTH_2, HG_DV), jnp.float32),
        "w_mem_kv": nrm(ks[11], (DEPTH_2, D, 2 * MX_WIDTH), jnp.float32) * D ** -0.5,
        "w_out": nrm(ks[12], (DEPTH_2, MIX_WIDTH, D), jnp.float32) * (MIX_WIDTH ** -0.5 * DEEPNORM_BETA_2),
        "ln1_g": 1.0 + 0.02 * nrm(ks[13], (DEPTH_2, D), jnp.float32),
        "ln1_b": 0.02 * nrm(ks[14], (DEPTH_2, D), jnp.float32),
        "w_up": nrm(ks[15], (DEPTH_2, D, 2 * D_FF), jnp.float32) * D ** -0.5,
        "conv_w": nrm(ks[16], (DEPTH_2, CONV_W, 2 * D_FF), jnp.float32) * CONV_W ** -0.5,
        "conv_b": 0.02 * nrm(ks[17], (DEPTH_2, 2 * D_FF), jnp.float32),
        "w_down": nrm(ks[18], (DEPTH_2, D_FF, D), jnp.float32) * (D_FF ** -0.5 * DEEPNORM_BETA_2),
        "ln2_g": 1.0 + 0.02 * nrm(ks[19], (DEPTH_2, D), jnp.float32),
        "ln2_b": 0.02 * nrm(ks[20], (DEPTH_2, D), jnp.float32),
    }

def second_block(x, mem, positions, ln_in_g, ln_in_b, w_in, da_lambda, da_norm_g, hg_lb_fwd,
              hg_lb_bwd, hg_norm_g, w_mem_kv, w_out, ln1_g, ln1_b, w_up, conv_w, conv_b,
              w_down, ln2_g, ln2_b):
    inv_freq = ROPE_THETA ** (-jnp.arange(0, ROPE_DIM, 2, dtype=jnp.float32) / ROPE_DIM)
    ang = positions.astype(jnp.float32)[..., None] * inv_freq
    cos = jnp.cos(ang)[:, :, None, None, :].astype(x.dtype)
    sin = jnp.sin(ang)[:, :, None, None, :].astype(x.dtype)

    h = layer_norm(x, ln_in_g, ln_in_b)
    for l in range(DEPTH_2):
        h = hybrid_layer(h, mem, cos, sin, l, w_in[l], da_lambda[l], da_norm_g[l],
                         hg_lb_fwd, hg_lb_bwd, hg_norm_g[l], w_mem_kv[l], w_out[l],
                         ln1_g[l], ln1_b[l], w_up[l], conv_w[l], conv_b[l], w_down[l],
                         ln2_g[l], ln2_b[l])
    return h


def setup_inputs(seed=0):
    out = dict(first_inputs(seed))
    for name, value in second_inputs(seed + 1).items():
        if name != "x":
            out[name + "_2"] = value
    return out


def reference(
    x, p, w_in, w_out, ln1_g, ln1_b, ssd_conv_w, ssd_conv_b, ssd_a_log, ssd_dt_bias, ssd_d,
    ssd_norm_g, rwkv_mu, rwkv_w0, rwkv_w_up, rwkv_a0, rwkv_a_up, rwkv_g_up, rwkv_k_k, rwkv_k_a,
    rwkv_r_k, rwkv_ln_g, rwkv_ln_b, gla_gate_up, gla_gate_b, gla_norm_g, mlstm_conv_w,
    mlstm_conv_b, mlstm_i_b, mlstm_f_b, mlstm_norm_g, router_w, router_b, exp_w_gu, exp_b_gu,
    exp_w_down, exp_b_down, ple_gate_w, ple_proj, ln2_g, ln2_b, mem_2, positions_2, ln_in_g_2,
    ln_in_b_2, w_in_2, da_lambda_2, da_norm_g_2, hg_lb_fwd_2, hg_lb_bwd_2, hg_norm_g_2,
    w_mem_kv_2, w_out_2, ln1_g_2, ln1_b_2, w_up_2, conv_w_2, conv_b_2, w_down_2, ln2_g_2,
    ln2_b_2,
):
    x = first_block(
        x, p, w_in, w_out, ln1_g, ln1_b, ssd_conv_w, ssd_conv_b, ssd_a_log, ssd_dt_bias, ssd_d,
        ssd_norm_g, rwkv_mu, rwkv_w0, rwkv_w_up, rwkv_a0, rwkv_a_up, rwkv_g_up, rwkv_k_k,
        rwkv_k_a, rwkv_r_k, rwkv_ln_g, rwkv_ln_b, gla_gate_up, gla_gate_b, gla_norm_g,
        mlstm_conv_w, mlstm_conv_b, mlstm_i_b, mlstm_f_b, mlstm_norm_g, router_w, router_b,
        exp_w_gu, exp_b_gu, exp_w_down, exp_b_down, ple_gate_w, ple_proj, ln2_g, ln2_b,
    )
    return second_block(
        x, mem_2, positions_2, ln_in_g_2, ln_in_b_2, w_in_2, da_lambda_2, da_norm_g_2,
        hg_lb_fwd_2, hg_lb_bwd_2, hg_norm_g_2, w_mem_kv_2, w_out_2, ln1_g_2, ln1_b_2, w_up_2,
        conv_w_2, conv_b_2, w_down_2, ln2_g_2, ln2_b_2,
    )


_drawn_inputs = setup_inputs


def setup_inputs(seed=0):
    import zlib

    import numpy as np

    out = dict(_drawn_inputs(seed))
    spreads = {}
    factors = {'mlstm_i_b': 8.0,
     'da_lambda_2': 3.295,
     'da_norm_g_2': 21.443,
     'hg_lb_fwd_2': 8.0,
     'hg_lb_bwd_2': 8.0,
     'hg_norm_g_2': 29.585,
     'conv_b_2': 6.618,
     'mem_2': 3.163,
     'w_mem_kv_2': 3.192}
    for name, (base, spread) in spreads.items():
        noise = np.random.default_rng([zlib.crc32(name.encode()), seed]).standard_normal(out[name].shape)
        drawn = base * np.exp(spread * noise) if base else spread * noise
        out[name] = __import__('jax').numpy.asarray(drawn.astype(out[name].dtype))
    for name, factor in factors.items():
        out[name] = (out[name] * factor).astype(out[name].dtype)
    return out
```

```python
from contextlib import ExitStack, contextmanager

import numpy as np
import concourse.bass as bass
from concourse import mybir

F32 = mybir.dt.float32
I32 = mybir.dt.int32
ALU = mybir.AluOpType
ACT = mybir.ActivationFunctionType
AX = mybir.AxisListType

P = 128
S = 512
NT = S // P
D = 1024
DT = D // P
H = 4
EXPERTS, TOP_K, FE = 32, 4, 1024
FF = 2816
FT = FF // P
MEM = 256
PLE = 256
ALPHA1 = 2 ** 0.25
ALPHA2 = 4 ** 0.25
SWIGLU_LIMIT, SWIGLU_ALPHA = 7.0, 1.702
HALVES = [1, 2, 4, 8, 16, 32, 64]

Z, XR, BM, CM = 0, 2, 4, 5
R_, K_, V_, LORA = 6, 8, 10, 12
GQ, GK, GV, GOG = 13, 14, 15, 17
MQ, MK, MV, MOG = 19, 21, 23, 25
NARROW, U_TILES = 27, 28
ROW_DT, ROW_I, ROW_F, ROW_GD = 0, 32, 64, 96
SSD0, RWKV0, GLA0, MLSTM0 = 0, 772, 1668, 2452

CONST = {}
_at = 0
for _name, _n in [("ident", P), ("causal", P), ("strict", P), ("anti", P), ("fwd", 7 * P), ("bwd", 7 * P),
                  ("ones", P), ("mean256", P), ("mean1024", P), ("mean128", P), ("mean64", P), ("sum64", P),
                  ("pick", H * P), ("pickneg", H * P), ("glamask", 2 * P), ("rot", P), ("freq", 1), ("iota", P)]:
    CONST[_name] = (_at, _n)
    _at += _n
CONST_W = _at


def constants():
    c = np.zeros((P, CONST_W), np.float32)

    def put(name, a):
        o, n = CONST[name]
        c[:a.shape[0], o:o + n] = a

    i = np.arange(P)
    s, t = i[:, None], i[None, :]
    put("ident", np.eye(P))
    put("causal", (t >= s) * 1.0)
    put("strict", (t > s) * 1.0)
    put("anti", (t <= s) * 1.0)
    lev = [((s // (2 * h) == t // (2 * h)) & (s % (2 * h) < h) & (t % (2 * h) >= h)) * 1.0 for h in HALVES]
    put("fwd", np.concatenate(lev, 1))
    put("bwd", np.concatenate([m.T for m in lev], 1))
    put("ones", np.ones((P, P)))
    put("mean256", np.full((P, P), 1 / 256))
    put("mean1024", np.full((P, P), 1 / D))
    put("mean128", np.full((P, P), 1 / P))
    put("mean64", (s // 64 == t // 64) / 64.0)
    put("sum64", (s // 64 == t // 64) * 1.0)
    pick = np.zeros((H, H, P))
    pick[np.arange(H), np.arange(H)] = 1
    put("pick", pick.reshape(H, H * P))
    put("pickneg", -pick.reshape(H, H * P))
    put("glamask", (s // 32 == np.arange(2 * P)[None, :] // 64) * 1.0)
    rot = np.zeros((P, P))
    for b in (0, 64):
        for d in range(8):
            rot[b + d + 8, b + d] = -1
            rot[b + d, b + d + 8] = 1
    put("rot", rot)
    inv = np.float32(500000.0) ** (-np.arange(0, 16, 2, dtype=np.float32) / np.float32(16))
    f = np.zeros((P, 1), np.float32)
    for b in (0, 8, 64, 72):
        f[b:b + 8, 0] = inv
    put("freq", f)
    put("iota", np.tile(i.astype(np.float32), (P, 1)))
    return c


COLS = {}
_at = 0
for _name, _n in [("ssd_conv_w", 16), ("ssd_conv_b", 4), ("mlstm_conv_w", 16), ("mlstm_conv_b", 4),
                  ("ssd_d", 2), ("ssd_norm_g", 2), ("ssd_dt_bias", 1), ("ssd_a_log", 1), ("mlstm_i_b", 1),
                  ("mlstm_f_b", 1), ("rwkv_mu", 7), ("rwkv_w0", 2), ("rwkv_a0", 2), ("rwkv_k_k", 2),
                  ("rwkv_k_a", 2), ("rwkv_r_k", 2), ("rwkv_ln_g", 2), ("rwkv_ln_b", 2), ("gla_gate_b", 1),
                  ("gla_norm_g", 2), ("mlstm_norm_g", 2), ("ln1_g", 8), ("ln1_b", 8), ("ln2_g", 8),
                  ("ln2_b", 8), ("ln_in_g_2", 8), ("ln_in_b_2", 8), ("ln1_g_2", 16), ("ln1_b_2", 16),
                  ("ln2_g_2", 16), ("ln2_b_2", 16), ("da_norm_g_2", 2), ("hg_norm_g_2", 2),
                  ("hg_lb_fwd_2", 8), ("hg_lb_bwd_2", 8), ("conv_w_2", 2 * 3 * 44), ("conv_b_2", 2 * 44),
                  ("da_lambda_2", 8)]:
    COLS[_name] = (_at, _n)
    _at += _n
COLS_W = _at


def pack_columns(i):
    c = np.zeros((P, COLS_W), np.float32)
    for name, (o, n) in COLS.items():
        a = np.asarray(i[name])
        if name == "ssd_d":
            a = np.repeat(a, 64)
        a = a.reshape(-1)
        if name in ("ssd_dt_bias", "ssd_a_log", "mlstm_i_b", "mlstm_f_b"):
            c[:H, o] = a
        elif name == "da_lambda_2":
            c[:64, o:o + n] = a.reshape(n, 64).T
        else:
            c[:, o:o + n] = a.reshape(n, P).T
    return c


def tiles_of(w):
    k, f = w.shape
    return np.ascontiguousarray(w.reshape(k // P, P, f // P, P).transpose(2, 1, 0, 3)).reshape(f // P, P, -1)


def pack_w_in(w):
    cols = [w[:, SSD0:SSD0 + 768], w[:, RWKV0:RWKV0 + 896], w[:, GLA0:GLA0 + 512],
            w[:, GLA0 + 528:GLA0 + 784], w[:, MLSTM0:MLSTM0 + 768], w[:, MLSTM0 + 776:MLSTM0 + 1032]]
    narrow = np.zeros((D, P), w.dtype)
    narrow[:, ROW_DT:ROW_DT + 4] = w[:, 768:772]
    narrow[:, ROW_I:ROW_I + 4] = w[:, MLSTM0 + 768:MLSTM0 + 772]
    narrow[:, ROW_F:ROW_F + 4] = w[:, MLSTM0 + 772:MLSTM0 + 776]
    narrow[:, ROW_GD:ROW_GD + 16] = w[:, GLA0 + 512:GLA0 + 528]
    return tiles_of(np.concatenate(cols + [narrow], 1))


def fm(a):
    return np.ascontiguousarray(a.reshape(a.shape[0], -1, P).transpose(2, 1, 0))


@contextmanager
def stage(nc, *names):
    with ExitStack() as ctx:
        sems = [ctx.enter_context(nc.semaphore(n)) for n in names]
        with nc.Block() as block:
            yield (block, *sems)
        nc.clear_and_free_semaphores(sems)
        nc.all_engine_barrier()


class Own:

    def __init__(self, eng, sem):
        self.eng, self.sem, self.n = eng, sem, 0

    def __call__(self, ins):
        self.n += 1
        ins.then_inc(self.sem, 1)
        self.eng.wait_ge(self.sem, self.n)

    def go(self, ins):
        self.n += 1
        ins.then_inc(self.sem, 1)

    def all(self):
        self.eng.wait_ge(self.sem, self.n)


class Kit:

    def __init__(self, nc, const, cols):
        self.nc, self.const, self.cols, self.made = nc, const, cols, 0

    def sb(self, ctx, name, shape, dtype=F32):
        self.made += 1
        return ctx.enter_context(self.nc.sbuf_tensor(f"{name}_{self.made}", shape, dtype))

    def ps(self, ctx, name, shape):
        self.made += 1
        return ctx.enter_context(self.nc.psum_tensor(f"{name}_{self.made}", shape, F32))

    def c(self, name, rows=P, part=None, width=P, base=0):
        o, n = CONST[name]
        if part is not None:
            o, n = o + part * width, width
        return self.const[base:rows, o:o + n]

    def col(self, name, k=0, rows=P, n=1):
        o = COLS[name][0] + k
        return self.cols[0:rows, o:o + n]


def load(K, pairs):
    nc = K.nc
    with stage(nc, "loaded") as (block, loaded):
        @block.sync
        def _(sp):
            for dst, src in pairs:
                sp.dma_start(dst, src).then_inc(loaded, 16)
            sp.wait_ge(loaded, 16 * len(pairs))


RING = 4
SLOT = [2 * (h % 2) + h // 2 for h in range(H)]


def project(K, w, n_tiles, kt, rhs, n, out, residual=None, alpha=1.0):
    nc = K.nc
    rounds = n_tiles // RING
    assert rounds * RING == n_tiles
    with ExitStack() as ctx:
        ring = K.sb(ctx, "wring", [P, RING, kt * P])
        acc = K.ps(ctx, "acc", [P, RING, 512])
        with stage(nc, *[f"loaded{r}" for r in range(RING)], "product", "taken") as (block, *sems):
            loaded, (product, taken) = sems[:RING], sems[RING:]

            @block.sync
            def _(sp):
                for r in range(RING):
                    sp.dma_start(ring[:, r, :], w[r]).then_inc(loaded[r], 16)
                if rounds > 1:
                    with sp.Fori(1, rounds) as i:
                        for r in range(RING):
                            sp.wait_ge(taken, (i - 1) * RING + r + 1)
                            sp.dma_start(ring[:, r, :], w[bass.ds(i * RING + r, 1), :, :].rearrange("a p k -> (a p) k")).then_inc(loaded[r], 16)

            @block.tensor
            def _(pe):
                with pe.Fori(0, rounds) as i:
                    for r in range(RING):
                        pe.wait_ge(loaded[r], i * 16 + 16)
                        for k in range(kt):
                            mm = nc.tensor.matmul(acc[:, r, 0:n], ring[:, r, k * P:(k + 1) * P], rhs(k),
                                                  start=(k == 0), stop=(k == kt - 1))
                        mm.then_inc(product, 1)

            if residual is None:
                @block.scalar
                def _(act):
                    with act.Fori(0, rounds) as i:
                        for r in range(RING):
                            act.wait_ge(product, i * RING + r + 1)
                            nc.scalar.activation(out[:, bass.ds(i * RING + r, 1), :], acc[:, r:r + 1, 0:n],
                                                 ACT.Copy).then_inc(taken, 1)
            else:
                @block.vector
                def _(dve):
                    with dve.Fori(0, rounds) as i:
                        for r in range(RING):
                            dve.wait_ge(product, i * RING + r + 1)
                            nc.vector.scalar_tensor_tensor(
                                out[:, bass.ds(i * RING + r, 1), :], residual[:, bass.ds(i * RING + r, 1), :],
                                alpha, acc[:, r:r + 1, 0:n], ALU.mult, ALU.add).then_inc(taken, 1)


def normalise(K, x, out, mean, eps, center, gain, bias=None, gate=None, scale=None):
    nc = K.nc
    flat = [t for g in x for t in g]
    oflat = [t for g in out for t in g]
    n = len(x[0])
    with ExitStack() as ctx:
        sq = K.sb(ctx, "sq", [P, n, S])
        sd = K.sb(ctx, "sd", [P, 2, S])
        ms = K.ps(ctx, "ms", [P, 2, S])
        mu = K.ps(ctx, "mu", [P, 2, S])
        with stage(nc, "mean_ready", "centred", "squared", "var_ready", "eps_added", "root", "own", "normed") as (
                block, mean_ready, centred, squared, var_ready, eps_added, root, own, normed):
            src = (lambda g, j: out[g][j]) if center else (lambda g, j: x[g][j])

            @block.tensor
            def _(pe):
                for g in range(len(x)):
                    if center:
                        if g >= 2:
                            pe.wait_ge(centred, n * (g - 1))
                        for j in range(n):
                            mm = nc.tensor.matmul(mu[:, g % 2, :], mean, x[g][j], start=(j == 0), stop=(j == n - 1))
                        mm.then_inc(mean_ready, 1)
                    pe.wait_ge(squared, n * (g + 1))
                    if g >= 2:
                        pe.wait_ge(eps_added, g - 1)
                    for j in range(n):
                        mm = nc.tensor.matmul(ms[:, g % 2, :], mean, sq[:, j, :], start=(j == 0), stop=(j == n - 1))
                    mm.then_inc(var_ready, 1)

            @block.scalar
            def _(act):
                for g in range(len(x)):
                    if g:
                        act.wait_ge(var_ready, g)
                    for j in range(n):
                        if center:
                            act.wait_ge(centred, n * g + j + 1)
                        nc.scalar.activation(sq[:, j, :], src(g, j), ACT.Square).then_inc(squared, 1)
                    act.wait_ge(eps_added, g + 1)
                    nc.scalar.activation(sd[:, g % 2, :], sd[:, g % 2, :], ACT.Sqrt).then_inc(root, 1)

            @block.vector
            def _(dve):
                step = Own(dve, own)
                for g in range(len(x)):
                    if center:
                        dve.wait_ge(mean_ready, g + 1)
                        for j in range(n):
                            nc.vector.tensor_tensor(out[g][j], x[g][j], mu[:, g % 2, :], ALU.subtract).then_inc(centred, 1)
                        dve.wait_ge(centred, n * (g + 1))
                    dve.wait_ge(var_ready, g + 1)
                    nc.vector.tensor_scalar(sd[:, g % 2, :], ms[:, g % 2, :], eps, None, ALU.add).then_inc(eps_added, 1)
                    dve.wait_ge(root, g + 1)
                    step(nc.vector.reciprocal(sd[:, g % 2, :], sd[:, g % 2, :]))
                    for j in range(n):
                        step.go(nc.vector.scalar_tensor_tensor(out[g][j], src(g, j), gain(n * g + j), sd[:, g % 2, :],
                                                               ALU.mult, ALU.mult))
                    step.all()
                    for j in range(n):
                        if bias is not None:
                            step.go(nc.vector.tensor_scalar(out[g][j], out[g][j], bias(n * g + j), None, ALU.add))
                        if scale is not None:
                            step.go(nc.vector.tensor_scalar(out[g][j], out[g][j], scale, None, ALU.mult))
                        if gate is not None:
                            step.go(nc.vector.tensor_tensor(out[g][j], out[g][j], gate(n * g + j), ALU.mult))
                    step.all()


def transposes(K, items):
    nc = K.nc
    with ExitStack() as ctx:
        bank = K.ps(ctx, "bank", [P, 4, NT, P])
        with stage(nc, "turned", "taken_v", "taken_a") as (block, turned, taken_v, taken_a):
            @block.tensor
            def _(pe):
                for n, (src, dst) in enumerate(items):
                    rows, wide = src.shape[0], src.shape[1] // P
                    if n >= 4:
                        pe.wait_ge(taken_a if n % 2 else taken_v, (n - 4) // 2 + 1)
                    for j in range(wide):
                        mm = nc.tensor.transpose(bank[:, n % 4, j, 0:rows], src[:, j * P:(j + 1) * P],
                                                 K.c("ident", rows, 0, rows))
                    mm.then_inc(turned, 1)

            @block.vector
            def _(dve):
                for n, (src, dst) in enumerate(items):
                    if n % 2 == 0:
                        dve.wait_ge(turned, n + 1)
                        nc.vector.tensor_copy(dst, bank[:, n % 4, 0:src.shape[1] // P, 0:src.shape[0]]).then_inc(taken_v, 1)

            @block.scalar
            def _(act):
                for n, (src, dst) in enumerate(items):
                    if n % 2 == 1:
                        act.wait_ge(turned, n + 1)
                        nc.scalar.activation(dst, bank[:, n % 4, 0:src.shape[1] // P, 0:src.shape[0]], ACT.Copy).then_inc(taken_a, 1)


def short_convs(K, U, conv):
    nc = K.nc
    tiles = [(XR + t, "ssd_conv", t) for t in range(4)] + [(MQ + t, "mlstm_conv", t) for t in range(4)]
    with stage(nc, "own", "convolved", "active") as (block, own, convolved, active):
        @block.vector
        def _(dve):
            step = Own(dve, own)
            for n, (u, name, t) in enumerate(tiles):
                step.go(nc.vector.tensor_scalar(conv[:, n, :], U[:, u, :], K.col(name + "_w", 12 + t),
                                                K.col(name + "_b", t), ALU.mult, ALU.add))
            for back in (1, 2, 3):
                step.all()
                for n, (u, name, t) in enumerate(tiles):
                    ins = nc.vector.scalar_tensor_tensor(conv[:, n, back:S], U[:, u, 0:S - back],
                                                         K.col(name + "_w", 4 * (3 - back) + t), conv[:, n, back:S],
                                                         ALU.mult, ALU.add)
                    if back < 3:
                        step.go(ins)
                    else:
                        ins.then_inc(convolved, 1)

        @block.scalar
        def _(act):
            for n in range(8):
                act.wait_ge(convolved, n + 1)
                nc.scalar.activation(conv[:, n, :], conv[:, n, :], ACT.Silu).then_inc(active, 1)


def scalar_gates(K, U, rows, cols):
    nc = K.nc
    with ExitStack() as ctx:
        t = K.sb(ctx, "gate_t", [H, 4, S])
        e = K.sb(ctx, "gate_e", [H, 2, S])
        one = K.sb(ctx, "gate_one", [H, S])
        a = K.sb(ctx, "gate_a", [H, 1])
        picked = K.ps(ctx, "picked", [H, 3, S])
        turned = K.ps(ctx, "turned", [P, 3, NT, H])
        with stage(nc, "rows_picked", "own", "abs_ready", "exp_ready", "log_ready", "rows_ready", "em_in",
                   "em_out", "cols_turned", "a_ready") as (
                block, rows_picked, own, abs_ready, exp_ready, log_ready, rows_ready, em_in, em_out,
                cols_turned, a_ready):
            @block.tensor
            def _(pe):
                for n, r in enumerate((ROW_DT, ROW_I, ROW_F)):
                    mm = nc.tensor.matmul(picked[:, n, :], K.c("ident")[:, r:r + H], U[:, NARROW, :], start=True, stop=True)
                mm.then_inc(rows_picked, 1)
                pe.wait_ge(rows_ready, 1)
                for n, q in enumerate((0, 1, 2)):
                    for j in range(NT):
                        mm = nc.tensor.transpose(turned[:, n, j, :], rows[:, q, j * P:(j + 1) * P], K.c("ident", H, 0, H))
                mm.then_inc(cols_turned, 1)

            @block.scalar
            def _(act):
                nc.scalar.activation(a[:, :], K.col("ssd_a_log", rows=H), ACT.Exp).then_inc(a_ready, 1)
                act.wait_ge(abs_ready, 2)
                nc.scalar.activation(e[:, :, :], e[:, :, :], ACT.Exp, scale=-1.0).then_inc(exp_ready, 1)
                act.wait_ge(exp_ready, 1)
                nc.scalar.activation(e[:, :, :], e[:, :, :], ACT.Ln, bias=1.0).then_inc(log_ready, 1)
                act.wait_ge(em_in, 1)
                nc.scalar.activation(rows[:, 4, :], t[:, 3, :], ACT.Exp).then_inc(em_out, 1)

            @block.vector
            def _(dve):
                step = Own(dve, own)
                step.go(nc.vector.memset(one[:, :], 1.0))
                dve.wait_ge(rows_picked, 1)
                for n, name in enumerate(("ssd_dt_bias", "mlstm_i_b", "mlstm_f_b")):
                    step.go(nc.vector.tensor_scalar(t[:, n, :], picked[:, n, :], K.col(name, rows=H), None, ALU.add))
                step.all()
                nc.vector.scalar_tensor_tensor(e[:, 0, :], t[:, 0, :], -1.0, t[:, 0, :], ALU.mult, ALU.max).then_inc(abs_ready, 1)
                nc.vector.scalar_tensor_tensor(e[:, 1, :], t[:, 2, :], -1.0, t[:, 2, :], ALU.mult, ALU.max).then_inc(abs_ready, 1)
                dve.wait_ge(log_ready, 1)
                step.go(nc.vector.scalar_tensor_tensor(rows[:, 1, :], t[:, 0, :], 0.0, e[:, 0, :], ALU.max, ALU.add))
                step(nc.vector.scalar_tensor_tensor(t[:, 2, :], t[:, 2, :], 0.0, e[:, 1, :], ALU.min, ALU.subtract))
                dve.wait_ge(a_ready, 1)
                step.go(nc.vector.tensor_scalar(t[:, 0, :], rows[:, 1, :], a[:, :], -1.0, ALU.mult, ALU.mult))
                step(nc.vector.tensor_tensor_scan(t[:, 3, :], one[:, :], t[:, 2, :], 0.0, ALU.mult, ALU.add))
                step.go(nc.vector.tensor_tensor_scan(rows[:, 0, :], one[:, :], t[:, 0, :], 0.0, ALU.mult, ALU.add))
                step(nc.vector.tensor_tensor(rows[:, 2, :], t[:, 1, :], t[:, 3, :], ALU.subtract))
                step(nc.vector.tensor_tensor_scan(rows[:, 3, :], one[:, :], rows[:, 2, :], 0.0, ALU.mult, ALU.max))
                nc.vector.tensor_tensor(t[:, 3, :], t[:, 3, :], rows[:, 3, :], ALU.add).then_inc(rows_ready, 1)
                dve.wait_ge(rows_ready, 1)
                nc.vector.tensor_scalar(t[:, 3, :], t[:, 3, :], -1.0, 87.0, ALU.mult, ALU.min).then_inc(em_in, 1)
                dve.wait_ge(cols_turned, 1)
                step.go(nc.vector.tensor_scalar(cols[:, 0, :, :], turned[:, 0, :, :], -1.0, None, ALU.mult))
                step.go(nc.vector.tensor_copy(cols[:, 1:3, :, :], turned[:, 1:3, :, :]))
                step.all()
                dve.wait_ge(em_out, 1)


def decayed_attention(K, key, query, row, pick, col, value, scale, out, den=None):
    nc = K.nc
    steps = [(h, j) for h in range(H) for j in range(NT)]
    with ExitStack() as ctx:
        dec = K.sb(ctx, "dec", [P, 2, S])
        att = K.sb(ctx, "att", [P, 2, S])
        st = K.ps(ctx, "st", [P, 2, S])
        rb = K.ps(ctx, "rb", [P, 2, S])
        with stage(nc, "row_spread", "exponent", "decayed", "masked", "scored", "weighted", "summed") as (
                block, row_spread, exponent, decayed, masked, scored, weighted, summed):
            @block.tensor
            def _(pe):
                def sums(n):
                    h, j = steps[n]
                    pe.wait_ge(weighted, n + 1)
                    o = 64 * (h % 2)
                    mm = nc.tensor.matmul(out[o:o + 64, h // 2, j * P:S], value(h, j), att[:, n % 2, j * P:S],
                                          start=(j == 0), stop=(j == NT - 1))
                    if den is not None:
                        mm = nc.tensor.matmul(den[o:o + 64, h // 2, j * P:S], K.c("ones", P, 0, 64),
                                              att[:, n % 2, j * P:S], start=(j == 0), stop=(j == NT - 1))
                    mm.then_inc(summed, 1)

                for n, (h, j) in enumerate(steps):
                    if j == 0:
                        if h >= 2:
                            pe.wait_ge(exponent, NT * (h - 1))
                        nc.tensor.matmul(rb[:, h % 2, :], K.c(pick, H, h), row, start=True, stop=True).then_inc(row_spread, 1)
                    if n >= 2:
                        pe.wait_ge(weighted, n - 1)
                    nc.tensor.matmul(st[:, n % 2, j * P:S], key(h)[:, j * P:(j + 1) * P], query(h)[:, j * P:S],
                                     start=True, stop=True).then_inc(scored, 1)
                    if n:
                        sums(n - 1)
                sums(len(steps) - 1)

            @block.scalar
            def _(act):
                for n, (h, j) in enumerate(steps):
                    act.wait_ge(exponent, n + 1)
                    nc.scalar.activation(dec[:, n % 2, j * P:S], dec[:, n % 2, j * P:S], ACT.Exp).then_inc(decayed, 1)

            @block.vector
            def _(dve):
                def exponents(n):
                    h, j = steps[n]
                    dve.wait_ge(row_spread, h + 1)
                    if n >= 2:
                        dve.wait_ge(weighted, n - 1)
                    nc.vector.tensor_scalar(dec[:, n % 2, j * P:S], rb[:, h % 2, j * P:S], col(h, j), 0.0,
                                            ALU.add, ALU.min).then_inc(exponent, 1)

                exponents(0)
                for n, (h, j) in enumerate(steps):
                    if n + 1 < len(steps):
                        exponents(n + 1)
                    dve.wait_ge(decayed, n + 1)
                    nc.vector.tensor_tensor(dec[:, n % 2, j * P:(j + 1) * P], dec[:, n % 2, j * P:(j + 1) * P],
                                            K.c("causal"), ALU.mult).then_inc(masked, 1)
                    dve.wait_ge(masked, n + 1)
                    dve.wait_ge(scored, n + 1)
                    if n >= 2:
                        dve.wait_ge(summed, n - 1)
                    nc.vector.scalar_tensor_tensor(att[:, n % 2, j * P:S], st[:, n % 2, j * P:S], scale,
                                                   dec[:, n % 2, j * P:S], ALU.mult, ALU.mult).then_inc(weighted, 1)


def ssd(K, U, conv, rows, cols, y):
    nc = K.nc
    with ExitStack() as ctx:
        xt = K.sb(ctx, "xt", [P, NT, 256])
        gz = K.sb(ctx, "gz", [P, 2, S])
        out = K.ps(ctx, "ssd_out", [P, 2, S])
        with ExitStack() as c2:
            transposes(K, [(conv[:, t, :], xt[:, :, t * P:(t + 1) * P]) for t in range(2)])
        with stage(nc, "scaled", "gated") as (block, scaled, gated):
            @block.vector
            def _(dve):
                for j in range(NT):
                    v = xt[:, j, :].rearrange("p (h d) -> p h d", h=H)
                    nc.vector.tensor_tensor(v, v, cols[:, 1, j, :].unsqueeze(2).to_broadcast([P, H, 64]),
                                            ALU.mult).then_inc(scaled, 1)

            @block.scalar
            def _(act):
                nc.scalar.activation(gz[:, :, :], U[:, Z:Z + 2, :], ACT.Silu).then_inc(gated, 1)
        decayed_attention(K, lambda h: conv[:, 2, :], lambda h: conv[:, 3, :], rows[:, 0, :], "pick",
                          lambda h, j: cols[:, 0, j, h:h + 1], lambda h, j: xt[:, j, h * 64:h * 64 + 64], 1.0, out)
        with stage(nc, "own") as (block, own):
            @block.vector
            def _(dve):
                step = Own(dve, own)
                for t in range(2):
                    step.go(nc.vector.scalar_tensor_tensor(y[:, t, :], conv[:, t, :], K.col("ssd_d", t), out[:, t, :],
                                                           ALU.mult, ALU.add))
                step.all()
                step(nc.vector.tensor_tensor(y[:, :, :], y[:, :, :], gz[:, :, :], ALU.mult))
    normalise(K, [[y[:, 0, :], y[:, 1, :]]], [[y[:, 0, :], y[:, 1, :]]], K.c("mean256"), 1e-5, False,
              lambda t: K.col("ssd_norm_g", t))


def mlstm(K, U, conv, rows, cols, y):
    nc = K.nc
    with ExitStack() as ctx:
        vt = K.sb(ctx, "vt", [P, NT, 256])
        dn = K.sb(ctx, "dn", [P, 2, S])
        so = K.sb(ctx, "so", [P, 2, S])
        out = K.ps(ctx, "ml_out", [P, 2, S])
        transposes(K, [(U[:, MV + t, :], vt[:, :, t * P:(t + 1) * P]) for t in range(2)])
        with ExitStack() as c2:
            den = K.ps(c2, "ml_den", [P, 2, S])
            decayed_attention(K, lambda h: conv[64 * (h % 2):64 * (h % 2) + 64, 6 + h // 2, :],
                              lambda h: conv[64 * (h % 2):64 * (h % 2) + 64, 4 + h // 2, :],
                              rows[:, 3, :], "pickneg", lambda h, j: cols[:, 2, j, h:h + 1],
                              lambda h, j: vt[:, j, h * 64:h * 64 + 64], 0.125, out, den)
            em = K.ps(c2, "em", [P, 2, S])
            with stage(nc, "own", "em_spread", "gate_ready", "den_abs") as (
                    block, own, em_spread, gate_ready, den_abs):
                @block.tensor
                def _(pe):
                    for h in range(H):
                        o = 64 * (h % 2)
                        mm = nc.tensor.matmul(em[o:o + 64, h // 2, :], K.c("pick", H, h)[:, 0:64], rows[:, 4, :],
                                              start=True, stop=True)
                    mm.then_inc(em_spread, 1)

                @block.scalar
                def _(act):
                    nc.scalar.activation(dn[:, :, :], den[:, :, :], ACT.Abs).then_inc(den_abs, 1)
                    nc.scalar.activation(so[:, :, :], U[:, MOG:MOG + 2, :], ACT.Sigmoid).then_inc(gate_ready, 1)

                @block.vector
                def _(dve):
                    step = Own(dve, own)
                    dve.wait_ge(em_spread, 1)
                    dve.wait_ge(den_abs, 1)
                    step(nc.vector.tensor_tensor(dn[:, :, :], dn[:, :, :], em[:, :, :], ALU.max))
                    step(nc.vector.reciprocal(dn[:, :, :], dn[:, :, :]))
                    step(nc.vector.tensor_tensor(y[:, :, :], dn[:, :, :], out[:, :, :], ALU.mult))
                    dve.wait_ge(gate_ready, 1)
                    step(nc.vector.tensor_tensor(y[:, :, :], y[:, :, :], so[:, :, :], ALU.mult))
    normalise(K, [[y[:, 0, :]], [y[:, 1, :]]], [[y[:, 0, :]], [y[:, 1, :]]], K.c("mean64"), 1e-5, True,
              lambda t: K.col("mlstm_norm_g", t))


def gla(K, U, gate_up, y):
    nc = K.nc
    L = [slice(c * P, (c + 1) * P) for c in range(NT)]
    MID = P // 2 - 1
    with ExitStack() as ctx:
        b = K.sb(ctx, "b", [P, S])
        e = K.sb(ctx, "e", [P, 2, S])
        qd = K.sb(ctx, "qd", [P, S])
        ki = K.sb(ctx, "ki", [P, S])
        kt = K.sb(ctx, "kt", [P, NT, P])
        vt = K.sb(ctx, "vt", [P, NT, 256])
        one = K.sb(ctx, "one", [P, P])
        ends = K.sb(ctx, "ends", [P, NT, 3])
        og = K.sb(ctx, "og", [P, 2, S])
        state = K.sb(ctx, "state", [P, 256])
        started = K.sb(ctx, "started", [P, 256])
        att = K.sb(ctx, "att", [P, 2, P])
        transposes(K, [(U[:, GV + t, :], vt[:, :, t * P:(t + 1) * P]) for t in range(2)])
        with ExitStack() as c2:
            logit = K.ps(c2, "logit", [P, S])
            with stage(nc, "own", "a_own", "logit_ready", "gate_in", "gate_out", "diff_ready", "exp_ready", "og_ready") as (
                    block, own, a_own, logit_ready, gate_in, gate_out, diff_ready, exp_ready, og_ready):
                @block.tensor
                def _(pe):
                    nc.tensor.matmul(logit[:, :], gate_up[ROW_GD:ROW_GD + 16, :], U[ROW_GD:ROW_GD + 16, NARROW, :],
                                     start=True, stop=True).then_inc(logit_ready, 1)

                @block.scalar
                def _(act):
                    step = Own(act, a_own)
                    act.wait_ge(gate_in, 1)
                    step(nc.scalar.activation(e[:, 1, :], e[:, 1, :], ACT.Exp, scale=-1.0))
                    nc.scalar.activation(e[:, 1, :], e[:, 1, :], ACT.Ln, bias=1.0).then_inc(gate_out, 1)
                    act.wait_ge(diff_ready, 1)
                    step.go(nc.scalar.activation(e[:, :, :], e[:, :, :], ACT.Exp))
                    step(nc.scalar.activation(ends[:, :, :], ends[:, :, :], ACT.Exp))
                    nc.scalar.activation(og[:, :, :], U[:, GOG:GOG + 2, :], ACT.Silu).then_inc(og_ready, 1)

                @block.vector
                def _(dve):
                    step = Own(dve, own)
                    step.go(nc.vector.memset(one[:, :], 1.0))
                    dve.wait_ge(logit_ready, 1)
                    step(nc.vector.tensor_scalar(e[:, 0, :], logit[:, :], K.col("gla_gate_b"), None, ALU.add))
                    nc.vector.scalar_tensor_tensor(e[:, 1, :], e[:, 0, :], -1.0, e[:, 0, :], ALU.mult, ALU.max).then_inc(gate_in, 1)
                    dve.wait_ge(gate_out, 1)
                    step(nc.vector.scalar_tensor_tensor(e[:, 0, :], e[:, 0, :], 0.0, e[:, 1, :], ALU.min, ALU.subtract))
                    step(nc.vector.tensor_scalar(e[:, 0, :], e[:, 0, :], 1 / 16, None, ALU.mult))
                    for c in range(NT):
                        step.go(nc.vector.tensor_tensor_scan(b[:, L[c]], one[:, :], e[:, 0, L[c]], 0.0, ALU.mult, ALU.add))
                    step.all()
                    for c in range(NT):
                        mid, last = b[:, c * P + MID:c * P + MID + 1], b[:, (c + 1) * P - 1:(c + 1) * P]
                        step.go(nc.vector.tensor_copy(ends[:, c, 0:1], mid))
                        step.go(nc.vector.tensor_tensor(ends[:, c, 1:2], last, mid, ALU.subtract))
                        step.go(nc.vector.tensor_copy(ends[:, c, 2:3], last))
                        step.go(nc.vector.tensor_scalar(e[:, 0, L[c]], b[:, L[c]], mid, None, ALU.subtract))
                    step.all()
                    nc.vector.tensor_scalar(e[:, 1, :], e[:, 0, :], -1.0, None, ALU.mult).then_inc(diff_ready, 1)
                    dve.wait_ge(og_ready, 1)
                    step.go(nc.vector.scalar_tensor_tensor(qd[:, :], U[:, GQ, :], 32 ** -0.5, e[:, 0, :], ALU.mult, ALU.mult))
                    step(nc.vector.tensor_tensor(ki[:, :], U[:, GK, :], e[:, 1, :], ALU.mult))
        transposes(K, [(ki[:, :], kt[:, :, :])])
        with ExitStack() as c2:
            out = K.ps(c2, "gla_out", [P, 2, S])
            sc = K.ps(c2, "sc", [P, 2, 512])
            kv = K.ps(c2, "kv", [P, 2, 512])
            with stage(nc, "own", "scored", "weighted", "contrib", "state_ready", "chunk_done") as (
                    block, own, scored, weighted, contrib, state_ready, chunk_done):
                @block.tensor
                def _(pe):
                    for c in range(NT):
                        nc.tensor.matmul(kv[:, c % 2, 0:256], kt[:, c, :], vt[:, c, :], start=True, stop=True).then_inc(contrib, 1)
                        if c:
                            pe.wait_ge(state_ready, c)
                            for t in range(2):
                                nc.tensor.matmul(out[:, t, L[c]], started[:, t * P:(t + 1) * P], qd[:, L[c]],
                                                 start=True, stop=False, skip_group_check=True)
                        for h in range(H):
                            n = c * H + h
                            if n >= 2:
                                pe.wait_ge(weighted, n - 1)
                            r = slice(32 * h, 32 * h + 32)
                            nc.tensor.matmul(sc[:, n % 2, 0:P], ki[r, L[c]], qd[r, L[c]], start=True, stop=True).then_inc(scored, 1)
                            pe.wait_ge(weighted, n + 1)
                            o = 64 * (h % 2)
                            mm = nc.tensor.matmul(out[o:o + 64, h // 2, L[c]], vt[:, c, h * 64:h * 64 + 64], att[:, n % 2, :],
                                                  start=(c == 0), stop=True, skip_group_check=True)
                        mm.then_inc(chunk_done, 1)

                @block.vector
                def _(dve):
                    step = Own(dve, own)
                    step.go(nc.vector.memset(att[:, :, :], 0.0))
                    step(nc.vector.memset(state[:, :], 0.0))
                    for c in range(NT):
                        for h in range(H):
                            n = c * H + h
                            dve.wait_ge(scored, n + 1)
                            nc.vector.copy_predicated(att[:, n % 2, :], K.c("causal").bitcast(I32), sc[:, n % 2, 0:P]).then_inc(weighted, 1)
                        if c < NT - 1:
                            dve.wait_ge(contrib, c + 1)
                            step(nc.vector.tensor_scalar(state[:, :], state[:, :], ends[:, c, 2:3], None, ALU.mult))
                            step(nc.vector.scalar_tensor_tensor(state[:, :], kv[:, c % 2, 0:256], ends[:, c, 1:2], state[:, :], ALU.mult, ALU.add))
                            dve.wait_ge(chunk_done, c + 1)
                            nc.vector.scalar_tensor_tensor(started[:, :], state[:, :], ends[:, c + 1, 0:1],
                                                           K.c("glamask", P, 0, 256), ALU.mult, ALU.mult).then_inc(state_ready, 1)
                    dve.wait_ge(chunk_done, NT)
                    step(nc.vector.tensor_copy(y[:, :, :], out[:, :, :]))
        normalise(K, [[y[:, 0, :]], [y[:, 1, :]]], [[y[:, 0, :]], [y[:, 1, :]]], K.c("mean64"), 1e-5, False,
                  lambda t: K.col("gla_norm_g", t), gate=lambda t: og[:, t, :])


def rwkv(K, U, lora, y):
    nc = K.nc
    L = [slice(c * P, (c + 1) * P) for c in range(NT)]
    MID = P // 2 - 1
    with ExitStack() as ctx:
        at = K.sb(ctx, "at", [P, 2, S])
        bt = K.sb(ctx, "bt", [P, 2, S])
        kt = K.sb(ctx, "kt", [P, 2, S])
        rt = K.sb(ctx, "rt", [P, 2, S])
        g = K.sb(ctx, "g", [P, 2, S])
        bonus = K.sb(ctx, "bonus", [P, 2, S])
        ends = K.sb(ctx, "ends", [P, 2, NT, 3])
        vt = K.sb(ctx, "vt", [P, NT, 256])
        btt = K.sb(ctx, "btt", [P, NT, 256])
        ktt = K.sb(ctx, "ktt", [P, NT, 256])
        cm = ExitStack()
        m = K.sb(cm, "m", [P, 7, S])
        with ExitStack() as c2:
            w = K.sb(c2, "w", [P, 2, S])
            a = K.sb(c2, "a", [P, 2, S])
            kk = K.sb(c2, "kk", [P, 2, S])
            t1 = K.sb(c2, "t1", [P, 2, S])
            b = K.sb(c2, "b", [P, 2, S])
            diff = K.sb(c2, "diff", [P, 7, S])
            one = K.sb(c2, "one", [P, P])
            th = K.sb(c2, "th", [P, S])
            wl = K.ps(c2, "wl", [P, 2, S])
            al = K.ps(c2, "al", [P, 2, S])
            gl = K.ps(c2, "gl", [P, 2, S])
            s1 = K.ps(c2, "s1", [P, 2, S])
            with stage(nc, "own", "a_own", "mixed", "lora_in", "lora_out", "gates", "kk_sq", "kk_sum", "kk_root", "diffs",
                       "exps", "rk", "rk_sum") as (
                    block, own, a_own, mixed, lora_in, lora_out, gates, kk_sq, kk_sum, kk_root, diffs, exps, rk, rk_sum):
                @block.tensor
                def _(pe):
                    pe.wait_ge(lora_in, 1)
                    for t in range(2):
                        c = slice(t * P, (t + 1) * P)
                        nc.tensor.matmul(wl[:, t, :], lora[0:32, c], th[0:32, :], start=True, stop=True)
                        nc.tensor.matmul(al[:, t, :], lora[32:64, c], th[32:64, :], start=True, stop=True)
                        mm = nc.tensor.matmul(gl[:, t, :], lora[64:128, c], th[64:128, :], start=True, stop=True)
                    mm.then_inc(lora_out, 1)
                    pe.wait_ge(kk_sq, 1)
                    for t in range(2):
                        mm = nc.tensor.matmul(s1[:, t, :], K.c("sum64"), t1[:, t, :], start=True, stop=True)
                    mm.then_inc(kk_sum, 1)
                    pe.wait_ge(rk, 1)
                    for t in range(2):
                        mm = nc.tensor.matmul(s1[:, t, :], K.c("sum64"), t1[:, t, :], start=True, stop=True)
                    mm.then_inc(rk_sum, 1)

                @block.scalar
                def _(act):
                    step = Own(act, a_own)
                    act.wait_ge(mixed, 7)
                    step.go(nc.scalar.activation(th[0:32, :], m[0:32, 6, :], ACT.Tanh))
                    step.go(nc.scalar.activation(th[32:64, :], m[32:64, 6, :], ACT.Copy))
                    step.go(nc.scalar.activation(th[64:128, :], m[64:128, 6, :], ACT.Sigmoid))
                    step.all()
                    nc.scalar.activation(ends[:, 0, 0, :], K.c("ones")[:, 0:3], ACT.Copy).then_inc(lora_in, 1)
                    act.wait_ge(lora_out, 1)
                    for t in range(2):
                        step.go(nc.scalar.activation(w[:, t, :], wl[:, t, :], ACT.Sigmoid, bias=K.col("rwkv_w0", t)))
                        step.go(nc.scalar.activation(a[:, t, :], al[:, t, :], ACT.Sigmoid, bias=K.col("rwkv_a0", t)))
                    step.all()
                    nc.scalar.activation(g[:, :, :], gl[:, :, :], ACT.Copy).then_inc(gates, 1)
                    act.wait_ge(kk_sum, 1)
                    nc.scalar.activation(diff[:, 0:2, :], s1[:, :, :], ACT.Sqrt).then_inc(kk_root, 1)
                    act.wait_ge(diffs, 1)
                    step.go(nc.scalar.activation(diff[:, 0:6, :], diff[:, 0:6, :], ACT.Exp))
                    step.all()
                    nc.scalar.activation(ends[:, :, :, :], ends[:, :, :, :], ACT.Exp).then_inc(exps, 1)

                @block.vector
                def _(dve):
                    step = Own(dve, own)
                    step.go(nc.vector.memset(one[:, :], 1.0))
                    u = U[:, R_:R_ + 7, :]
                    step.go(nc.vector.tensor_tensor(diff[:, :, 1:S], u[:, :, 0:S - 1], u[:, :, 1:S], ALU.subtract))
                    step(nc.vector.tensor_scalar(diff[:, :, 0:1], u[:, :, 0:1], -1.0, None, ALU.mult))
                    for t in range(7):
                        nc.vector.scalar_tensor_tensor(m[:, t, :], diff[:, t, :], K.col("rwkv_mu", t), U[:, R_ + t, :],
                                                       ALU.mult, ALU.add).then_inc(mixed, 1)
                    dve.wait_ge(mixed, 7)
                    for t in range(2):
                        step.go(nc.vector.tensor_scalar(kk[:, t, :], m[:, 2 + t, :], K.col("rwkv_k_k", t), None, ALU.mult))
                    step.all()
                    nc.vector.tensor_tensor(t1[:, :, :], kk[:, :, :], kk[:, :, :], ALU.mult).then_inc(kk_sq, 1)
                    dve.wait_ge(kk_root, 1)
                    step(nc.vector.tensor_scalar(diff[:, 0:2, :], diff[:, 0:2, :], 1e-12, None, ALU.max))
                    step(nc.vector.reciprocal(diff[:, 0:2, :], diff[:, 0:2, :]))
                    step(nc.vector.tensor_tensor(kk[:, :, :], kk[:, :, :], diff[:, 0:2, :], ALU.mult))
                    dve.wait_ge(gates, 1)
                    for t in range(2):
                        step.go(nc.vector.tensor_scalar(t1[:, t, :], a[:, t, :], -1.0, K.col("rwkv_k_a", t), ALU.add, ALU.mult))
                    step.go(nc.vector.tensor_scalar(w[:, :, :], w[:, :, :], -float(np.exp(-0.5)), None, ALU.mult))
                    step.all()
                    step.go(nc.vector.scalar_tensor_tensor(m[:, 2:4, :], t1[:, :, :], 1.0, m[:, 2:4, :], ALU.add, ALU.mult))
                    for t in range(2):
                        for c in range(NT):
                            step.go(nc.vector.tensor_tensor_scan(b[:, t, L[c]], one[:, :], w[:, t, L[c]], 0.0, ALU.mult, ALU.add))
                    step.all()
                    for t in range(2):
                        for c in range(NT):
                            mid, last = b[:, t, c * P + MID:c * P + MID + 1], b[:, t, (c + 1) * P - 1:(c + 1) * P]
                            step.go(nc.vector.tensor_copy(ends[:, t, c, 0:1], mid))
                            step.go(nc.vector.tensor_tensor(ends[:, t, c, 1:2], last, mid, ALU.subtract))
                            step.go(nc.vector.tensor_copy(ends[:, t, c, 2:3], last))
                            step.go(nc.vector.tensor_scalar(diff[:, t, L[c]], b[:, t, L[c]], mid, None, ALU.subtract))
                    step.all()
                    step.go(nc.vector.tensor_scalar(diff[:, 2:4, :], diff[:, 0:2, :], -1.0, None, ALU.mult))
                    nc.vector.tensor_tensor(diff[:, 4:6, :], diff[:, 0:2, :], w[:, :, :], ALU.subtract).then_inc(diffs, 1)
                    step.all()
                    for t in range(2):
                        step.go(nc.vector.scalar_tensor_tensor(t1[:, t, :], m[:, t, :], K.col("rwkv_r_k", t), m[:, 2 + t, :],
                                                               ALU.mult, ALU.mult))
                    dve.wait_ge(exps, 1)
                    step.go(nc.vector.tensor_tensor(rt[:, :, :], m[:, 0:2, :], diff[:, 0:2, :], ALU.mult))
                    step.go(nc.vector.tensor_tensor(kt[:, :, :], m[:, 2:4, :], diff[:, 2:4, :], ALU.mult))
                    step.go(nc.vector.scalar_tensor_tensor(at[:, :, :], kk[:, :, :], -1.0, diff[:, 4:6, :], ALU.mult, ALU.mult))
                    step(nc.vector.tensor_tensor(bt[:, :, :], kk[:, :, :], a[:, :, :], ALU.mult))
                    nc.vector.tensor_tensor(bt[:, :, :], bt[:, :, :], diff[:, 2:4, :], ALU.mult).then_inc(rk, 1)
                    dve.wait_ge(rk_sum, 1)
                    step(nc.vector.tensor_tensor(bonus[:, :, :], m[:, 4:6, :], s1[:, :, :], ALU.mult))
                    dve.wait_ge(rk, 1)
        transposes(K, [(m[:, 4 + t, :], vt[:, :, t * P:(t + 1) * P]) for t in range(2)]
                   + [(bt[:, t, :], btt[:, :, t * P:(t + 1) * P]) for t in range(2)]
                   + [(kt[:, t, :], ktt[:, :, t * P:(t + 1) * P]) for t in range(2)])
        cm.close()
        with ExitStack() as c2:
            nt = K.sb(c2, "nt", [P, NT, H, P])
            mak = K.sb(c2, "mak", [P, NT, H, P])
            mrb = K.sb(c2, "mrb", [P, NT, H, P])
            mrk = K.sb(c2, "mrk", [P, NT, H, P])
            x = K.sb(c2, "x", [P, NT, H, P])
            xt = K.sb(c2, "xt", [P, NT, H, P])

            def spread(mask):
                return mask.unsqueeze(1).to_broadcast([P, H, P])

            with ExitStack() as c3:
                pr = K.ps(c3, "pr", [P, 4, 2, S])
                with stage(nc, "product", "masked") as (block, product, masked):
                    pairs = [(bt, at, nt, "strict"), (kt, at, mak, "strict"), (bt, rt, mrb, "causal"), (kt, rt, mrk, "causal")]

                    @block.tensor
                    def _(pe):
                        for c in range(NT):
                            for q, (left, right, dst, mask) in enumerate(pairs):
                                n = 4 * c + q
                                if n >= 4:
                                    pe.wait_ge(masked, n - 3)
                                for h in range(H):
                                    r = slice(64 * (h % 2), 64 * (h % 2) + 64)
                                    mm = nc.tensor.matmul(pr[:, n % 4, h % 2, h // 2 * P:(h // 2 + 1) * P], left[r, h // 2, L[c]], right[r, h // 2, L[c]],
                                                          start=True, stop=True)
                                mm.then_inc(product, 1)

                    @block.vector
                    def _(dve):
                        for c in range(NT):
                            for q, (left, right, dst, mask) in enumerate(pairs):
                                n = 4 * c + q
                                dve.wait_ge(product, n + 1)
                                for odd in (0, 1):
                                    last = nc.vector.tensor_tensor(
                                        dst[:, c, 2 * odd:2 * odd + 2, :],
                                        pr[:, n % 4, odd, 0:2 * P].rearrange("p (h t) -> p h t", h=2),
                                        K.c(mask).unsqueeze(1).to_broadcast([P, 2, P]), ALU.mult)
                                last.then_inc(masked, 1)
            with ExitStack() as c3:
                nm = K.sb(c3, "nm", [P, 2, H, P])
                yb = K.sb(c3, "yb", [P, 2, H, P])
                py = K.ps(c3, "py", [P, 2, H, P])
                pz = K.ps(c3, "pz", [P, 2, H, P])
                pzt = K.ps(c3, "pzt", [P, 2, H, P])
                rounds = [(lv, c) for lv in range(len(HALVES)) for c in range(NT)]
                with stage(nc, "own", "level_ready", "y_ready", "y_taken", "z_ready", "x_ready") as (
                        block, own, level_ready, y_ready, y_taken, z_ready, x_ready):
                    @block.tensor
                    def _(pe):
                        def first(n):
                            lv, c = rounds[n]
                            pe.wait_ge(level_ready, n + 1)
                            if lv:
                                pe.wait_ge(x_ready, n - NT + 1)
                            if n >= 2:
                                pe.wait_ge(y_taken, n - 1)
                            for h in range(H):
                                mm = nc.tensor.matmul(py[:, n % 2, h, :], nm[:, n % 2, h, :], x[:, c, h, :], start=True, stop=True)
                            mm.then_inc(y_ready, 1)

                        first(0)
                        for n, (lv, c) in enumerate(rounds):
                            if n + 1 < len(rounds):
                                first(n + 1)
                            pe.wait_ge(y_taken, n + 1)
                            if n >= 2:
                                pe.wait_ge(x_ready, n - 1)
                            for h in range(H):
                                nc.tensor.matmul(pz[:, n % 2, h, :], xt[:, c, h, :], yb[:, n % 2, h, :], start=True, stop=True)
                                mm = nc.tensor.matmul(pzt[:, n % 2, h, :], yb[:, n % 2, h, :], xt[:, c, h, :], start=True, stop=True)
                            mm.then_inc(z_ready, 1)

                    @block.scalar
                    def _(act):
                        for n in range(len(rounds)):
                            act.wait_ge(y_ready, n + 1)
                            if n >= 2:
                                act.wait_ge(z_ready, n - 1)
                            nc.scalar.activation(yb[:, n % 2, :, :], py[:, n % 2, :, :], ACT.Copy).then_inc(y_taken, 1)

                    @block.vector
                    def _(dve):
                        step = Own(dve, own)
                        for c in range(NT):
                            step.go(nc.vector.tensor_copy(x[:, c, :, :], spread(K.c("ident"))))
                            step.go(nc.vector.tensor_copy(xt[:, c, :, :], spread(K.c("ident"))))
                        step.all()

                        def level(n):
                            lv, c = rounds[n]
                            if n >= 2:
                                dve.wait_ge(y_ready, n - 1)
                            nc.vector.tensor_tensor(nm[:, n % 2, :, :], nt[:, c, :, :], spread(K.c("fwd", P, lv)),
                                                    ALU.mult).then_inc(level_ready, 1)

                        level(0)
                        for n, (lv, c) in enumerate(rounds):
                            if n + 1 < len(rounds):
                                level(n + 1)
                            dve.wait_ge(z_ready, n + 1)
                            step.go(nc.vector.tensor_tensor(x[:, c, :, :], x[:, c, :, :], pz[:, n % 2, :, :], ALU.add))
                            step.all()
                            nc.vector.tensor_tensor(xt[:, c, :, :], xt[:, c, :, :], pzt[:, n % 2, :, :], ALU.add).then_inc(x_ready, 1)
            with ExitStack() as c3:
                state = K.sb(c3, "state", [P, 2, 64])
                started = K.sb(c3, "started", [P, 2, 64])
                rhs = K.sb(c3, "rhs", [P, 256])
                sa = K.sb(c3, "sa", [P, 256])
                prhs = K.ps(c3, "prhs", [P, 2, 512])
                psa = K.ps(c3, "psa", [P, 512])
                pst = K.ps(c3, "pst", [P, 2, 64])
                out = K.ps(c3, "rw_out", [P, 2, S])
                with stage(nc, "own", "rhs_ready", "rhs_taken", "sa_ready", "sa_taken", "contrib", "started_ready", "chunk_done") as (
                        block, own, rhs_ready, rhs_taken, sa_ready, sa_taken, contrib, started_ready, chunk_done):
                    @block.tensor
                    def _(pe):
                        for c in range(NT):
                            pe.wait_ge(started_ready, c + 1)
                            for h in range(H):
                                r, v = slice(64 * (h % 2), 64 * (h % 2) + 64), slice(64 * h, 64 * h + 64)
                                o = prhs[:, h % 2, 64 * (h // 2):64 * (h // 2) + 64]
                                nc.tensor.matmul(o, at[r, h // 2, L[c]], started[r, h // 2, :], start=True, stop=False)
                                mm = nc.tensor.matmul(o, mak[:, c, SLOT[h], :], vt[:, c, v], start=False, stop=True)
                            mm.then_inc(rhs_ready, 1)
                            pe.wait_ge(rhs_taken, c + 1)
                            for h in range(H):
                                v = slice(64 * SLOT[h], 64 * SLOT[h] + 64)
                                mm = nc.tensor.matmul(psa[:, v], xt[:, c, SLOT[h], :], rhs[:, v], start=True, stop=True)
                            mm.then_inc(sa_ready, 1)
                            pe.wait_ge(sa_taken, c + 1)
                            for h in range(H):
                                r, v = slice(64 * (h % 2), 64 * (h % 2) + 64), slice(64 * h, 64 * h + 64)
                                nc.tensor.matmul(pst[r, h // 2, :], btt[:, c, v], sa[:, 64 * SLOT[h]:64 * SLOT[h] + 64], start=True, stop=False)
                                mm = nc.tensor.matmul(pst[r, h // 2, :], ktt[:, c, v], vt[:, c, v], start=False, stop=True)
                            mm.then_inc(contrib, 1)
                            for h in range(H):
                                r, v = slice(64 * (h % 2), 64 * (h % 2) + 64), slice(64 * h, 64 * h + 64)
                                o = out[r, h // 2, L[c]]
                                nc.tensor.matmul(o, started[r, h // 2, :], rt[r, h // 2, L[c]], start=True, stop=False)
                                nc.tensor.matmul(o, sa[:, 64 * SLOT[h]:64 * SLOT[h] + 64], mrb[:, c, SLOT[h], :], start=False, stop=False)
                                mm = nc.tensor.matmul(o, vt[:, c, v], mrk[:, c, SLOT[h], :], start=False, stop=True)
                            mm.then_inc(chunk_done, 1)

                    @block.scalar
                    def _(act):
                        for c in range(NT):
                            act.wait_ge(rhs_ready, c + 1)
                            nc.scalar.activation(rhs[:, :].rearrange("p (a b) -> p a b", a=2), prhs[:, :, 0:128], ACT.Copy).then_inc(rhs_taken, 1)
                            act.wait_ge(sa_ready, c + 1)
                            if c:
                                act.wait_ge(chunk_done, c)
                            nc.scalar.activation(sa[:, :], psa[:, 0:256], ACT.Copy).then_inc(sa_taken, 1)

                    @block.vector
                    def _(dve):
                        step = Own(dve, own)
                        step.go(nc.vector.memset(state[:, :, :], 0.0))
                        nc.vector.memset(started[:, :, :], 0.0).then_inc(started_ready, 1)
                        step.all()
                        for c in range(NT - 1):
                            for t in range(2):
                                step.go(nc.vector.tensor_scalar(state[:, t, :], state[:, t, :], ends[:, t, c, 2:3], None, ALU.mult))
                            step.all()
                            dve.wait_ge(contrib, c + 1)
                            for t in range(2):
                                step.go(nc.vector.scalar_tensor_tensor(state[:, t, :], pst[:, t, :], ends[:, t, c, 1:2], state[:, t, :],
                                                                       ALU.mult, ALU.add))
                            step.all()
                            dve.wait_ge(chunk_done, c + 1)
                            step(nc.vector.tensor_scalar(started[:, 0, :], state[:, 0, :], ends[:, 0, c + 1, 0:1], None, ALU.mult))
                            nc.vector.tensor_scalar(started[:, 1, :], state[:, 1, :], ends[:, 1, c + 1, 0:1], None,
                                                    ALU.mult).then_inc(started_ready, 1)
                        dve.wait_ge(chunk_done, NT)
                        step(nc.vector.tensor_copy(y[:, :, :], out[:, :, :]))
        normalise(K, [[y[:, 0, :]], [y[:, 1, :]]], [[y[:, 0, :]], [y[:, 1, :]]], K.c("mean64"), 64e-5, True,
                  lambda t: K.col("rwkv_ln_g", t), bias=lambda t: K.col("rwkv_ln_b", t))
        with stage(nc, "own") as (block, own):
            @block.vector
            def _(dve):
                step = Own(dve, own)
                step(nc.vector.tensor_tensor(y[:, :, :], y[:, :, :], bonus[:, :, :], ALU.add))
                step(nc.vector.tensor_tensor(y[:, :, :], y[:, :, :], g[:, :, :], ALU.mult))


def router(K, x, w, b, gates):
    nc = K.nc
    with ExitStack() as ctx:
        lg = K.sb(ctx, "lg", [P, NT, EXPERTS])
        top = K.sb(ctx, "top", [P, NT, 8])
        at = K.sb(ctx, "at", [P, NT, 8], mybir.dt.uint32)
        atf = K.sb(ctx, "atf", [P, NT, 8])
        ex = K.sb(ctx, "ex", [P, NT, 4])
        total = K.sb(ctx, "total", [P, NT, 1])
        one = K.sb(ctx, "onehot", [P, NT, TOP_K, EXPERTS])
        ps = K.ps(ctx, "lg", [P, NT, EXPERTS])
        with stage(nc, "own", "a_own", "logits", "shifted", "exps") as (block, own, a_own, logits, shifted, exps):
            @block.tensor
            def _(pe):
                for j in range(NT):
                    for k in range(DT):
                        nc.tensor.matmul(ps[:, j, :], x[:, k, j * P:(j + 1) * P], w[:, k, :], start=(k == 0), stop=False)
                    mm = nc.tensor.matmul(ps[:, j, :], K.c("ones", 1), b[0:1, :], start=False, stop=True)
                mm.then_inc(logits, 1)

            @block.scalar
            def _(act):
                act.wait_ge(shifted, 1)
                nc.scalar.activation(ex[:, :, :], ex[:, :, :], ACT.Exp).then_inc(exps, 1)

            @block.vector
            def _(dve):
                step = Own(dve, own)
                dve.wait_ge(logits, 1)
                step(nc.vector.tensor_copy(lg[:, :, :], ps[:, :, :]))
                for j in range(NT):
                    step.go(nc.vector.max(top[:, j, :], lg[:, j, :]))
                step.all()
                for j in range(NT):
                    step.go(nc.vector.max_index(at[:, j, :], top[:, j, :], lg[:, j, :]))
                for j in range(NT):
                    ins = nc.vector.tensor_scalar(ex[:, j, :], top[:, j, 0:TOP_K], top[:, j, 0:1], None, ALU.subtract)
                    step.go(ins) if j < NT - 1 else ins.then_inc(shifted, 1)
                step.all()
                step(nc.vector.tensor_copy(atf[:, :, :], at[:, :, :]))
                dve.wait_ge(exps, 1)
                step(nc.vector.tensor_reduce(total[:, :, :], ex[:, :, :], AX.X, ALU.add))
                step(nc.vector.reciprocal(total[:, :, :], total[:, :, :]))
                step(nc.vector.tensor_tensor(ex[:, :, :], ex[:, :, :], total[:, :, :].to_broadcast([P, NT, TOP_K]), ALU.mult))
                for j in range(NT):
                    for k in range(TOP_K):
                        step.go(nc.vector.tensor_scalar(one[:, j, k, :], K.c("iota", P, 0, EXPERTS), atf[:, j, k:k + 1],
                                                        ex[:, j, k:k + 1], ALU.is_equal, ALU.mult))
                step.all()
                step.go(nc.vector.tensor_tensor(one[:, :, 0:2, :], one[:, :, 0:2, :], one[:, :, 2:4, :], ALU.add))
                step.all()
                step(nc.vector.tensor_tensor(gates[:, :, :], one[:, :, 0, :], one[:, :, 1, :], ALU.add))


def experts(K, x, gates, w_gu, w_down, b_gu, b_down, spill, out):
    nc = K.nc
    FJ = FE // P
    with ExitStack() as ctx:
        gfm = K.sb(ctx, "gfm", [EXPERTS, S])
        with ExitStack() as c2:
            bank = K.ps(c2, "bank", [EXPERTS, S])
            with stage(nc, "turned", "taken", "stored") as (block, turned, taken, stored):
                @block.tensor
                def _(pe):
                    for j in range(NT):
                        mm = nc.tensor.transpose(bank[:, j * P:(j + 1) * P], gates[:, j, :], K.c("ident"))
                    mm.then_inc(turned, 1)

                @block.vector
                def _(dve):
                    dve.wait_ge(turned, 1)
                    nc.vector.tensor_copy(gfm[:, :], bank[:, :]).then_inc(taken, 1)

                @block.sync
                def _(sp):
                    sp.wait_ge(taken, 1)
                    sp.dma_start(spill, gfm[:, :]).then_inc(stored, 16)
                    sp.wait_ge(stored, 16)
        with ExitStack() as c2:
            ps = K.ps(c2, "bias", [P, DT, S])
            with stage(nc, "product", "taken") as (block, product, taken):
                @block.tensor
                def _(pe):
                    for i in range(DT):
                        nc.tensor.matmul(ps[:, i, :], b_down[:, i * P:(i + 1) * P], gfm[:, :], start=True, stop=True).then_inc(product, 1)

                @block.vector
                def _(dve):
                    for i in range(DT):
                        dve.wait_ge(product, i + 1)
                        nc.vector.scalar_tensor_tensor(out[:, i, :], x[:, i, :], ALPHA1, ps[:, i, :], ALU.mult, ALU.add).then_inc(taken, 1)
        gu = K.sb(ctx, "gu", [P, FJ, 2 * DT * P])
        dn = K.sb(ctx, "dnw", [P, DT, FJ * P])
        bias = K.sb(ctx, "bias", [P, 2, 2 * FJ])
        gb = K.sb(ctx, "gb", [P, 2, S])
        h = K.sb(ctx, "hact", [P, FJ, S])
        gt = K.sb(ctx, "gt", [P, 2, S])
        vl = K.sb(ctx, "vl", [P, 2, S])
        sg = K.sb(ctx, "sg", [P, 2, S])
        pg = K.ps(ctx, "pg", [P, 2, S])
        pv = K.ps(ctx, "pv", [P, 2, S])
        pd = K.ps(ctx, "pd", [P, 2, S])
        with stage(nc, *[f"gu_in{j}" for j in range(FJ)], *[f"dn_in{i}" for i in range(DT)], "rows_in0", "rows_in1",
                   "up", "clipped", "sigmoid", "value", "glu", "down", "added") as (block, *sems):
            gu_in, dn_in, rows_in = sems[:FJ], sems[FJ:FJ + DT], sems[FJ + DT:FJ + DT + 2]
            up, clipped, sigmoid, value, glu, down, added = sems[FJ + DT + 2:]

            @block.sync
            def _(sp):
                def one(e, j):
                    sp.dma_start(gu[:, j, :], w_gu[bass.ds(e, 1), j, :, :].rearrange("a p k -> (a p) k")).then_inc(gu_in[j], 16)

                def two(e, i):
                    sp.dma_start(dn[:, i, :], w_down[bass.ds(e, 1), i, :, :].rearrange("a p k -> (a p) k")).then_inc(dn_in[i], 16)

                for j in range(FJ):
                    one(0, j)
                for i in range(DT):
                    two(0, i)
                with sp.Fori(1, EXPERTS) as e:
                    for j in range(FJ):
                        sp.wait_ge(up, (e - 1) * FJ + (j + 1))
                        one(e, j)
                    for i in range(DT):
                        sp.wait_ge(down, (e - 1) * DT + (i + 1))
                        two(e, i)

            @block.gpsimd
            def _(pool):
                def rows(e, s):
                    pool.dma_start(gb[:, s, :], spill[bass.ds(e, 1), :].to_broadcast([P, S])).then_inc(rows_in[s], 16)
                    pool.dma_start(bias[:, s, :], b_gu[bass.ds(e, 1), :, :].rearrange("a p k -> (a p) k")).then_inc(rows_in[s], 16)

                rows(0, 0)
                rows(1, 1)
                with pool.Fori(1, EXPERTS // 2) as i:
                    for s in (0, 1):
                        pool.wait_ge(glu, (i - 1) * 2 * FJ + (s * FJ + FJ + 2))
                        rows(i * 2 + s, s)

            @block.tensor
            def _(pe):
                with pe.Fori(0, EXPERTS // 2) as i:
                    for s in (0, 1):
                        for j in range(FJ):
                            pe.wait_ge(gu_in[j], i * 32 + (16 * s + 16))
                            pe.wait_ge(glu, i * 2 * FJ + (s * FJ + j + 1))
                            for bank, o in ((pg, 0), (pv, DT * P)):
                                for k in range(DT):
                                    mm = nc.tensor.matmul(bank[:, j % 2, :], gu[:, j, o + k * P:o + (k + 1) * P], x[:, k, :],
                                                          start=(k == 0), stop=(k == DT - 1))
                            mm.then_inc(up, 1)
                        pe.wait_ge(glu, i * 2 * FJ + (s * FJ + FJ + 2))
                        for t in range(DT):
                            pe.wait_ge(dn_in[t], i * 32 + (16 * s + 16))
                            pe.wait_ge(added, i * 2 * DT + (s * DT + t + 1))
                            for k in range(FJ):
                                mm = nc.tensor.matmul(pd[:, t % 2, :], dn[:, t, k * P:(k + 1) * P], h[:, k, :],
                                                      start=(k == 0), stop=(k == FJ - 1))
                            mm.then_inc(down, 1)

            @block.scalar
            def _(act):
                with act.Fori(0, EXPERTS) as e:
                    for j in range(FJ):
                        act.wait_ge(clipped, e * FJ + (j + 1))
                        nc.scalar.activation(sg[:, j % 2, :], gt[:, j % 2, :], ACT.Sigmoid, scale=SWIGLU_ALPHA).then_inc(sigmoid, 1)

            @block.vector
            def _(dve):
                dve.sem_inc(glu, 2)
                dve.sem_inc(added, 2)
                with dve.Fori(0, EXPERTS // 2) as i:
                    for s in (0, 1):
                        dve.wait_ge(rows_in[s], i * 32 + 32)
                        for j in range(FJ):
                            b, n = j % 2, s * FJ + j
                            dve.wait_ge(up, i * 2 * FJ + (n + 1))
                            nc.vector.tensor_scalar(gt[:, b, :], pg[:, b, :], bias[:, s, j:j + 1], SWIGLU_LIMIT,
                                                    ALU.add, ALU.min).then_inc(clipped, 1)
                            nc.vector.tensor_scalar(vl[:, b, :], pv[:, b, :], bias[:, s, FJ + j:FJ + j + 1], SWIGLU_LIMIT,
                                                    ALU.add, ALU.min).then_inc(value, 1)
                            dve.wait_ge(value, i * 8 * FJ + (4 * n + 1))
                            nc.vector.tensor_scalar(vl[:, b, :], vl[:, b, :], -SWIGLU_LIMIT, 1.0, ALU.max, ALU.add).then_inc(value, 1)
                            dve.wait_ge(value, i * 8 * FJ + (4 * n + 2))
                            nc.vector.tensor_tensor(vl[:, b, :], vl[:, b, :], gt[:, b, :], ALU.mult).then_inc(value, 1)
                            dve.wait_ge(value, i * 8 * FJ + (4 * n + 3))
                            nc.vector.tensor_tensor(vl[:, b, :], vl[:, b, :], gb[:, s, :], ALU.mult).then_inc(value, 1)
                            dve.wait_ge(value, i * 8 * FJ + (4 * n + 4))
                            dve.wait_ge(sigmoid, i * 2 * FJ + (n + 1))
                            nc.vector.tensor_tensor(h[:, j, :], vl[:, b, :], sg[:, b, :], ALU.mult).then_inc(glu, 1)
                        for t in range(DT):
                            dve.wait_ge(down, i * 2 * DT + (s * DT + t + 1))
                            nc.vector.tensor_tensor(out[:, t, :], out[:, t, :], pd[:, t % 2, :], ALU.add).then_inc(added, 1)


def per_layer_embedding(K, h, w_gate, w_proj, p):
    nc = K.nc
    with ExitStack() as ctx:
        pp = K.sb(ctx, "pp", [P, PLE // P, S])
        g = K.sb(ctx, "g", [P, DT, S])
        e = K.sb(ctx, "e", [P, DT, S])
        load(K, [(pp[:, :, :], p)])
        project(K, w_gate, DT, DT, lambda k: h[:, k, :], S, g)
        project(K, w_proj, DT, PLE // P, lambda k: pp[:, k, :], S, e)
        with stage(nc, "gate", "own") as (block, gate, own):
            @block.scalar
            def _(act):
                for t in range(DT):
                    nc.scalar.activation(g[:, t, :], g[:, t, :], ACT.Sigmoid).then_inc(gate, 1)

            @block.vector
            def _(dve):
                step = Own(dve, own)
                for t in range(DT):
                    dve.wait_ge(gate, t + 1)
                    step.go(nc.vector.tensor_tensor(g[:, t, :], g[:, t, :], e[:, t, :], ALU.mult))
                step.all()
                step(nc.vector.tensor_tensor(h[:, :, :], h[:, :, :], g[:, :, :], ALU.add))


def tiles(x, n=DT):
    return [x[:, t, :] for t in range(n)]


def first_block(K, a, x):
    nc = K.nc
    with ExitStack() as ctx:
        y = K.sb(ctx, "y", [P, DT, S])
        with ExitStack() as c2:
            U = K.sb(c2, "U", [P, U_TILES, S])
            gate_up = K.sb(c2, "gate_up", [P, P])
            lora = K.sb(c2, "lora", [P, 256])
            load(K, [(gate_up[ROW_GD:ROW_GD + 16, :], a["gla_gate_up"]), (lora[:, :], a["rwkv_lora"])])
            project(K, a["w_in"], U_TILES, DT, lambda k: x[:, k, :], S, U)
            with ExitStack() as c3:
                conv = K.sb(c3, "conv", [P, 8, S])
                rows = K.sb(c3, "rows", [H, 5, S])
                cols = K.sb(c3, "gate_cols", [P, 3, NT, H])
                short_convs(K, U, conv)
                scalar_gates(K, U, rows, cols)
                ssd(K, U, conv, rows, cols, y[:, 0:2, :])
                mlstm(K, U, conv, rows, cols, y[:, 6:8, :])
            gla(K, U, gate_up, y[:, 4:6, :])
            rwkv(K, U, lora, y[:, 2:4, :])
        project(K, a["w_out"], DT, DT, lambda k: y[:, k, :], S, x, residual=x, alpha=ALPHA1)
        normalise(K, [tiles(x)], [tiles(x)], K.c("mean1024"), 1e-5, True, lambda t: K.col("ln1_g", t),
                  bias=lambda t: K.col("ln1_b", t))
    with ExitStack() as ctx:
        h = K.sb(ctx, "h", [P, DT, S])
        gates = K.sb(ctx, "gates", [P, NT, EXPERTS])
        b_down = K.sb(ctx, "b_down", [EXPERTS, D])
        with ExitStack() as c2:
            rw = K.sb(c2, "rw", [P, DT, EXPERTS])
            rb = K.sb(c2, "rb", [1, EXPERTS])
            load(K, [(rw[:, :, :], a["router_w"]), (rb[:, :], a["router_b"]), (b_down[:, :], a["exp_b_down"])])
            router(K, x, rw, rb, gates)
        experts(K, x, gates, a["exp_w_gu"], a["exp_w_down"], a["exp_b_gu"], b_down, a["gate_rows"], h)
        per_layer_embedding(K, h, a["ple_gate_w"], a["ple_proj"], a["p"])
        normalise(K, [tiles(h)], [tiles(x)], K.c("mean1024"), 1e-5, True, lambda t: K.col("ln2_g", t),
                  bias=lambda t: K.col("ln2_b", t))


DQ, DK, DV = 0, 4, 8
HQ, HFF, HFB, HI, HG = 0, 4, 8, 12, 16
DA_TILES, HG_TILES, MX_TILES = 12, 20, 4
MIX_TILES = 12
TWO_PI_HI = 6.28125
TWO_PI_LO = float(2 * np.pi - 6.28125)
ROUND = 1.5 * 2.0 ** 23


def rope_tables(K, positions, cs, sn):
    nc = K.nc
    with ExitStack() as ctx:
        pi = K.sb(ctx, "pi", [P, S], I32)
        ang = K.sb(ctx, "ang", [P, S])
        k = K.sb(ctx, "k", [P, S])
        with stage(nc, "loaded", "own", "reduced", "done") as (block, loaded, own, reduced, done):
            @block.sync
            def _(sp):
                sp.dma_start(pi[:, :], positions.to_broadcast([P, S])).then_inc(loaded, 16)

            @block.vector
            def _(dve):
                step = Own(dve, own)
                dve.wait_ge(loaded, 16)
                step(nc.vector.tensor_copy(ang[:, :], pi[:, :]))
                step(nc.vector.tensor_scalar(ang[:, :], ang[:, :], K.const[:, CONST["freq"][0]:CONST["freq"][0] + 1], None, ALU.mult))
                step(nc.vector.tensor_scalar(k[:, :], ang[:, :], float(1 / (2 * np.pi)), None, ALU.mult))
                step(nc.vector.tensor_scalar(k[:, :], k[:, :], ROUND, None, ALU.add))
                step(nc.vector.tensor_scalar(k[:, :], k[:, :], ROUND, None, ALU.subtract))
                step(nc.vector.scalar_tensor_tensor(ang[:, :], k[:, :], -TWO_PI_HI, ang[:, :], ALU.mult, ALU.add))
                step(nc.vector.scalar_tensor_tensor(ang[:, :], k[:, :], -TWO_PI_LO, ang[:, :], ALU.mult, ALU.add))
                step(nc.vector.tensor_scalar(ang[:, :], ang[:, :], 3.141592, -3.141592, ALU.min, ALU.max))
                step(nc.vector.scalar_tensor_tensor(k[:, :], ang[:, :], -1.0, ang[:, :], ALU.mult, ALU.max))
                nc.vector.tensor_scalar(k[:, :], k[:, :], -1.0, float(np.pi / 2), ALU.mult, ALU.add).then_inc(reduced, 1)

            @block.scalar
            def _(act):
                act.wait_ge(reduced, 1)
                nc.scalar.activation(sn[:, :], ang[:, :], ACT.Sin).then_inc(done, 1)
                nc.scalar.activation(cs[:, :], k[:, :], ACT.Sin).then_inc(done, 1)


def rope(K, U, n, cs, sn):
    nc = K.nc
    with ExitStack() as ctx:
        t = K.sb(ctx, "t", [P, 2, S])
        ps = K.ps(ctx, "ps", [P, 2, S])
        with stage(nc, "turned", "own", "done") as (block, turned, own, done):
            @block.tensor
            def _(pe):
                for i in range(n):
                    if i >= 2:
                        pe.wait_ge(done, i - 1)
                    nc.tensor.matmul(ps[:, i % 2, :], K.c("rot"), U[:, i, :], start=True, stop=True).then_inc(turned, 1)

            @block.vector
            def _(dve):
                step = Own(dve, own)
                for i in range(n):
                    dve.wait_ge(turned, i + 1)
                    step.go(nc.vector.tensor_tensor(t[:, i % 2, :], ps[:, i % 2, :], sn[:, :], ALU.mult))
                    step(nc.vector.tensor_tensor(U[:, i, :], U[:, i, :], cs[:, :], ALU.mult))
                    nc.vector.tensor_tensor(U[:, i, :], U[:, i, :], t[:, i % 2, :], ALU.add).then_inc(done, 1)


def softmax_attention(K, parts, query, key, n_key, value, scale, neglam, out):
    nc = K.nc
    KT = n_key // P
    steps = [(h, q) for h in range(H) for q in range(NT)]
    with ExitStack() as ctx:
        p = K.sb(ctx, "p", [P, 2, parts, n_key])
        at = K.sb(ctx, "at", [P, 2, KT, S])
        top = K.sb(ctx, "top", [P, 2, 2])
        total = K.sb(ctx, "total", [P, 2, 2])
        sc = K.ps(ctx, "sc", [P, 2, parts, 512])
        tr = K.ps(ctx, "tr", [P, 2, 512])
        po = K.ps(ctx, "po", [P, 2, 512])
        with stage(nc, "own", "scored", "maximum", "exps", "mixed", "turned", "gathered", "summed", "stored") as (
                block, own, scored, maximum, exps, mixed, turned, gathered, summed, stored):
            @block.tensor
            def _(pe):
                def scores(n):
                    h, q = steps[n]
                    if n >= 2:
                        pe.wait_ge(exps, parts * (n - 1))
                    for c in range(parts):
                        mm = nc.tensor.matmul(sc[:, n % 2, c, 0:n_key], query(h, c)[:, q * P:(q + 1) * P], key(h, c),
                                              start=True, stop=True)
                    mm.then_inc(scored, 1)

                scores(0)
                for n, (h, q) in enumerate(steps):
                    if n + 1 < len(steps):
                        scores(n + 1)
                    pe.wait_ge(mixed, n + 1)
                    if n >= 2:
                        pe.wait_ge(gathered, n - 1)
                    for t in range(KT):
                        mm = nc.tensor.transpose(tr[:, n % 2, t * P:(t + 1) * P], p[:, n % 2, 0, t * P:(t + 1) * P], K.c("ident"))
                    mm.then_inc(turned, 1)
                    if q == NT - 1:
                        pe.wait_ge(gathered, n + 1)
                        if h >= 2:
                            pe.wait_ge(stored, h - 1)
                        for t in range(KT):
                            mm = nc.tensor.matmul(po[:, h % 2, :], value(h, t), at[:, h % 2, t, :], start=(t == 0), stop=(t == KT - 1))
                        mm.then_inc(summed, 1)

            @block.scalar
            def _(act):
                def gather(n):
                    h, q = steps[n]
                    act.wait_ge(turned, n + 1)
                    if h >= 2 and q == 0:
                        act.wait_ge(summed, h - 1)
                    nc.scalar.activation(at[:, h % 2, :, q * P:(q + 1) * P], tr[:, n % 2, 0:KT * P].rearrange("p (t q) -> p t q", q=P),
                                         ACT.Copy).then_inc(gathered, 1)

                def store(h):
                    act.wait_ge(summed, h + 1)
                    nc.scalar.activation(out(h), po[:, h % 2, :], ACT.Copy).then_inc(stored, 1)

                for n, (h, q) in enumerate(steps):
                    act.wait_ge(maximum, n + 1)
                    if n >= 2:
                        act.wait_ge(turned, n - 1)
                    for c in range(parts):
                        nc.scalar.activation(p[:, n % 2, c, :], sc[:, n % 2, c, 0:n_key], ACT.Exp, bias=top[:, n % 2, c:c + 1],
                                             scale=scale, accum_out=total[:, n % 2, c:c + 1]).then_inc(exps, 1)
                    if n:
                        gather(n - 1)
                    if q == 1 and h:
                        store(h - 1)
                gather(len(steps) - 1)
                store(H - 1)

            @block.vector
            def _(dve):
                step = Own(dve, own)

                def maxima(n):
                    dve.wait_ge(scored, n + 1)
                    if n >= 2:
                        dve.wait_ge(exps, parts * (n - 1))
                    step(nc.vector.tensor_reduce(top[:, n % 2, 0:parts], sc[:, n % 2, :, 0:n_key], AX.X, ALU.max, negate=True))
                    nc.vector.tensor_scalar(top[:, n % 2, 0:parts], top[:, n % 2, 0:parts], scale, None, ALU.mult).then_inc(maximum, 1)

                maxima(0)
                for n in range(len(steps)):
                    if n + 1 < len(steps):
                        maxima(n + 1)
                    dve.wait_ge(exps, parts * (n + 1))
                    step(nc.vector.reciprocal(total[:, n % 2, 0:parts], total[:, n % 2, 0:parts]))
                    a, b = p[:, n % 2, 0, :], p[:, n % 2, parts - 1, :]
                    if parts == 2:
                        step.go(nc.vector.tensor_scalar(total[:, n % 2, 1:2], total[:, n % 2, 1:2], neglam[:, 0:1], None, ALU.mult))
                        step(nc.vector.tensor_scalar(a, a, total[:, n % 2, 0:1], None, ALU.mult))
                        nc.vector.scalar_tensor_tensor(a, b, total[:, n % 2, 1:2], a, ALU.mult, ALU.add).then_inc(mixed, 1)
                    else:
                        nc.vector.tensor_scalar(a, a, total[:, n % 2, 0:1], None, ALU.mult).then_inc(mixed, 1)


def differential(K, layer, x, w, cs, sn, y):
    nc = K.nc
    lam_init = 0.8 - 0.6 * float(np.exp(-0.3 * layer))
    with ExitStack() as ctx:
        U = K.sb(ctx, "Uda", [P, DA_TILES, S])
        project(K, w, DA_TILES, DT, lambda k: x[:, k, :], S, U)
        vt = K.sb(ctx, "vt", [P, NT, H * P])
        neglam = K.sb(ctx, "neglam", [P, 2])
        pr = K.sb(ctx, "pr", [64, 2])
        with ExitStack() as c2:
            ps = K.ps(c2, "ps", [P, 2])
            with stage(nc, "own", "product", "summed", "exps") as (block, own, product, summed, exps):
                lf = K.col("da_lambda_2", 4 * layer, 64, 4).rearrange("p (a b) -> p a b", b=2)

                @block.vector
                def _(dve):
                    step = Own(dve, own)
                    nc.vector.tensor_tensor(pr[:, :], lf[:, :, 0], lf[:, :, 1], ALU.mult).then_inc(product, 1)
                    dve.wait_ge(exps, 1)
                    step(nc.vector.tensor_tensor(neglam[:, 0:1], neglam[:, 1:2], neglam[:, 0:1], ALU.subtract))
                    step(nc.vector.tensor_scalar(neglam[:, 0:1], neglam[:, 0:1], lam_init, None, ALU.subtract))

                @block.tensor
                def _(pe):
                    pe.wait_ge(product, 1)
                    nc.tensor.matmul(ps[:, :], K.c("ones", 64), pr[:, :], start=True, stop=True).then_inc(summed, 1)

                @block.scalar
                def _(act):
                    act.wait_ge(summed, 1)
                    nc.scalar.activation(neglam[:, :], ps[:, :], ACT.Exp).then_inc(exps, 1)
        rope(K, U, DV, cs, sn)
        transposes(K, [(U[:, DV + t, :], vt[:, :, t * P:(t + 1) * P]) for t in range(H)])
        softmax_attention(K, 2, lambda h, c: U[64 * c:64 * c + 64, DQ + h, :], lambda h, c: U[64 * c:64 * c + 64, DK + h, :],
                          S, lambda h, t: vt[:, t, h * P:(h + 1) * P], 0.125, neglam, lambda h: y[h])
    normalise(K, [[t] for t in y], [[t] for t in y], K.c("mean128"), 1e-6, False, lambda t: K.col("da_norm_g_2", layer),
              scale=1.0 - lam_init)


def memory(K, x, w, w_kv, mem, y):
    with ExitStack() as ctx:
        U = K.sb(ctx, "Umx", [P, MX_TILES, S])
        kv = K.sb(ctx, "kv", [P, 2 * H, MEM])
        vt = K.sb(ctx, "vt", [P, MEM // P, H * P])
        project(K, w, MX_TILES, DT, lambda k: x[:, k, :], S, U)
        with ExitStack() as c2:
            mm = K.sb(c2, "mem", [P, DT, MEM])
            load(K, [(mm[:, :, :], mem)])
            project(K, w_kv, 2 * H, DT, lambda k: mm[:, k, :], MEM, kv)
        transposes(K, [(kv[:, H + t, :], vt[:, :, t * P:(t + 1) * P]) for t in range(H)])
        softmax_attention(K, 1, lambda h, c: U[:, h, :], lambda h, c: kv[:, h, :], MEM,
                          lambda h, t: vt[:, t, h * P:(h + 1) * P], P ** -0.5, None, lambda h: y[h])


def hgrn_direction(K, q, z, lb, back, vt, out, add):
    nc = K.nc
    order = list(range(NT - 1, -1, -1)) if back else list(range(NT))
    with ExitStack() as ctx:
        b = K.sb(ctx, "b", [P, H, S])
        k = K.sb(ctx, "k", [P, H, S])
        e = K.sb(ctx, "e", [P, H, S])
        qe = K.sb(ctx, "qe", [P, H, S])
        ke = K.sb(ctx, "ke", [P, H, S])
        att = K.sb(ctx, "att", [P, NT, H, P])
        one = K.sb(ctx, "one", [P, P])
        with stage(nc, "own", "sigmoid", "ready", "logs", "low_in") as (block, own, sigmoid, ready, logs, low_in):
            @block.scalar
            def _(act):
                nc.scalar.activation(e[:, :, :], z, ACT.Sigmoid).then_inc(sigmoid, 1)
                act.wait_ge(ready, 1)
                nc.scalar.activation(qe[:, :, :], qe[:, :, :], ACT.Ln).then_inc(logs, 1)
                nc.scalar.activation(ke[:, :, :], ke[:, :, :], ACT.Ln, scale=2.0 ** 60).then_inc(logs, 1)

            @block.vector
            def _(dve):
                step = Own(dve, own)
                step.go(nc.vector.memset(one[:, :], 1.0))
                step.go(nc.vector.memset(att[:, :, :, :], 0.0))
                dve.wait_ge(sigmoid, 1)
                if lb is not None:
                    step.all()
                    step(nc.vector.tensor_scalar(k[:, 0, 0:H], lb, -1.0, 1.0, ALU.mult, ALU.add))
                    for h in range(H):
                        step.go(nc.vector.tensor_scalar(e[:, h, :], e[:, h, :], k[:, 0, h:h + 1], lb[:, h:h + 1], ALU.mult, ALU.add))
                step.all()
                step(nc.vector.tensor_scalar(e[:, :, :], e[:, :, :], 1e-20, None, ALU.max))
                step.go(nc.vector.tensor_scalar(k[:, :, :], e[:, :, :], -1.0, 1.0, ALU.mult, ALU.add))
                step.go(nc.vector.tensor_scalar(qe[:, :, :], e[:, :, :], 2.0 ** -60, None, ALU.max))
                nc.vector.tensor_scalar(ke[:, :, :], e[:, :, :], 2.0 ** -60, None, ALU.min).then_inc(ready, 1)
                step.all()
                dve.wait_ge(logs, 2)
                step(nc.vector.tensor_tensor(e[:, :, :], qe[:, :, :], ke[:, :, :], ALU.add))
                for h in range(H):
                    for c in range(NT):
                        to, at = b[:, h, c * P:(c + 1) * P], e[:, h, c * P:(c + 1) * P]
                        if back:
                            to, at = to[:, ::-1], at[:, ::-1]
                        step.go(nc.vector.tensor_tensor_scan(to, one[:, :], at, 0.0, ALU.mult, ALU.add))
                step.all()
        with ExitStack() as c2:
            ps = K.ps(c2, "ps", [P, 4, H, P])
            mask = "bwd" if back else "fwd"
            rounds = [None] + list(range(len(HALVES)))
            with stage(nc, "own", "offset", "size", "decay", "decayed", "product", "kept") as (
                    block, own, offset, size, decay, decayed, product, kept):
                @block.tensor
                def _(pe):
                    for i, lv in enumerate(rounds):
                        if i:
                            pe.wait_ge(decayed, 2 * i)
                        for c in range(NT):
                            n = i * NT + c
                            if n >= 4:
                                pe.wait_ge(kept, n - 3)
                            for h in range(H):
                                left, right = (k, q) if lv is None else (ke, qe)
                                mm = nc.tensor.matmul(ps[:, c, h, :], left[:, h, c * P:(c + 1) * P], right[:, h, c * P:(c + 1) * P],
                                                      start=True, stop=True)
                            mm.then_inc(product, 1)

                @block.scalar
                def _(act):
                    for i in range(len(HALVES)):
                        act.wait_ge(offset, i + 1)
                        nc.scalar.activation(e[:, :, :], e[:, :, :], ACT.Abs).then_inc(size, 1)
                        act.wait_ge(size, i + 1)
                        nc.scalar.activation(e[:, :, :], e[:, :, :], ACT.Exp, scale=-1.0).then_inc(decay, 1)

                @block.vector
                def _(dve):
                    for i, lv in enumerate(rounds):
                        if lv is not None:
                            half = HALVES[lv]
                            pivot = half if back else half - 1
                            bb = b[:, :, :].rearrange("p h (n m) -> p (h n) m", m=2 * half)
                            ee = e[:, :, :].rearrange("p h (n m) -> p (h n) m", m=2 * half)
                            nc.vector.tensor_tensor(ee, bb, bb[:, :, pivot:pivot + 1].to_broadcast([P, H * S // (2 * half), 2 * half]),
                                                    ALU.subtract).then_inc(offset, 1)
                            dve.wait_ge(decay, i)
                            dve.wait_ge(product, i * NT)
                            nc.vector.tensor_tensor(qe[:, :, :], q, e[:, :, :], ALU.mult).then_inc(decayed, 1)
                            nc.vector.tensor_tensor(ke[:, :, :], k[:, :, :], e[:, :, :], ALU.mult).then_inc(decayed, 1)
                            m = K.c(mask, P, lv)
                            dve.wait_ge(decayed, 2 * i)
                        else:
                            m = K.c("ident")
                        m = m.bitcast(I32).unsqueeze(1).to_broadcast([P, H, P])
                        for c in range(NT):
                            dve.wait_ge(product, i * NT + c + 1)
                            nc.vector.copy_predicated(att[:, c, :, :], m, ps[:, c, :, :]).then_inc(kept, 1)
                        dve.wait_ge(kept, (i + 1) * NT)
        ends = K.sb(ctx, "ends", [P, H, NT])
        end = 0 if back else P - 1
        with stage(nc, "own", "offset", "decay") as (block, own, offset, decay):
            @block.vector
            def _(dve):
                step = Own(dve, own)
                bb = b[:, :, :].rearrange("p h (n m) -> p (h n) m", m=P)
                step.go(nc.vector.tensor_copy(ends[:, :, :].rearrange("p h n -> p (h n)").unsqueeze(2), bb[:, :, end:end + 1]))
                nc.vector.tensor_tensor(e[:, :, :].rearrange("p h (n m) -> p (h n) m", m=P),
                                        bb[:, :, end:end + 1].to_broadcast([P, H * NT, P]), bb, ALU.subtract).then_inc(offset, 1)
                step.all()
                dve.wait_ge(decay, 3)
                step.go(nc.vector.tensor_tensor(qe[:, :, :], q, qe[:, :, :], ALU.mult))
                step.go(nc.vector.tensor_tensor(ke[:, :, :], k[:, :, :], e[:, :, :], ALU.mult))
                step.all()

            @block.scalar
            def _(act):
                nc.scalar.activation(qe[:, :, :], b[:, :, :], ACT.Exp).then_inc(decay, 1)
                act.wait_ge(offset, 1)
                nc.scalar.activation(e[:, :, :], e[:, :, :], ACT.Exp).then_inc(decay, 1)
                nc.scalar.activation(ends[:, :, :], ends[:, :, :], ACT.Exp).then_inc(decay, 1)
        kt = e[:, :, :].rearrange("p h (n m) -> p n h m", m=P)
        transposes(K, [(ke[:, h, :], kt[:, :, h, :]) for h in range(H)])
        state = k
        with ExitStack() as c2:
            po = K.ps(c2, "po", [P, H, S])
            kv = K.ps(c2, "kv", [P, 2, H, P])
            with stage(nc, "own", "contrib", "state_ready", "chunk_done") as (block, own, contrib, state_ready, chunk_done):
                @block.tensor
                def _(pe):
                    for i, c in enumerate(order):
                        for h in range(H):
                            mm = nc.tensor.matmul(kv[:, i % 2, h, :], kt[:, c, h, :], vt[:, c, h * P:(h + 1) * P], start=True, stop=True)
                        mm.then_inc(contrib, 1)
                        if i:
                            pe.wait_ge(state_ready, i)
                        for h in range(H):
                            o = po[:, h, c * P:(c + 1) * P]
                            if i:
                                nc.tensor.matmul(o, state[:, h, 0:P], qe[:, h, c * P:(c + 1) * P], start=True, stop=False)
                            mm = nc.tensor.matmul(o, vt[:, c, h * P:(h + 1) * P], att[:, c, h, :], start=(i == 0), stop=True)
                        mm.then_inc(chunk_done, 1)

                @block.vector
                def _(dve):
                    step = Own(dve, own)
                    for i, c in enumerate(order[:-1]):
                        dve.wait_ge(contrib, i + 1)
                        if i:
                            dve.wait_ge(chunk_done, i + 1)
                            for h in range(H):
                                step.go(nc.vector.tensor_scalar(state[:, h, 0:P], state[:, h, 0:P], ends[:, h, c:c + 1], None, ALU.mult))
                            step.all()
                            nc.vector.tensor_tensor(state[:, :, 0:P], state[:, :, 0:P], kv[:, i % 2, :, :], ALU.add).then_inc(state_ready, 1)
                        else:
                            nc.vector.tensor_copy(state[:, :, 0:P], kv[:, 0, :, :]).then_inc(state_ready, 1)
                        dve.wait_ge(state_ready, i + 1)
                    dve.wait_ge(chunk_done, NT)
                    if add:
                        step(nc.vector.tensor_tensor(out, out, po[:, :, :], ALU.add))
                    else:
                        step(nc.vector.tensor_copy(out, po[:, :, :]))


def hgrn(K, layer, x, w, y):
    nc = K.nc
    with ExitStack() as ctx:
        U = K.sb(ctx, "Uhg", [P, HG_TILES, S])
        lb = K.sb(ctx, "lb", [P, 2, H])
        project(K, w, HG_TILES, DT, lambda k: x[:, k, :], S, U)
        vt = K.sb(ctx, "vt", [P, NT, H * P])
        transposes(K, [(U[:, HI + t, :], vt[:, :, t * P:(t + 1) * P]) for t in range(H)])
        with stage(nc, "own", "silu", "diff") as (block, own, silu, diff):
            @block.vector
            def _(dve):
                for i, name in enumerate(("hg_lb_fwd_2", "hg_lb_bwd_2")):
                    nc.vector.tensor_tensor(lb[:, i, :], K.col(name, H, P, H), K.col(name, 0, P, H), ALU.subtract).then_inc(diff, 1)

            @block.scalar
            def _(act):
                nc.scalar.activation(U[:, HQ:HQ + H, :], U[:, HQ:HQ + H, :], ACT.Silu).then_inc(silu, 1)
                nc.scalar.activation(U[:, HG:HG + H, :], U[:, HG:HG + H, :], ACT.Silu).then_inc(silu, 1)
                act.wait_ge(diff, 2)
                nc.scalar.activation(lb[:, :, :], lb[:, :, :], ACT.Sigmoid).then_inc(silu, 1)
        for i, back in enumerate((False, True)):
            z = U[:, (HFB if back else HFF):(HFB if back else HFF) + H, :]
            hgrn_direction(K, U[:, HQ:HQ + H, :], z, lb[:, i, :] if layer else None, back, vt, y, back)
        normalise(K, [[y[:, h, :]] for h in range(H)], [[y[:, h, :]] for h in range(H)], K.c("mean128"), 1e-6, False,
                  lambda t: K.col("hg_norm_g_2", layer), gate=lambda t: U[:, HG + t, :])


def conv_up(K, layer, x, w, act_out):
    nc = K.nc
    wcol, bcol = COLS["conv_w_2"][0] + 3 * 2 * FT * layer, COLS["conv_b_2"][0] + 2 * FT * layer
    with ExitStack() as ctx:
        ring = K.sb(ctx, "ring", [P, 2, 2 * DT * P])
        cv = K.sb(ctx, "cv", [P, 2, 2, S])
        sg = K.sb(ctx, "sg", [P, 2, S])
        ps = K.ps(ctx, "ps", [P, 2, 2, S])
        with stage(nc, "in0", "in1", "up", "centre", "sides", "value", "silu", "done") as (
                block, in0, in1, up, centre, sides, value, silu, done):
            loaded = (in0, in1)

            @block.sync
            def _(sp):
                for s in (0, 1):
                    sp.dma_start(ring[:, s, :], w[s]).then_inc(loaded[s], 16)
                with sp.Fori(1, FT // 2) as i:
                    for s in (0, 1):
                        sp.wait_ge(up, (i - 1) * 2 + (s + 1))
                        sp.dma_start(ring[:, s, :], w[bass.ds(i * 2 + s, 1), :, :].rearrange("a p k -> (a p) k")).then_inc(loaded[s], 16)

            @block.tensor
            def _(pe):
                with pe.Fori(0, FT // 2) as i:
                    for s in (0, 1):
                        pe.wait_ge(loaded[s], i * 16 + 16)
                        pe.wait_ge(done, i * 2 + (s + 1))
                        for g in (0, 1):
                            for k in range(DT):
                                mm = nc.tensor.matmul(ps[:, s, g, :], ring[:, s, (g * DT + k) * P:(g * DT + k + 1) * P], x[:, k, :],
                                                      start=(k == 0), stop=(k == DT - 1))
                        mm.then_inc(up, 1)

            @block.scalar
            def _(act):
                with act.Fori(0, FT // 2) as i:
                    for s in (0, 1):
                        act.wait_ge(up, i * 2 + (s + 1))
                        for g in (0, 1):
                            j = i * 2 + (s + FT * g)
                            nc.scalar.activation(cv[:, s, g, :], ps[:, s, g, :], ACT.Identity,
                                                 bias=K.cols[:, bass.ds(j + bcol, 1)],
                                                 scale=K.cols[:, bass.ds(j + (wcol + 2 * FT), 1)]).then_inc(centre, 1)
                        act.wait_ge(sides, i * 8 + (4 * s + 4))
                        nc.scalar.activation(sg[:, s, :], cv[:, s, 0, :], ACT.Silu).then_inc(silu, 1)

            @block.vector
            def _(dve):
                dve.sem_inc(done, 2)
                with dve.Fori(0, FT // 2) as i:
                    for s in (0, 1):
                        dve.wait_ge(centre, i * 4 + (2 * s + 2))
                        for g in (0, 1):
                            nc.vector.scalar_tensor_tensor(cv[:, s, g, 1:S], ps[:, s, g, 0:S - 1],
                                                           K.cols[:, bass.ds(i * 2 + (s + FT * g + wcol), 1)], cv[:, s, g, 1:S],
                                                           ALU.mult, ALU.add).then_inc(sides, 1)
                        for g in (0, 1):
                            dve.wait_ge(sides, i * 8 + (4 * s + g + 1))
                            nc.vector.scalar_tensor_tensor(cv[:, s, g, 0:S - 1], ps[:, s, g, 1:S],
                                                           K.cols[:, bass.ds(i * 2 + (s + FT * g + wcol + 4 * FT), 1)],
                                                           cv[:, s, g, 0:S - 1], ALU.mult, ALU.add).then_inc(sides, 1)
                        dve.wait_ge(sides, i * 8 + (4 * s + 4))
                        dve.wait_ge(silu, i * 2 + (s + 1))
                        nc.vector.tensor_tensor(act_out[:, bass.ds(i * 2 + s, 1), :], cv[:, s, 1:2, :], sg[:, s:s + 1, :],
                                                ALU.mult).then_inc(done, 1)


def second_layer(K, a, layer, x, cs, sn):
    with ExitStack() as ctx:
        y = K.sb(ctx, "mix", [P, MIX_TILES, S])
        t = tiles(y, MIX_TILES)
        w = a["w_in_2"][layer]
        differential(K, layer, x, w[0:12], cs, sn, t[0:4])
        hgrn(K, layer, x, w[12:32], y[:, 4:8, :])
        memory(K, x, w[32:36], a["w_mem_kv_2"][layer], a["mem_2"], t[8:12])
        project(K, a["w_out_2"][layer], DT, MIX_TILES, lambda k: y[:, k, :], S, x, residual=x, alpha=ALPHA2)
    normalise(K, [tiles(x)], [tiles(x)], K.c("mean1024"), 1e-5, True, lambda t: K.col("ln1_g_2", 8 * layer + t),
              bias=lambda t: K.col("ln1_b_2", 8 * layer + t))
    with ExitStack() as ctx:
        h = K.sb(ctx, "h", [P, FT, S])
        conv_up(K, layer, x, a["w_up_2"][layer], h)
        project(K, a["w_down_2"][layer], DT, FT, lambda k: h[:, k, :], S, x, residual=x, alpha=ALPHA2)
    normalise(K, [tiles(x)], [tiles(x)], K.c("mean1024"), 1e-5, True, lambda t: K.col("ln2_g_2", 8 * layer + t),
              bias=lambda t: K.col("ln2_b_2", 8 * layer + t))


def second_block(K, a, x):
    with ExitStack() as ctx:
        cs = K.sb(ctx, "cs", [P, S])
        sn = K.sb(ctx, "sn", [P, S])
        rope_tables(K, a["positions_2"], cs, sn)
        normalise(K, [tiles(x)], [tiles(x)], K.c("mean1024"), 1e-5, True, lambda t: K.col("ln_in_g_2", t),
                  bias=lambda t: K.col("ln_in_b_2", t))
        for layer in (0, 1):
            second_layer(K, a, layer, x, cs, sn)


def lay_out(i):
    i = {k: np.asarray(v) for k, v in i.items()}
    rw = i["router_w"][0]
    return {
        "const": constants(), "cols": pack_columns(i), "x": fm(i["x"][0]), "p": fm(i["p"][0, 0]),
        "w_in": pack_w_in(i["w_in"][0]), "w_out": tiles_of(i["w_out"][0]),
        "gla_gate_up": i["gla_gate_up"][0],
        "rwkv_lora": np.concatenate([i["rwkv_w_up"][0], i["rwkv_a_up"][0], i["rwkv_g_up"][0]], 0),
        "router_w": np.ascontiguousarray(rw.reshape(DT, P, EXPERTS).transpose(1, 0, 2)), "router_b": i["router_b"],
        "exp_w_gu": np.ascontiguousarray(i["exp_w_gu"][0].reshape(EXPERTS, DT, P, 2, FE // P, P)
                                         .transpose(0, 4, 2, 3, 1, 5)).reshape(EXPERTS, FE // P, P, 2 * D),
        "exp_w_down": np.ascontiguousarray(i["exp_w_down"][0].reshape(EXPERTS, FE // P, P, DT, P)
                                           .transpose(0, 3, 2, 1, 4)).reshape(EXPERTS, DT, P, FE),
        "exp_b_gu": np.ascontiguousarray(i["exp_b_gu"][0].reshape(EXPERTS, 2 * FE // P, P).transpose(0, 2, 1)),
        "exp_b_down": i["exp_b_down"][0],
        "ple_gate_w": tiles_of(i["ple_gate_w"][0]), "ple_proj": tiles_of(i["ple_proj"][0]),
        "mem_2": fm(i["mem_2"][0]), "positions_2": i["positions_2"],
        "w_in_2": np.stack([tiles_of(w) for w in i["w_in_2"]]),
        "w_mem_kv_2": np.stack([tiles_of(w) for w in i["w_mem_kv_2"]]),
        "w_out_2": np.stack([tiles_of(w) for w in i["w_out_2"]]),
        "w_up_2": np.ascontiguousarray(i["w_up_2"].reshape(2, DT, P, 2, FT, P).transpose(0, 4, 2, 3, 1, 5)).reshape(2, FT, P, 2 * D),
        "w_down_2": np.stack([tiles_of(w) for w in i["w_down_2"]]),
    }


def build(nc, a, out):
    with ExitStack() as ctx:
        const = ctx.enter_context(nc.sbuf_tensor("const", [P, CONST_W], F32))
        cols = ctx.enter_context(nc.sbuf_tensor("cols", [P, COLS_W], F32))
        x = ctx.enter_context(nc.sbuf_tensor("x", [P, DT, S], F32))
        K = Kit(nc, const, cols)
        load(K, [(const[:, :], a["const"]), (cols[:, :], a["cols"]), (x[:, :, :], a["x"])])
        first_block(K, a, x)
        second_block(K, a, x)
        with stage(nc, "stored") as (block, stored):
            @block.sync
            def _(sp):
                sp.dma_start(out, x[:, :, :]).then_inc(stored, 16)
                sp.wait_ge(stored, 16)


def kernel(**inputs):
    import concourse.bacc as bacc
    from concourse.bass_utils import run_bass_kernel_spmd

    arrays = lay_out(inputs)
    nc = bacc.Bacc("TRN2", target_bir_lowering=False, num_devices=1)
    a = {n: nc.dram_tensor(f"in_{n}", v.shape, mybir.dt.from_np(v.dtype), kind="ExternalInput").ap() for n, v in arrays.items()}
    a["gate_rows"] = nc.dram_tensor("gate_rows", (EXPERTS, S), F32, kind="Internal").ap()
    out = nc.dram_tensor("out", (P, DT, S), F32, kind="ExternalOutput").ap()
    build(nc, a, out)
    r = run_bass_kernel_spmd(nc, [{f"in_{n}": v for n, v in arrays.items()}], core_ids=[0])
    y = r.results[0]["out"]
    return np.ascontiguousarray(np.asarray(y).transpose(2, 1, 0)).reshape(1, S, D)
```

```python
from contextlib import ExitStack, contextmanager

import numpy as np
import concourse.bass as bass
from concourse import mybir

F32 = mybir.dt.float32
I32 = mybir.dt.int32
F32R = mybir.dt.float32r
ALU = mybir.AluOpType
ACT = mybir.ActivationFunctionType
AX = mybir.AxisListType

P = 128
S = 512
NT = S // P
D = 1024
DT = D // P
H = 4
EXPERTS, TOP_K, FE = 32, 4, 1024
FF = 2816
FT = FF // P
MEM = 256
PLE = 256
ALPHA1 = 2 ** 0.25
ALPHA2 = 4 ** 0.25
SWIGLU_LIMIT, SWIGLU_ALPHA = 7.0, 1.702
HALVES = [1, 2, 4, 8, 16, 32, 64]

Z, XR, BM, CM = 0, 2, 4, 5
R_, K_, V_, LORA = 6, 8, 10, 12
GQ, GK, GV, GOG = 13, 14, 15, 17
MQ, MK, MV, MOG = 19, 21, 23, 25
NARROW, U_TILES = 27, 28
ROW_DT, ROW_I, ROW_F, ROW_GD = 0, 32, 64, 96
SSD0, RWKV0, GLA0, MLSTM0 = 0, 772, 1668, 2452

CONST = {}
_at = 0
for _name, _n in [("ident", P), ("causal", P), ("strict", P), ("anti", P), ("fwd", 7 * P), ("bwd", 7 * P),
                  ("ones", P), ("mean256", P), ("mean1024", P), ("mean128", P), ("mean64", P), ("sum64", P),
                  ("pick", H * P), ("pickneg", H * P), ("glamask", 2 * P), ("rot", P), ("freq", 1), ("iota", P), ("slot", 1)]:
    CONST[_name] = (_at, _n)
    _at += _n
CONST_W = _at


def constants():
    c = np.zeros((P, CONST_W), np.float32)

    def put(name, a):
        o, n = CONST[name]
        c[:a.shape[0], o:o + n] = a

    i = np.arange(P)
    s, t = i[:, None], i[None, :]
    put("ident", np.eye(P))
    put("causal", (t >= s) * 1.0)
    put("strict", (t > s) * 1.0)
    put("anti", (t <= s) * 1.0)
    lev = [((s // (2 * h) == t // (2 * h)) & (s % (2 * h) < h) & (t % (2 * h) >= h)) * 1.0 for h in HALVES]
    put("fwd", np.concatenate(lev, 1))
    put("bwd", np.concatenate([m.T for m in lev], 1))
    put("ones", np.ones((P, P)))
    put("mean256", np.full((P, P), 1 / 256))
    put("mean1024", np.full((P, P), 1 / D))
    put("mean128", np.full((P, P), 1 / P))
    put("mean64", (s // 64 == t // 64) / 64.0)
    put("sum64", (s // 64 == t // 64) * 1.0)
    pick = np.zeros((H, H, P))
    pick[np.arange(H), np.arange(H)] = 1
    put("pick", pick.reshape(H, H * P))
    put("pickneg", -pick.reshape(H, H * P))
    put("glamask", (s // 32 == np.arange(2 * P)[None, :] // 64) * 1.0)
    rot = np.zeros((P, P))
    for b in (0, 64):
        for d in range(8):
            rot[b + d + 8, b + d] = -1
            rot[b + d, b + d + 8] = 1
    put("rot", rot)
    inv = np.float32(500000.0) ** (-np.arange(0, 16, 2, dtype=np.float32) / np.float32(16))
    f = np.zeros((P, 1), np.float32)
    for b in (0, 8, 64, 72):
        f[b:b + 8, 0] = inv
    put("freq", f)
    put("iota", np.tile(i.astype(np.float32), (P, 1)))
    put("slot", s.astype(np.float32))
    return c


COLS = {}
_at = 0
for _name, _n in [("ssd_conv_w", 16), ("ssd_conv_b", 4), ("mlstm_conv_w", 16), ("mlstm_conv_b", 4),
                  ("ssd_d", 2), ("ssd_norm_g", 2), ("ssd_dt_bias", 1), ("ssd_a_log", 1), ("mlstm_i_b", 1),
                  ("mlstm_f_b", 1), ("rwkv_mu", 7), ("rwkv_w0", 2), ("rwkv_a0", 2), ("rwkv_k_k", 2),
                  ("rwkv_k_a", 2), ("rwkv_r_k", 2), ("rwkv_ln_g", 2), ("rwkv_ln_b", 2), ("gla_gate_b", 1),
                  ("gla_norm_g", 2), ("mlstm_norm_g", 2), ("ln1_g", 8), ("ln1_b", 8), ("ln2_g", 8),
                  ("ln2_b", 8), ("ln_in_g_2", 8), ("ln_in_b_2", 8), ("ln1_g_2", 16), ("ln1_b_2", 16),
                  ("ln2_g_2", 16), ("ln2_b_2", 16), ("da_norm_g_2", 2), ("hg_norm_g_2", 2),
                  ("hg_lb_fwd_2", 8), ("hg_lb_bwd_2", 8), ("conv_w_2", 2 * 3 * 44), ("conv_b_2", 2 * 44),
                  ("da_lambda_2", 8)]:
    COLS[_name] = (_at, _n)
    _at += _n
COLS_W = _at


def pack_columns(i):
    c = np.zeros((P, COLS_W), np.float32)
    for name, (o, n) in COLS.items():
        a = np.asarray(i[name])
        if name == "ssd_d":
            a = np.repeat(a, 64)
        a = a.reshape(-1)
        if name in ("ssd_dt_bias", "ssd_a_log", "mlstm_i_b", "mlstm_f_b"):
            c[:H, o] = a
        elif name == "da_lambda_2":
            c[:64, o:o + n] = a.reshape(n, 64).T
        else:
            c[:, o:o + n] = a.reshape(n, P).T
    return c


def tiles_of(w):
    k, f = w.shape
    return np.ascontiguousarray(w.reshape(k // P, P, f // P, P).transpose(2, 1, 0, 3)).reshape(f // P, P, -1)


def pack_w_in(w):
    cols = [w[:, SSD0:SSD0 + 768], w[:, RWKV0:RWKV0 + 896], w[:, GLA0:GLA0 + 512],
            w[:, GLA0 + 528:GLA0 + 784], w[:, MLSTM0:MLSTM0 + 768], w[:, MLSTM0 + 776:MLSTM0 + 1032]]
    narrow = np.zeros((D, P), w.dtype)
    narrow[:, ROW_DT:ROW_DT + 4] = w[:, 768:772]
    narrow[:, ROW_I:ROW_I + 4] = w[:, MLSTM0 + 768:MLSTM0 + 772]
    narrow[:, ROW_F:ROW_F + 4] = w[:, MLSTM0 + 772:MLSTM0 + 776]
    narrow[:, ROW_GD:ROW_GD + 16] = w[:, GLA0 + 512:GLA0 + 528]
    return tiles_of(np.concatenate(cols + [narrow], 1))


def fm(a):
    return np.ascontiguousarray(a.reshape(a.shape[0], -1, P).transpose(2, 1, 0))


@contextmanager
def stage(nc, *names):
    with ExitStack() as ctx:
        sems = [ctx.enter_context(nc.semaphore(n)) for n in names]
        with nc.Block() as block:
            yield (block, *sems)
        nc.clear_and_free_semaphores(sems)
        nc.all_engine_barrier()


class Own:

    def __init__(self, eng, sem):
        self.eng, self.sem, self.n = eng, sem, 0

    def __call__(self, ins):
        self.n += 1
        ins.then_inc(self.sem, 1)
        self.eng.wait_ge(self.sem, self.n)

    def go(self, ins):
        self.n += 1
        ins.then_inc(self.sem, 1)

    def all(self):
        self.eng.wait_ge(self.sem, self.n)


class Kit:

    def __init__(self, nc, const, cols):
        self.nc, self.const, self.cols, self.made = nc, const, cols, 0

    def sb(self, ctx, name, shape, dtype=F32):
        self.made += 1
        return ctx.enter_context(self.nc.sbuf_tensor(f"{name}_{self.made}", shape, dtype))

    def ps(self, ctx, name, shape):
        self.made += 1
        return ctx.enter_context(self.nc.psum_tensor(f"{name}_{self.made}", shape, F32))

    def c(self, name, rows=P, part=None, width=P, base=0):
        o, n = CONST[name]
        if part is not None:
            o, n = o + part * width, width
        return self.const[base:rows, o:o + n]

    def col(self, name, k=0, rows=P, n=1):
        o = COLS[name][0] + k
        return self.cols[0:rows, o:o + n]


def load(K, pairs):
    nc = K.nc
    with stage(nc, "loaded") as (block, loaded):
        @block.sync
        def _(sp):
            for dst, src in pairs:
                sp.dma_start(dst, src).then_inc(loaded, 16)
            sp.wait_ge(loaded, 16 * len(pairs))


SLOT = [2 * (h % 2) + h // 2 for h in range(H)]


def split(K, x, high, low):
    nc = K.nc
    with stage(nc, "high_ready", "low_ready") as (block, high_ready, low_ready):
        @block.scalar
        def _(act):
            for k in range(x.shape[1]):
                nc.scalar.activation(high[:, k, :], x[:, k, :], ACT.Copy).then_inc(high_ready, 1)

        @block.vector
        def _(dve):
            for k in range(x.shape[1]):
                dve.wait_ge(high_ready, k + 1)
                nc.vector.tensor_tensor(low[:, k, :], x[:, k, :], high[:, k, :], ALU.subtract).then_inc(low_ready, 1)


def project(K, w, n_tiles, kt, high, low, n, out, residual=None, alpha=1.0, ring=4):
    nc = K.nc
    rounds = n_tiles // ring
    assert rounds * ring == n_tiles
    with ExitStack() as ctx:
        raw = K.sb(ctx, "w_raw", [P, ring, kt * P])
        wh = K.sb(ctx, "w_high", [P, ring, kt * P], F32R)
        wl = K.sb(ctx, "w_low", [P, ring, kt * P], F32R)
        acc = K.ps(ctx, "acc", [P, ring, 512])
        with stage(nc, *[f"loaded{r}" for r in range(ring)], "high_ready", "low_ready", "product", "taken") as (block, *sems):
            loaded, (high_ready, low_ready, product, taken) = sems[:ring], sems[ring:]

            @block.sync
            def _(sp):
                for r in range(ring):
                    sp.dma_start(raw[:, r, :], w[r]).then_inc(loaded[r], 16)
                if rounds > 1:
                    with sp.Fori(1, rounds) as i:
                        for r in range(ring):
                            sp.wait_ge(low_ready, (i - 1) * ring + (r + 1))
                            sp.dma_start(raw[:, r, :], w[bass.ds(i * ring + r, 1), :, :].rearrange("a p k -> (a p) k")).then_inc(loaded[r], 16)

            @block.scalar
            def _(act):
                def round_of(i, first):
                    for r in range(ring):
                        act.wait_ge(loaded[r], i * 16 + 16)
                        if not first:
                            act.wait_ge(product, (i - 1) * ring + (r + 1))
                        nc.scalar.activation(wh[:, r, :], raw[:, r, :], ACT.Copy).then_inc(high_ready, 1)

                round_of(0, True)
                if rounds > 1:
                    with act.Fori(1, rounds) as i:
                        round_of(i, False)

            @block.vector
            def _(dve):
                def take(i, r):
                    dve.wait_ge(product, i * ring + (r + 1))
                    if residual is None:
                        ins = nc.vector.tensor_copy(out[:, bass.ds(i * ring + r, 1), :], acc[:, r:r + 1, 0:n])
                    else:
                        ins = nc.vector.scalar_tensor_tensor(
                            out[:, bass.ds(i * ring + r, 1), :], residual[:, bass.ds(i * ring + r, 1), :],
                            alpha, acc[:, r:r + 1, 0:n], ALU.mult, ALU.add)
                    ins.then_inc(taken, 1)

                def round_of(i, first):
                    for r in range(ring):
                        dve.wait_ge(high_ready, i * ring + (r + 1))
                        nc.vector.tensor_tensor(wl[:, r, :], raw[:, r, :], wh[:, r, :], ALU.subtract).then_inc(low_ready, 1)
                        if r:
                            take(i, r - 1)
                        elif not first:
                            take(i - 1, ring - 1)

                round_of(0, True)
                if rounds > 1:
                    with dve.Fori(1, rounds) as i:
                        round_of(i, False)
                take(rounds - 1, ring - 1)

            @block.tensor
            def _(pe):
                def round_of(i, first):
                    for r in range(ring):
                        pe.wait_ge(low_ready, i * ring + (r + 1))
                        if not first:
                            pe.wait_ge(taken, (i - 1) * ring + (r + 1))
                        for k in range(kt):
                            c = slice(k * P, (k + 1) * P)
                            nc.tensor.matmul(acc[:, r, 0:n], wh[:, r, c], high[:, k, :], start=(k == 0), stop=False)
                            nc.tensor.matmul(acc[:, r, 0:n], wh[:, r, c], low[:, k, :], start=False, stop=False)
                            mm = nc.tensor.matmul(acc[:, r, 0:n], wl[:, r, c], high[:, k, :], start=False, stop=(k == kt - 1))
                        mm.then_inc(product, 1)

                round_of(0, True)
                if rounds > 1:
                    with pe.Fori(1, rounds) as i:
                        round_of(i, False)


@contextmanager
def parts_of(K, x, n=S):
    with ExitStack() as ctx:
        high = K.sb(ctx, "x_high", [P, x.shape[1], n], F32R)
        low = K.sb(ctx, "x_low", [P, x.shape[1], n], F32R)
        split(K, x, high, low)
        yield high, low


def normalise(K, x, out, mean, eps, center, gain, bias=None, gate=None, scale=None):
    nc = K.nc
    flat = [t for g in x for t in g]
    oflat = [t for g in out for t in g]
    n = len(x[0])
    with ExitStack() as ctx:
        sq = K.sb(ctx, "sq", [P, n, S])
        sd = K.sb(ctx, "sd", [P, 2, S])
        ms = K.ps(ctx, "ms", [P, 2, S])
        mu = K.ps(ctx, "mu", [P, 2, S])
        with stage(nc, "mean_ready", "centred", "squared", "var_ready", "eps_added", "root", "own", "normed") as (
                block, mean_ready, centred, squared, var_ready, eps_added, root, own, normed):
            src = (lambda g, j: out[g][j]) if center else (lambda g, j: x[g][j])

            @block.tensor
            def _(pe):
                for g in range(len(x)):
                    if center:
                        if g >= 2:
                            pe.wait_ge(centred, n * (g - 1))
                        for j in range(n):
                            mm = nc.tensor.matmul(mu[:, g % 2, :], mean, x[g][j], start=(j == 0), stop=(j == n - 1))
                        mm.then_inc(mean_ready, 1)
                    pe.wait_ge(squared, n * (g + 1))
                    if g >= 2:
                        pe.wait_ge(eps_added, g - 1)
                    for j in range(n):
                        mm = nc.tensor.matmul(ms[:, g % 2, :], mean, sq[:, j, :], start=(j == 0), stop=(j == n - 1))
                    mm.then_inc(var_ready, 1)

            @block.scalar
            def _(act):
                for g in range(len(x)):
                    if g:
                        act.wait_ge(var_ready, g)
                    for j in range(n):
                        if center:
                            act.wait_ge(centred, n * g + j + 1)
                        nc.scalar.activation(sq[:, j, :], src(g, j), ACT.Square).then_inc(squared, 1)
                    act.wait_ge(eps_added, g + 1)
                    nc.scalar.activation(sd[:, g % 2, :], sd[:, g % 2, :], ACT.Sqrt).then_inc(root, 1)

            @block.vector
            def _(dve):
                step = Own(dve, own)
                for g in range(len(x)):
                    if center:
                        dve.wait_ge(mean_ready, g + 1)
                        for j in range(n):
                            nc.vector.tensor_tensor(out[g][j], x[g][j], mu[:, g % 2, :], ALU.subtract).then_inc(centred, 1)
                        dve.wait_ge(centred, n * (g + 1))
                    dve.wait_ge(var_ready, g + 1)
                    nc.vector.tensor_scalar(sd[:, g % 2, :], ms[:, g % 2, :], eps, None, ALU.add).then_inc(eps_added, 1)
                    dve.wait_ge(root, g + 1)
                    step(nc.vector.reciprocal(sd[:, g % 2, :], sd[:, g % 2, :]))
                    for j in range(n):
                        step.go(nc.vector.scalar_tensor_tensor(out[g][j], src(g, j), gain(n * g + j), sd[:, g % 2, :],
                                                               ALU.mult, ALU.mult))
                    step.all()
                    for j in range(n):
                        if bias is not None:
                            step.go(nc.vector.tensor_scalar(out[g][j], out[g][j], bias(n * g + j), None, ALU.add))
                        if scale is not None:
                            step.go(nc.vector.tensor_scalar(out[g][j], out[g][j], scale, None, ALU.mult))
                        if gate is not None:
                            step.go(nc.vector.tensor_tensor(out[g][j], out[g][j], gate(n * g + j), ALU.mult))
                    step.all()


def transposes(K, items):
    nc = K.nc
    with ExitStack() as ctx:
        bank = K.ps(ctx, "bank", [P, 4, NT, P])
        with stage(nc, "turned", "taken_v", "taken_a") as (block, turned, taken_v, taken_a):
            @block.tensor
            def _(pe):
                for n, (src, dst) in enumerate(items):
                    rows, wide = src.shape[0], src.shape[1] // P
                    if n >= 4:
                        pe.wait_ge(taken_a if n % 2 else taken_v, (n - 4) // 2 + 1)
                    for j in range(wide):
                        mm = nc.tensor.transpose(bank[:, n % 4, j, 0:rows], src[:, j * P:(j + 1) * P],
                                                 K.c("ident", rows, 0, rows))
                    mm.then_inc(turned, 1)

            @block.vector
            def _(dve):
                for n, (src, dst) in enumerate(items):
                    if n % 2 == 0:
                        dve.wait_ge(turned, n + 1)
                        nc.vector.tensor_copy(dst, bank[:, n % 4, 0:src.shape[1] // P, 0:src.shape[0]]).then_inc(taken_v, 1)

            @block.scalar
            def _(act):
                for n, (src, dst) in enumerate(items):
                    if n % 2 == 1:
                        act.wait_ge(turned, n + 1)
                        nc.scalar.activation(dst, bank[:, n % 4, 0:src.shape[1] // P, 0:src.shape[0]], ACT.Copy).then_inc(taken_a, 1)


def short_convs(K, U, conv):
    nc = K.nc
    tiles = [(XR + t, "ssd_conv", t) for t in range(4)] + [(MQ + t, "mlstm_conv", t) for t in range(4)]
    with stage(nc, "own", "convolved", "active") as (block, own, convolved, active):
        @block.vector
        def _(dve):
            step = Own(dve, own)
            for n, (u, name, t) in enumerate(tiles):
                step.go(nc.vector.tensor_scalar(conv[:, n, :], U[:, u, :], K.col(name + "_w", 12 + t),
                                                K.col(name + "_b", t), ALU.mult, ALU.add))
            for back in (1, 2, 3):
                step.all()
                for n, (u, name, t) in enumerate(tiles):
                    ins = nc.vector.scalar_tensor_tensor(conv[:, n, back:S], U[:, u, 0:S - back],
                                                         K.col(name + "_w", 4 * (3 - back) + t), conv[:, n, back:S],
                                                         ALU.mult, ALU.add)
                    if back < 3:
                        step.go(ins)
                    else:
                        ins.then_inc(convolved, 1)

        @block.scalar
        def _(act):
            for n in range(8):
                act.wait_ge(convolved, n + 1)
                nc.scalar.activation(conv[:, n, :], conv[:, n, :], ACT.Silu).then_inc(active, 1)


def scalar_gates(K, U, rows, cols):
    nc = K.nc
    with ExitStack() as ctx:
        t = K.sb(ctx, "gate_t", [H, 4, S])
        e = K.sb(ctx, "gate_e", [H, 2, S])
        one = K.sb(ctx, "gate_one", [H, S])
        a = K.sb(ctx, "gate_a", [H, 1])
        picked = K.ps(ctx, "picked", [H, 3, S])
        turned = K.ps(ctx, "turned", [P, 3, NT, H])
        with stage(nc, "rows_picked", "own", "abs_ready", "exp_ready", "log_ready", "rows_ready", "em_in",
                   "em_out", "cols_turned", "a_ready") as (
                block, rows_picked, own, abs_ready, exp_ready, log_ready, rows_ready, em_in, em_out,
                cols_turned, a_ready):
            @block.tensor
            def _(pe):
                for n, r in enumerate((ROW_DT, ROW_I, ROW_F)):
                    mm = nc.tensor.matmul(picked[:, n, :], K.c("ident")[:, r:r + H], U[:, NARROW, :], start=True, stop=True)
                mm.then_inc(rows_picked, 1)
                pe.wait_ge(rows_ready, 1)
                for n, q in enumerate((0, 1, 2)):
                    for j in range(NT):
                        mm = nc.tensor.transpose(turned[:, n, j, :], rows[:, q, j * P:(j + 1) * P], K.c("ident", H, 0, H))
                mm.then_inc(cols_turned, 1)

            @block.scalar
            def _(act):
                nc.scalar.activation(a[:, :], K.col("ssd_a_log", rows=H), ACT.Exp).then_inc(a_ready, 1)
                act.wait_ge(abs_ready, 2)
                nc.scalar.activation(e[:, :, :], e[:, :, :], ACT.Exp, scale=-1.0).then_inc(exp_ready, 1)
                act.wait_ge(exp_ready, 1)
                nc.scalar.activation(e[:, :, :], e[:, :, :], ACT.Ln, bias=1.0).then_inc(log_ready, 1)
                act.wait_ge(em_in, 1)
                nc.scalar.activation(rows[:, 4, :], t[:, 3, :], ACT.Exp).then_inc(em_out, 1)

            @block.vector
            def _(dve):
                step = Own(dve, own)
                step.go(nc.vector.memset(one[:, :], 1.0))
                dve.wait_ge(rows_picked, 1)
                for n, name in enumerate(("ssd_dt_bias", "mlstm_i_b", "mlstm_f_b")):
                    step.go(nc.vector.tensor_scalar(t[:, n, :], picked[:, n, :], K.col(name, rows=H), None, ALU.add))
                step.all()
                nc.vector.scalar_tensor_tensor(e[:, 0, :], t[:, 0, :], -1.0, t[:, 0, :], ALU.mult, ALU.max).then_inc(abs_ready, 1)
                nc.vector.scalar_tensor_tensor(e[:, 1, :], t[:, 2, :], -1.0, t[:, 2, :], ALU.mult, ALU.max).then_inc(abs_ready, 1)
                dve.wait_ge(log_ready, 1)
                step.go(nc.vector.scalar_tensor_tensor(rows[:, 1, :], t[:, 0, :], 0.0, e[:, 0, :], ALU.max, ALU.add))
                step(nc.vector.scalar_tensor_tensor(t[:, 2, :], t[:, 2, :], 0.0, e[:, 1, :], ALU.min, ALU.subtract))
                dve.wait_ge(a_ready, 1)
                step.go(nc.vector.tensor_scalar(t[:, 0, :], rows[:, 1, :], a[:, :], -1.0, ALU.mult, ALU.mult))
                step(nc.vector.tensor_tensor_scan(t[:, 3, :], one[:, :], t[:, 2, :], 0.0, ALU.mult, ALU.add))
                step.go(nc.vector.tensor_tensor_scan(rows[:, 0, :], one[:, :], t[:, 0, :], 0.0, ALU.mult, ALU.add))
                step(nc.vector.tensor_tensor(rows[:, 2, :], t[:, 1, :], t[:, 3, :], ALU.subtract))
                step(nc.vector.tensor_tensor_scan(rows[:, 3, :], one[:, :], rows[:, 2, :], 0.0, ALU.mult, ALU.max))
                nc.vector.tensor_tensor(t[:, 3, :], t[:, 3, :], rows[:, 3, :], ALU.add).then_inc(rows_ready, 1)
                dve.wait_ge(rows_ready, 1)
                nc.vector.tensor_scalar(t[:, 3, :], t[:, 3, :], -1.0, 87.0, ALU.mult, ALU.min).then_inc(em_in, 1)
                dve.wait_ge(cols_turned, 1)
                step.go(nc.vector.tensor_scalar(cols[:, 0, :, :], turned[:, 0, :, :], -1.0, None, ALU.mult))
                step.go(nc.vector.tensor_copy(cols[:, 1:3, :, :], turned[:, 1:3, :, :]))
                step.all()
                dve.wait_ge(em_out, 1)


def decayed_attention(K, key, query, row, pick, col, value, scale, out, den=None):
    nc = K.nc
    steps = [(h, j) for h in range(H) for j in range(NT)]
    with ExitStack() as ctx:
        dec = K.sb(ctx, "dec", [P, 2, S])
        att = K.sb(ctx, "att", [P, 2, S])
        st = K.ps(ctx, "st", [P, 2, S])
        rb = K.ps(ctx, "rb", [P, 2, S])
        with stage(nc, "row_spread", "exponent", "decayed", "masked", "scored", "weighted", "summed") as (
                block, row_spread, exponent, decayed, masked, scored, weighted, summed):
            @block.tensor
            def _(pe):
                def sums(n):
                    h, j = steps[n]
                    pe.wait_ge(weighted, n + 1)
                    o = 64 * (h % 2)
                    mm = nc.tensor.matmul(out[o:o + 64, h // 2, j * P:S], value(h, j), att[:, n % 2, j * P:S],
                                          start=(j == 0), stop=(j == NT - 1))
                    if den is not None:
                        mm = nc.tensor.matmul(den[o:o + 64, h // 2, j * P:S], K.c("ones", P, 0, 64),
                                              att[:, n % 2, j * P:S], start=(j == 0), stop=(j == NT - 1))
                    mm.then_inc(summed, 1)

                for n, (h, j) in enumerate(steps):
                    if j == 0:
                        if h >= 2:
                            pe.wait_ge(exponent, NT * (h - 1))
                        nc.tensor.matmul(rb[:, h % 2, :], K.c(pick, H, h), row, start=True, stop=True).then_inc(row_spread, 1)
                    if n >= 2:
                        pe.wait_ge(weighted, n - 1)
                    nc.tensor.matmul(st[:, n % 2, j * P:S], key(h)[:, j * P:(j + 1) * P], query(h)[:, j * P:S],
                                     start=True, stop=True).then_inc(scored, 1)
                    if n:
                        sums(n - 1)
                sums(len(steps) - 1)

            @block.scalar
            def _(act):
                for n, (h, j) in enumerate(steps):
                    act.wait_ge(exponent, n + 1)
                    nc.scalar.activation(dec[:, n % 2, j * P:S], dec[:, n % 2, j * P:S], ACT.Exp).then_inc(decayed, 1)

            @block.vector
            def _(dve):
                def exponents(n):
                    h, j = steps[n]
                    dve.wait_ge(row_spread, h + 1)
                    if n >= 2:
                        dve.wait_ge(weighted, n - 1)
                    nc.vector.tensor_scalar(dec[:, n % 2, j * P:S], rb[:, h % 2, j * P:S], col(h, j), 0.0,
                                            ALU.add, ALU.min).then_inc(exponent, 1)

                exponents(0)
                for n, (h, j) in enumerate(steps):
                    if n + 1 < len(steps):
                        exponents(n + 1)
                    dve.wait_ge(decayed, n + 1)
                    nc.vector.tensor_tensor(dec[:, n % 2, j * P:(j + 1) * P], dec[:, n % 2, j * P:(j + 1) * P],
                                            K.c("causal"), ALU.mult).then_inc(masked, 1)
                    dve.wait_ge(masked, n + 1)
                    dve.wait_ge(scored, n + 1)
                    if n >= 2:
                        dve.wait_ge(summed, n - 1)
                    nc.vector.scalar_tensor_tensor(att[:, n % 2, j * P:S], st[:, n % 2, j * P:S], scale,
                                                   dec[:, n % 2, j * P:S], ALU.mult, ALU.mult).then_inc(weighted, 1)


def ssd(K, U, conv, rows, cols, y):
    nc = K.nc
    with ExitStack() as ctx:
        xt = K.sb(ctx, "xt", [P, NT, 256])
        gz = K.sb(ctx, "gz", [P, 2, S])
        out = K.ps(ctx, "ssd_out", [P, 2, S])
        with ExitStack() as c2:
            transposes(K, [(conv[:, t, :], xt[:, :, t * P:(t + 1) * P]) for t in range(2)])
        with stage(nc, "scaled", "gated") as (block, scaled, gated):
            @block.vector
            def _(dve):
                for j in range(NT):
                    v = xt[:, j, :].rearrange("p (h d) -> p h d", h=H)
                    nc.vector.tensor_tensor(v, v, cols[:, 1, j, :].unsqueeze(2).to_broadcast([P, H, 64]),
                                            ALU.mult).then_inc(scaled, 1)

            @block.scalar
            def _(act):
                nc.scalar.activation(gz[:, :, :], U[:, Z:Z + 2, :], ACT.Silu).then_inc(gated, 1)
        decayed_attention(K, lambda h: conv[:, 2, :], lambda h: conv[:, 3, :], rows[:, 0, :], "pick",
                          lambda h, j: cols[:, 0, j, h:h + 1], lambda h, j: xt[:, j, h * 64:h * 64 + 64], 1.0, out)
        with stage(nc, "own") as (block, own):
            @block.vector
            def _(dve):
                step = Own(dve, own)
                for t in range(2):
                    step.go(nc.vector.scalar_tensor_tensor(y[:, t, :], conv[:, t, :], K.col("ssd_d", t), out[:, t, :],
                                                           ALU.mult, ALU.add))
                step.all()
                step(nc.vector.tensor_tensor(y[:, :, :], y[:, :, :], gz[:, :, :], ALU.mult))
    normalise(K, [[y[:, 0, :], y[:, 1, :]]], [[y[:, 0, :], y[:, 1, :]]], K.c("mean256"), 1e-5, False,
              lambda t: K.col("ssd_norm_g", t))


def mlstm(K, U, conv, rows, cols, y):
    nc = K.nc
    with ExitStack() as ctx:
        vt = K.sb(ctx, "vt", [P, NT, 256])
        dn = K.sb(ctx, "dn", [P, 2, S])
        so = K.sb(ctx, "so", [P, 2, S])
        out = K.ps(ctx, "ml_out", [P, 2, S])
        transposes(K, [(U[:, MV + t, :], vt[:, :, t * P:(t + 1) * P]) for t in range(2)])
        with ExitStack() as c2:
            den = K.ps(c2, "ml_den", [P, 2, S])
            decayed_attention(K, lambda h: conv[64 * (h % 2):64 * (h % 2) + 64, 6 + h // 2, :],
                              lambda h: conv[64 * (h % 2):64 * (h % 2) + 64, 4 + h // 2, :],
                              rows[:, 3, :], "pickneg", lambda h, j: cols[:, 2, j, h:h + 1],
                              lambda h, j: vt[:, j, h * 64:h * 64 + 64], 0.125, out, den)
            em = K.ps(c2, "em", [P, 2, S])
            with stage(nc, "own", "em_spread", "gate_ready", "den_abs") as (
                    block, own, em_spread, gate_ready, den_abs):
                @block.tensor
                def _(pe):
                    for h in range(H):
                        o = 64 * (h % 2)
                        mm = nc.tensor.matmul(em[o:o + 64, h // 2, :], K.c("pick", H, h)[:, 0:64], rows[:, 4, :],
                                              start=True, stop=True)
                    mm.then_inc(em_spread, 1)

                @block.scalar
                def _(act):
                    nc.scalar.activation(dn[:, :, :], den[:, :, :], ACT.Abs).then_inc(den_abs, 1)
                    nc.scalar.activation(so[:, :, :], U[:, MOG:MOG + 2, :], ACT.Sigmoid).then_inc(gate_ready, 1)

                @block.vector
                def _(dve):
                    step = Own(dve, own)
                    dve.wait_ge(em_spread, 1)
                    dve.wait_ge(den_abs, 1)
                    step(nc.vector.tensor_tensor(dn[:, :, :], dn[:, :, :], em[:, :, :], ALU.max))
                    step(nc.vector.reciprocal(dn[:, :, :], dn[:, :, :]))
                    step(nc.vector.tensor_tensor(y[:, :, :], dn[:, :, :], out[:, :, :], ALU.mult))
                    dve.wait_ge(gate_ready, 1)
                    step(nc.vector.tensor_tensor(y[:, :, :], y[:, :, :], so[:, :, :], ALU.mult))
    normalise(K, [[y[:, 0, :]], [y[:, 1, :]]], [[y[:, 0, :]], [y[:, 1, :]]], K.c("mean64"), 1e-5, True,
              lambda t: K.col("mlstm_norm_g", t))


def gla(K, U, gate_up, y):
    nc = K.nc
    L = [slice(c * P, (c + 1) * P) for c in range(NT)]
    MID = P // 2 - 1
    with ExitStack() as ctx:
        b = K.sb(ctx, "b", [P, S])
        e = K.sb(ctx, "e", [P, 2, S])
        qd = K.sb(ctx, "qd", [P, S])
        ki = K.sb(ctx, "ki", [P, S])
        kt = K.sb(ctx, "kt", [P, NT, P])
        vt = K.sb(ctx, "vt", [P, NT, 256])
        one = K.sb(ctx, "one", [P, P])
        ends = K.sb(ctx, "ends", [P, NT, 3])
        og = K.sb(ctx, "og", [P, 2, S])
        state = K.sb(ctx, "state", [P, 256])
        started = K.sb(ctx, "started", [P, 256])
        att = K.sb(ctx, "att", [P, 2, P])
        transposes(K, [(U[:, GV + t, :], vt[:, :, t * P:(t + 1) * P]) for t in range(2)])
        with ExitStack() as c2:
            logit = K.ps(c2, "logit", [P, S])
            with stage(nc, "own", "a_own", "logit_ready", "gate_in", "gate_out", "diff_ready", "exp_ready", "og_ready") as (
                    block, own, a_own, logit_ready, gate_in, gate_out, diff_ready, exp_ready, og_ready):
                @block.tensor
                def _(pe):
                    nc.tensor.matmul(logit[:, :], gate_up[ROW_GD:ROW_GD + 16, :], U[ROW_GD:ROW_GD + 16, NARROW, :],
                                     start=True, stop=True).then_inc(logit_ready, 1)

                @block.scalar
                def _(act):
                    step = Own(act, a_own)
                    act.wait_ge(gate_in, 1)
                    step(nc.scalar.activation(e[:, 1, :], e[:, 1, :], ACT.Exp, scale=-1.0))
                    nc.scalar.activation(e[:, 1, :], e[:, 1, :], ACT.Ln, bias=1.0).then_inc(gate_out, 1)
                    act.wait_ge(diff_ready, 1)
                    step.go(nc.scalar.activation(e[:, :, :], e[:, :, :], ACT.Exp))
                    step(nc.scalar.activation(ends[:, :, :], ends[:, :, :], ACT.Exp))
                    nc.scalar.activation(og[:, :, :], U[:, GOG:GOG + 2, :], ACT.Silu).then_inc(og_ready, 1)

                @block.vector
                def _(dve):
                    step = Own(dve, own)
                    step.go(nc.vector.memset(one[:, :], 1.0))
                    dve.wait_ge(logit_ready, 1)
                    step(nc.vector.tensor_scalar(e[:, 0, :], logit[:, :], K.col("gla_gate_b"), None, ALU.add))
                    nc.vector.scalar_tensor_tensor(e[:, 1, :], e[:, 0, :], -1.0, e[:, 0, :], ALU.mult, ALU.max).then_inc(gate_in, 1)
                    dve.wait_ge(gate_out, 1)
                    step(nc.vector.scalar_tensor_tensor(e[:, 0, :], e[:, 0, :], 0.0, e[:, 1, :], ALU.min, ALU.subtract))
                    step(nc.vector.tensor_scalar(e[:, 0, :], e[:, 0, :], 1 / 16, None, ALU.mult))
                    for c in range(NT):
                        step.go(nc.vector.tensor_tensor_scan(b[:, L[c]], one[:, :], e[:, 0, L[c]], 0.0, ALU.mult, ALU.add))
                    step.all()
                    for c in range(NT):
                        mid, last = b[:, c * P + MID:c * P + MID + 1], b[:, (c + 1) * P - 1:(c + 1) * P]
                        step.go(nc.vector.tensor_copy(ends[:, c, 0:1], mid))
                        step.go(nc.vector.tensor_tensor(ends[:, c, 1:2], last, mid, ALU.subtract))
                        step.go(nc.vector.tensor_copy(ends[:, c, 2:3], last))
                        step.go(nc.vector.tensor_scalar(e[:, 0, L[c]], b[:, L[c]], mid, None, ALU.subtract))
                    step.all()
                    nc.vector.tensor_scalar(e[:, 1, :], e[:, 0, :], -1.0, None, ALU.mult).then_inc(diff_ready, 1)
                    dve.wait_ge(og_ready, 1)
                    step.go(nc.vector.scalar_tensor_tensor(qd[:, :], U[:, GQ, :], 32 ** -0.5, e[:, 0, :], ALU.mult, ALU.mult))
                    step(nc.vector.tensor_tensor(ki[:, :], U[:, GK, :], e[:, 1, :], ALU.mult))
        transposes(K, [(ki[:, :], kt[:, :, :])])
        with ExitStack() as c2:
            out = K.ps(c2, "gla_out", [P, 2, S])
            sc = K.ps(c2, "sc", [P, 2, 512])
            kv = K.ps(c2, "kv", [P, 2, 512])
            with stage(nc, "own", "scored", "weighted", "contrib", "state_ready", "chunk_done") as (
                    block, own, scored, weighted, contrib, state_ready, chunk_done):
                @block.tensor
                def _(pe):
                    for c in range(NT):
                        nc.tensor.matmul(kv[:, c % 2, 0:256], kt[:, c, :], vt[:, c, :], start=True, stop=True).then_inc(contrib, 1)
                        if c:
                            pe.wait_ge(state_ready, c)
                            for t in range(2):
                                nc.tensor.matmul(out[:, t, L[c]], started[:, t * P:(t + 1) * P], qd[:, L[c]],
                                                 start=True, stop=False, skip_group_check=True)
                        for h in range(H):
                            n = c * H + h
                            if n >= 2:
                                pe.wait_ge(weighted, n - 1)
                            r = slice(32 * h, 32 * h + 32)
                            nc.tensor.matmul(sc[:, n % 2, 0:P], ki[r, L[c]], qd[r, L[c]], start=True, stop=True).then_inc(scored, 1)
                            pe.wait_ge(weighted, n + 1)
                            o = 64 * (h % 2)
                            mm = nc.tensor.matmul(out[o:o + 64, h // 2, L[c]], vt[:, c, h * 64:h * 64 + 64], att[:, n % 2, :],
                                                  start=(c == 0), stop=True, skip_group_check=True)
                        mm.then_inc(chunk_done, 1)

                @block.vector
                def _(dve):
                    step = Own(dve, own)
                    step.go(nc.vector.memset(att[:, :, :], 0.0))
                    step(nc.vector.memset(state[:, :], 0.0))
                    for c in range(NT):
                        for h in range(H):
                            n = c * H + h
                            dve.wait_ge(scored, n + 1)
                            nc.vector.copy_predicated(att[:, n % 2, :], K.c("causal").bitcast(I32), sc[:, n % 2, 0:P]).then_inc(weighted, 1)
                        if c < NT - 1:
                            dve.wait_ge(contrib, c + 1)
                            step(nc.vector.tensor_scalar(state[:, :], state[:, :], ends[:, c, 2:3], None, ALU.mult))
                            step(nc.vector.scalar_tensor_tensor(state[:, :], kv[:, c % 2, 0:256], ends[:, c, 1:2], state[:, :], ALU.mult, ALU.add))
                            dve.wait_ge(chunk_done, c + 1)
                            nc.vector.scalar_tensor_tensor(started[:, :], state[:, :], ends[:, c + 1, 0:1],
                                                           K.c("glamask", P, 0, 256), ALU.mult, ALU.mult).then_inc(state_ready, 1)
                    dve.wait_ge(chunk_done, NT)
                    step(nc.vector.tensor_copy(y[:, :, :], out[:, :, :]))
        normalise(K, [[y[:, 0, :]], [y[:, 1, :]]], [[y[:, 0, :]], [y[:, 1, :]]], K.c("mean64"), 1e-5, False,
                  lambda t: K.col("gla_norm_g", t), gate=lambda t: og[:, t, :])


def rwkv(K, U, lora, y):
    nc = K.nc
    L = [slice(c * P, (c + 1) * P) for c in range(NT)]
    MID = P // 2 - 1
    with ExitStack() as ctx:
        at = K.sb(ctx, "at", [P, 2, S])
        bt = K.sb(ctx, "bt", [P, 2, S])
        kt = K.sb(ctx, "kt", [P, 2, S])
        rt = K.sb(ctx, "rt", [P, 2, S])
        g = K.sb(ctx, "g", [P, 2, S])
        bonus = K.sb(ctx, "bonus", [P, 2, S])
        ends = K.sb(ctx, "ends", [P, 2, NT, 3])
        vt = K.sb(ctx, "vt", [P, NT, 256])
        btt = K.sb(ctx, "btt", [P, NT, 256])
        ktt = K.sb(ctx, "ktt", [P, NT, 256])
        cm = ExitStack()
        m = K.sb(cm, "m", [P, 7, S])
        with ExitStack() as c2:
            w = K.sb(c2, "w", [P, 2, S])
            a = K.sb(c2, "a", [P, 2, S])
            kk = K.sb(c2, "kk", [P, 2, S])
            t1 = K.sb(c2, "t1", [P, 2, S])
            b = K.sb(c2, "b", [P, 2, S])
            diff = K.sb(c2, "diff", [P, 7, S])
            one = K.sb(c2, "one", [P, P])
            th = K.sb(c2, "th", [P, S])
            wl = K.ps(c2, "wl", [P, 2, S])
            al = K.ps(c2, "al", [P, 2, S])
            gl = K.ps(c2, "gl", [P, 2, S])
            s1 = K.ps(c2, "s1", [P, 2, S])
            with stage(nc, "own", "a_own", "mixed", "lora_in", "lora_out", "gates", "kk_sq", "kk_sum", "kk_root", "diffs",
                       "exps", "rk", "rk_sum") as (
                    block, own, a_own, mixed, lora_in, lora_out, gates, kk_sq, kk_sum, kk_root, diffs, exps, rk, rk_sum):
                @block.tensor
                def _(pe):
                    pe.wait_ge(lora_in, 1)
                    for t in range(2):
                        c = slice(t * P, (t + 1) * P)
                        nc.tensor.matmul(wl[:, t, :], lora[0:32, c], th[0:32, :], start=True, stop=True)
                        nc.tensor.matmul(al[:, t, :], lora[32:64, c], th[32:64, :], start=True, stop=True)
                        mm = nc.tensor.matmul(gl[:, t, :], lora[64:128, c], th[64:128, :], start=True, stop=True)
                    mm.then_inc(lora_out, 1)
                    pe.wait_ge(kk_sq, 1)
                    for t in range(2):
                        mm = nc.tensor.matmul(s1[:, t, :], K.c("sum64"), t1[:, t, :], start=True, stop=True)
                    mm.then_inc(kk_sum, 1)
                    pe.wait_ge(rk, 1)
                    for t in range(2):
                        mm = nc.tensor.matmul(s1[:, t, :], K.c("sum64"), t1[:, t, :], start=True, stop=True)
                    mm.then_inc(rk_sum, 1)

                @block.scalar
                def _(act):
                    step = Own(act, a_own)
                    act.wait_ge(mixed, 7)
                    step.go(nc.scalar.activation(th[0:32, :], m[0:32, 6, :], ACT.Tanh))
                    step.go(nc.scalar.activation(th[32:64, :], m[32:64, 6, :], ACT.Copy))
                    step.go(nc.scalar.activation(th[64:128, :], m[64:128, 6, :], ACT.Sigmoid))
                    step.all()
                    nc.scalar.activation(ends[:, 0, 0, :], K.c("ones")[:, 0:3], ACT.Copy).then_inc(lora_in, 1)
                    act.wait_ge(lora_out, 1)
                    for t in range(2):
                        step.go(nc.scalar.activation(w[:, t, :], wl[:, t, :], ACT.Sigmoid, bias=K.col("rwkv_w0", t)))
                        step.go(nc.scalar.activation(a[:, t, :], al[:, t, :], ACT.Sigmoid, bias=K.col("rwkv_a0", t)))
                    step.all()
                    nc.scalar.activation(g[:, :, :], gl[:, :, :], ACT.Copy).then_inc(gates, 1)
                    act.wait_ge(kk_sum, 1)
                    nc.scalar.activation(diff[:, 0:2, :], s1[:, :, :], ACT.Sqrt).then_inc(kk_root, 1)
                    act.wait_ge(diffs, 1)
                    step.go(nc.scalar.activation(diff[:, 0:6, :], diff[:, 0:6, :], ACT.Exp))
                    step.all()
                    nc.scalar.activation(ends[:, :, :, :], ends[:, :, :, :], ACT.Exp).then_inc(exps, 1)

                @block.vector
                def _(dve):
                    step = Own(dve, own)
                    step.go(nc.vector.memset(one[:, :], 1.0))
                    u = U[:, R_:R_ + 7, :]
                    step.go(nc.vector.tensor_tensor(diff[:, :, 1:S], u[:, :, 0:S - 1], u[:, :, 1:S], ALU.subtract))
                    step(nc.vector.tensor_scalar(diff[:, :, 0:1], u[:, :, 0:1], -1.0, None, ALU.mult))
                    for t in range(7):
                        nc.vector.scalar_tensor_tensor(m[:, t, :], diff[:, t, :], K.col("rwkv_mu", t), U[:, R_ + t, :],
                                                       ALU.mult, ALU.add).then_inc(mixed, 1)
                    dve.wait_ge(mixed, 7)
                    for t in range(2):
                        step.go(nc.vector.tensor_scalar(kk[:, t, :], m[:, 2 + t, :], K.col("rwkv_k_k", t), None, ALU.mult))
                    step.all()
                    nc.vector.tensor_tensor(t1[:, :, :], kk[:, :, :], kk[:, :, :], ALU.mult).then_inc(kk_sq, 1)
                    dve.wait_ge(kk_root, 1)
                    step(nc.vector.tensor_scalar(diff[:, 0:2, :], diff[:, 0:2, :], 1e-12, None, ALU.max))
                    step(nc.vector.reciprocal(diff[:, 0:2, :], diff[:, 0:2, :]))
                    step(nc.vector.tensor_tensor(kk[:, :, :], kk[:, :, :], diff[:, 0:2, :], ALU.mult))
                    dve.wait_ge(gates, 1)
                    for t in range(2):
                        step.go(nc.vector.tensor_scalar(t1[:, t, :], a[:, t, :], -1.0, K.col("rwkv_k_a", t), ALU.add, ALU.mult))
                    step.go(nc.vector.tensor_scalar(w[:, :, :], w[:, :, :], -float(np.exp(-0.5)), None, ALU.mult))
                    step.all()
                    step.go(nc.vector.scalar_tensor_tensor(m[:, 2:4, :], t1[:, :, :], 1.0, m[:, 2:4, :], ALU.add, ALU.mult))
                    for t in range(2):
                        for c in range(NT):
                            step.go(nc.vector.tensor_tensor_scan(b[:, t, L[c]], one[:, :], w[:, t, L[c]], 0.0, ALU.mult, ALU.add))
                    step.all()
                    for t in range(2):
                        for c in range(NT):
                            mid, last = b[:, t, c * P + MID:c * P + MID + 1], b[:, t, (c + 1) * P - 1:(c + 1) * P]
                            step.go(nc.vector.tensor_copy(ends[:, t, c, 0:1], mid))
                            step.go(nc.vector.tensor_tensor(ends[:, t, c, 1:2], last, mid, ALU.subtract))
                            step.go(nc.vector.tensor_copy(ends[:, t, c, 2:3], last))
                            step.go(nc.vector.tensor_scalar(diff[:, t, L[c]], b[:, t, L[c]], mid, None, ALU.subtract))
                    step.all()
                    step.go(nc.vector.tensor_scalar(diff[:, 2:4, :], diff[:, 0:2, :], -1.0, None, ALU.mult))
                    nc.vector.tensor_tensor(diff[:, 4:6, :], diff[:, 0:2, :], w[:, :, :], ALU.subtract).then_inc(diffs, 1)
                    step.all()
                    for t in range(2):
                        step.go(nc.vector.scalar_tensor_tensor(t1[:, t, :], m[:, t, :], K.col("rwkv_r_k", t), m[:, 2 + t, :],
                                                               ALU.mult, ALU.mult))
                    dve.wait_ge(exps, 1)
                    step.go(nc.vector.tensor_tensor(rt[:, :, :], m[:, 0:2, :], diff[:, 0:2, :], ALU.mult))
                    step.go(nc.vector.tensor_tensor(kt[:, :, :], m[:, 2:4, :], diff[:, 2:4, :], ALU.mult))
                    step.go(nc.vector.scalar_tensor_tensor(at[:, :, :], kk[:, :, :], -1.0, diff[:, 4:6, :], ALU.mult, ALU.mult))
                    step(nc.vector.tensor_tensor(bt[:, :, :], kk[:, :, :], a[:, :, :], ALU.mult))
                    nc.vector.tensor_tensor(bt[:, :, :], bt[:, :, :], diff[:, 2:4, :], ALU.mult).then_inc(rk, 1)
                    dve.wait_ge(rk_sum, 1)
                    step(nc.vector.tensor_tensor(bonus[:, :, :], m[:, 4:6, :], s1[:, :, :], ALU.mult))
                    dve.wait_ge(rk, 1)
        transposes(K, [(m[:, 4 + t, :], vt[:, :, t * P:(t + 1) * P]) for t in range(2)]
                   + [(bt[:, t, :], btt[:, :, t * P:(t + 1) * P]) for t in range(2)]
                   + [(kt[:, t, :], ktt[:, :, t * P:(t + 1) * P]) for t in range(2)])
        cm.close()
        with ExitStack() as c2:
            nt = K.sb(c2, "nt", [P, NT, H, P])
            mak = K.sb(c2, "mak", [P, NT, H, P])
            mrb = K.sb(c2, "mrb", [P, NT, H, P])
            mrk = K.sb(c2, "mrk", [P, NT, H, P])
            x = K.sb(c2, "x", [P, NT, H, P])
            xt = K.sb(c2, "xt", [P, NT, H, P])

            def spread(mask):
                return mask.unsqueeze(1).to_broadcast([P, H, P])

            with ExitStack() as c3:
                pr = K.ps(c3, "pr", [P, 4, 2, S])
                with stage(nc, "product", "masked") as (block, product, masked):
                    pairs = [(bt, at, nt, "strict"), (kt, at, mak, "strict"), (bt, rt, mrb, "causal"), (kt, rt, mrk, "causal")]

                    @block.tensor
                    def _(pe):
                        for c in range(NT):
                            for q, (left, right, dst, mask) in enumerate(pairs):
                                n = 4 * c + q
                                if n >= 4:
                                    pe.wait_ge(masked, n - 3)
                                for h in range(H):
                                    r = slice(64 * (h % 2), 64 * (h % 2) + 64)
                                    mm = nc.tensor.matmul(pr[:, n % 4, h % 2, h // 2 * P:(h // 2 + 1) * P], left[r, h // 2, L[c]], right[r, h // 2, L[c]],
                                                          start=True, stop=True)
                                mm.then_inc(product, 1)

                    @block.vector
                    def _(dve):
                        for c in range(NT):
                            for q, (left, right, dst, mask) in enumerate(pairs):
                                n = 4 * c + q
                                dve.wait_ge(product, n + 1)
                                for odd in (0, 1):
                                    last = nc.vector.tensor_tensor(
                                        dst[:, c, 2 * odd:2 * odd + 2, :],
                                        pr[:, n % 4, odd, 0:2 * P].rearrange("p (h t) -> p h t", h=2),
                                        K.c(mask).unsqueeze(1).to_broadcast([P, 2, P]), ALU.mult)
                                last.then_inc(masked, 1)
            with ExitStack() as c3:
                nm = K.sb(c3, "nm", [P, 2, H, P])
                yb = K.sb(c3, "yb", [P, 2, H, P])
                py = K.ps(c3, "py", [P, 2, H, P])
                pz = K.ps(c3, "pz", [P, 2, H, P])
                pzt = K.ps(c3, "pzt", [P, 2, H, P])
                rounds = [(lv, c) for lv in range(len(HALVES)) for c in range(NT)]
                with stage(nc, "own", "level_ready", "y_ready", "y_taken", "z_ready", "x_ready") as (
                        block, own, level_ready, y_ready, y_taken, z_ready, x_ready):
                    @block.tensor
                    def _(pe):
                        def first(n):
                            lv, c = rounds[n]
                            pe.wait_ge(level_ready, n + 1)
                            if lv:
                                pe.wait_ge(x_ready, n - NT + 1)
                            if n >= 2:
                                pe.wait_ge(y_taken, n - 1)
                            for h in range(H):
                                mm = nc.tensor.matmul(py[:, n % 2, h, :], nm[:, n % 2, h, :], x[:, c, h, :], start=True, stop=True)
                            mm.then_inc(y_ready, 1)

                        first(0)
                        for n, (lv, c) in enumerate(rounds):
                            if n + 1 < len(rounds):
                                first(n + 1)
                            pe.wait_ge(y_taken, n + 1)
                            if n >= 2:
                                pe.wait_ge(x_ready, n - 1)
                            for h in range(H):
                                nc.tensor.matmul(pz[:, n % 2, h, :], xt[:, c, h, :], yb[:, n % 2, h, :], start=True, stop=True)
                                mm = nc.tensor.matmul(pzt[:, n % 2, h, :], yb[:, n % 2, h, :], xt[:, c, h, :], start=True, stop=True)
                            mm.then_inc(z_ready, 1)

                    @block.scalar
                    def _(act):
                        for n in range(len(rounds)):
                            act.wait_ge(y_ready, n + 1)
                            if n >= 2:
                                act.wait_ge(z_ready, n - 1)
                            nc.scalar.activation(yb[:, n % 2, :, :], py[:, n % 2, :, :], ACT.Copy).then_inc(y_taken, 1)

                    @block.vector
                    def _(dve):
                        step = Own(dve, own)
                        for c in range(NT):
                            step.go(nc.vector.tensor_copy(x[:, c, :, :], spread(K.c("ident"))))
                            step.go(nc.vector.tensor_copy(xt[:, c, :, :], spread(K.c("ident"))))
                        step.all()

                        def level(n):
                            lv, c = rounds[n]
                            if n >= 2:
                                dve.wait_ge(y_ready, n - 1)
                            nc.vector.tensor_tensor(nm[:, n % 2, :, :], nt[:, c, :, :], spread(K.c("fwd", P, lv)),
                                                    ALU.mult).then_inc(level_ready, 1)

                        level(0)
                        for n, (lv, c) in enumerate(rounds):
                            if n + 1 < len(rounds):
                                level(n + 1)
                            dve.wait_ge(z_ready, n + 1)
                            step.go(nc.vector.tensor_tensor(x[:, c, :, :], x[:, c, :, :], pz[:, n % 2, :, :], ALU.add))
                            step.all()
                            nc.vector.tensor_tensor(xt[:, c, :, :], xt[:, c, :, :], pzt[:, n % 2, :, :], ALU.add).then_inc(x_ready, 1)
            with ExitStack() as c3:
                state = K.sb(c3, "state", [P, 2, 64])
                started = K.sb(c3, "started", [P, 2, 64])
                rhs = K.sb(c3, "rhs", [P, 256])
                sa = K.sb(c3, "sa", [P, 256])
                prhs = K.ps(c3, "prhs", [P, 2, 512])
                psa = K.ps(c3, "psa", [P, 512])
                pst = K.ps(c3, "pst", [P, 2, 64])
                out = K.ps(c3, "rw_out", [P, 2, S])
                with stage(nc, "own", "rhs_ready", "rhs_taken", "sa_ready", "sa_taken", "contrib", "started_ready", "chunk_done") as (
                        block, own, rhs_ready, rhs_taken, sa_ready, sa_taken, contrib, started_ready, chunk_done):
                    @block.tensor
                    def _(pe):
                        for c in range(NT):
                            pe.wait_ge(started_ready, c + 1)
                            for h in range(H):
                                r, v = slice(64 * (h % 2), 64 * (h % 2) + 64), slice(64 * h, 64 * h + 64)
                                o = prhs[:, h % 2, 64 * (h // 2):64 * (h // 2) + 64]
                                nc.tensor.matmul(o, at[r, h // 2, L[c]], started[r, h // 2, :], start=True, stop=False)
                                mm = nc.tensor.matmul(o, mak[:, c, SLOT[h], :], vt[:, c, v], start=False, stop=True)
                            mm.then_inc(rhs_ready, 1)
                            pe.wait_ge(rhs_taken, c + 1)
                            for h in range(H):
                                v = slice(64 * SLOT[h], 64 * SLOT[h] + 64)
                                mm = nc.tensor.matmul(psa[:, v], xt[:, c, SLOT[h], :], rhs[:, v], start=True, stop=True)
                            mm.then_inc(sa_ready, 1)
                            pe.wait_ge(sa_taken, c + 1)
                            for h in range(H):
                                r, v = slice(64 * (h % 2), 64 * (h % 2) + 64), slice(64 * h, 64 * h + 64)
                                nc.tensor.matmul(pst[r, h // 2, :], btt[:, c, v], sa[:, 64 * SLOT[h]:64 * SLOT[h] + 64], start=True, stop=False)
                                mm = nc.tensor.matmul(pst[r, h // 2, :], ktt[:, c, v], vt[:, c, v], start=False, stop=True)
                            mm.then_inc(contrib, 1)
                            for h in range(H):
                                r, v = slice(64 * (h % 2), 64 * (h % 2) + 64), slice(64 * h, 64 * h + 64)
                                o = out[r, h // 2, L[c]]
                                nc.tensor.matmul(o, started[r, h // 2, :], rt[r, h // 2, L[c]], start=True, stop=False)
                                nc.tensor.matmul(o, sa[:, 64 * SLOT[h]:64 * SLOT[h] + 64], mrb[:, c, SLOT[h], :], start=False, stop=False)
                                mm = nc.tensor.matmul(o, vt[:, c, v], mrk[:, c, SLOT[h], :], start=False, stop=True)
                            mm.then_inc(chunk_done, 1)

                    @block.scalar
                    def _(act):
                        for c in range(NT):
                            act.wait_ge(rhs_ready, c + 1)
                            nc.scalar.activation(rhs[:, :].rearrange("p (a b) -> p a b", a=2), prhs[:, :, 0:128], ACT.Copy).then_inc(rhs_taken, 1)
                            act.wait_ge(sa_ready, c + 1)
                            if c:
                                act.wait_ge(chunk_done, c)
                            nc.scalar.activation(sa[:, :], psa[:, 0:256], ACT.Copy).then_inc(sa_taken, 1)

                    @block.vector
                    def _(dve):
                        step = Own(dve, own)
                        step.go(nc.vector.memset(state[:, :, :], 0.0))
                        nc.vector.memset(started[:, :, :], 0.0).then_inc(started_ready, 1)
                        step.all()
                        for c in range(NT - 1):
                            for t in range(2):
                                step.go(nc.vector.tensor_scalar(state[:, t, :], state[:, t, :], ends[:, t, c, 2:3], None, ALU.mult))
                            step.all()
                            dve.wait_ge(contrib, c + 1)
                            for t in range(2):
                                step.go(nc.vector.scalar_tensor_tensor(state[:, t, :], pst[:, t, :], ends[:, t, c, 1:2], state[:, t, :],
                                                                       ALU.mult, ALU.add))
                            step.all()
                            dve.wait_ge(chunk_done, c + 1)
                            step(nc.vector.tensor_scalar(started[:, 0, :], state[:, 0, :], ends[:, 0, c + 1, 0:1], None, ALU.mult))
                            nc.vector.tensor_scalar(started[:, 1, :], state[:, 1, :], ends[:, 1, c + 1, 0:1], None,
                                                    ALU.mult).then_inc(started_ready, 1)
                        dve.wait_ge(chunk_done, NT)
                        step(nc.vector.tensor_copy(y[:, :, :], out[:, :, :]))
        normalise(K, [[y[:, 0, :]], [y[:, 1, :]]], [[y[:, 0, :]], [y[:, 1, :]]], K.c("mean64"), 64e-5, True,
                  lambda t: K.col("rwkv_ln_g", t), bias=lambda t: K.col("rwkv_ln_b", t))
        with stage(nc, "own") as (block, own):
            @block.vector
            def _(dve):
                step = Own(dve, own)
                step(nc.vector.tensor_tensor(y[:, :, :], y[:, :, :], bonus[:, :, :], ALU.add))
                step(nc.vector.tensor_tensor(y[:, :, :], y[:, :, :], g[:, :, :], ALU.mult))


def router(K, x, w, b, gates):
    nc = K.nc
    with ExitStack() as ctx:
        lg = K.sb(ctx, "lg", [P, NT, EXPERTS])
        top = K.sb(ctx, "top", [P, NT, 8])
        at = K.sb(ctx, "at", [P, NT, 8], mybir.dt.uint32)
        atf = K.sb(ctx, "atf", [P, NT, 8])
        ex = K.sb(ctx, "ex", [P, NT, 4])
        total = K.sb(ctx, "total", [P, NT, 1])
        one = K.sb(ctx, "onehot", [P, NT, TOP_K, EXPERTS])
        ps = K.ps(ctx, "lg", [P, NT, EXPERTS])
        with stage(nc, "own", "a_own", "logits", "shifted", "exps") as (block, own, a_own, logits, shifted, exps):
            @block.tensor
            def _(pe):
                for j in range(NT):
                    for k in range(DT):
                        nc.tensor.matmul(ps[:, j, :], x[:, k, j * P:(j + 1) * P], w[:, k, :], start=(k == 0), stop=False)
                    mm = nc.tensor.matmul(ps[:, j, :], K.c("ones", 1), b[0:1, :], start=False, stop=True)
                mm.then_inc(logits, 1)

            @block.scalar
            def _(act):
                act.wait_ge(shifted, 1)
                nc.scalar.activation(ex[:, :, :], ex[:, :, :], ACT.Exp).then_inc(exps, 1)

            @block.vector
            def _(dve):
                step = Own(dve, own)
                dve.wait_ge(logits, 1)
                step(nc.vector.tensor_copy(lg[:, :, :], ps[:, :, :]))
                for j in range(NT):
                    step.go(nc.vector.max(top[:, j, :], lg[:, j, :]))
                step.all()
                for j in range(NT):
                    step.go(nc.vector.max_index(at[:, j, :], top[:, j, :], lg[:, j, :]))
                for j in range(NT):
                    ins = nc.vector.tensor_scalar(ex[:, j, :], top[:, j, 0:TOP_K], top[:, j, 0:1], None, ALU.subtract)
                    step.go(ins) if j < NT - 1 else ins.then_inc(shifted, 1)
                step.all()
                step(nc.vector.tensor_copy(atf[:, :, :], at[:, :, :]))
                dve.wait_ge(exps, 1)
                step(nc.vector.tensor_reduce(total[:, :, :], ex[:, :, :], AX.X, ALU.add))
                step(nc.vector.reciprocal(total[:, :, :], total[:, :, :]))
                step(nc.vector.tensor_tensor(ex[:, :, :], ex[:, :, :], total[:, :, :].to_broadcast([P, NT, TOP_K]), ALU.mult))
                for j in range(NT):
                    for k in range(TOP_K):
                        step.go(nc.vector.tensor_scalar(one[:, j, k, :], K.c("iota", P, 0, EXPERTS), atf[:, j, k:k + 1],
                                                        ex[:, j, k:k + 1], ALU.is_equal, ALU.mult))
                step.all()
                step.go(nc.vector.tensor_tensor(one[:, :, 0:2, :], one[:, :, 0:2, :], one[:, :, 2:4, :], ALU.add))
                step.all()
                step(nc.vector.tensor_tensor(gates[:, :, :], one[:, :, 0, :], one[:, :, 1, :], ALU.add))


CHUNKS = 12
CW = 2048
SLOTS = P
AHEAD = 2
RETURN = 2
RAW = 4
PARTS = 3


def dispatch(K, x, gates, b_down, pos, gpart, xh, xl, over, spill, keep):
    nc = K.nc
    with ExitStack() as ctx:
        routed = K.sb(ctx, "routed", [P, NT, EXPERTS])
        late = K.sb(ctx, "late", [P, NT, EXPERTS])
        few = K.sb(ctx, "few", [EXPERTS, 2])
        with ExitStack() as c2:
            place = K.ps(c2, "place", [P, NT, EXPERTS])
            count = K.ps(c2, "count", [EXPERTS, 2])
            number = K.ps(c2, "number", [1, 2])
            with stage(nc, "own", "mask_ready", "placed", "over_ready", "number_ready", "g_high") as (
                    block, own, mask_ready, placed, over_ready, number_ready, g_high):
                @block.tensor
                def _(pe):
                    pe.wait_ge(mask_ready, 1)
                    for j in range(NT):
                        for i in range(j):
                            nc.tensor.matmul(place[:, j, :], K.c("ones"), routed[:, i, :], start=(i == 0), stop=False)
                        nc.tensor.matmul(place[:, j, :], K.c("strict"), routed[:, j, :], start=(j == 0), stop=True)
                    for j in range(NT):
                        mm = nc.tensor.matmul(count[:, 0:2], routed[:, j, :], K.c("ones", P, 0, 2), start=(j == 0), stop=(j == NT - 1))
                    mm.then_inc(placed, 1)
                    pe.wait_ge(over_ready, 1)
                    nc.tensor.matmul(number[:, :], few[:, 0:1], K.c("ones", EXPERTS, 0, 2), start=True, stop=True).then_inc(number_ready, 1)

                @block.scalar
                def _(act):
                    nc.scalar.activation(gpart[:, :, :, 0], gates[:, :, :], ACT.Copy).then_inc(g_high, 1)

                @block.vector
                def _(dve):
                    step = Own(dve, own)
                    nc.vector.tensor_scalar(routed[:, :, :], gates[:, :, :], 0.0, None, ALU.is_gt).then_inc(mask_ready, 1)
                    dve.wait_ge(mask_ready, 1)
                    dve.wait_ge(placed, 1)
                    nc.vector.tensor_scalar(few[:, :], count[:, :], float(SLOTS), None, ALU.is_gt).then_inc(over_ready, 1)
                    step(nc.vector.tensor_scalar(late[:, :, :], place[:, :, :], float(SLOTS), None, ALU.is_ge))
                    step.go(nc.vector.tensor_tensor(late[:, :, :], late[:, :, :], gates[:, :, :], ALU.mult))
                    step(nc.vector.scalar_tensor_tensor(pos[:, :, :], place[:, :, :], 1.0, routed[:, :, :], ALU.add, ALU.mult))
                    step(nc.vector.tensor_scalar(pos[:, :, :], pos[:, :, :], 1.0, None, ALU.subtract))
                    dve.wait_ge(number_ready, 1)
                    step(nc.vector.tensor_copy(over[:, :], number[:, :]))
                    dve.wait_ge(g_high, 1)
                    step(nc.vector.tensor_tensor(gpart[:, :, :, 1], gates[:, :, :], gpart[:, :, :, 0], ALU.subtract))
        rows = K.sb(ctx, "rows", [EXPERTS, 3, S])
        with ExitStack() as c2:
            bank = K.ps(c2, "bank", [EXPERTS, 3, S])
            with stage(nc, "turned", "taken", "stored") as (block, turned, taken, stored):
                @block.tensor
                def _(pe):
                    for q, src in enumerate((gates, pos, late)):
                        for j in range(NT):
                            mm = nc.tensor.transpose(bank[:, q, j * P:(j + 1) * P], src[:, j, :], K.c("ident"))
                    mm.then_inc(turned, 1)

                @block.vector
                def _(dve):
                    dve.wait_ge(turned, 1)
                    nc.vector.tensor_copy(rows[:, :, :], bank[:, :, :]).then_inc(taken, 1)

                @block.sync
                def _(sp):
                    sp.wait_ge(taken, 1)
                    sp.dma_start(spill.rearrange("q e s -> e q s"), rows[:, 1:3, :]).then_inc(stored, 16)
                    sp.dma_start(keep, x[:, :, :]).then_inc(stored, 16)
                    sp.wait_ge(stored, 32)
        xt = K.sb(ctx, "x_tokens", [P, NT, D])
        transposes(K, [(x[:, k, :], xt[:, :, k * P:(k + 1) * P]) for k in range(DT)])
        split(K, xt, xh, xl)
        with ExitStack() as c2:
            ps = K.ps(c2, "bias", [P, DT, S])
            with stage(nc, "product", "taken") as (block, product, taken):
                @block.tensor
                def _(pe):
                    for i in range(DT):
                        nc.tensor.matmul(ps[:, i, :], b_down[:, i * P:(i + 1) * P], rows[:, 0, :], start=True, stop=True).then_inc(product, 1)

                @block.vector
                def _(dve):
                    for i in range(DT):
                        dve.wait_ge(product, i + 1)
                        nc.vector.scalar_tensor_tensor(x[:, i, :], x[:, i, :], ALPHA1, ps[:, i, :], ALU.mult, ALU.add).then_inc(taken, 1)


def split_biases(K, b_gu, parts):
    nc = K.nc
    with ExitStack() as ctx:
        b = K.sb(ctx, "b", [EXPERTS, 1, 2 * FE])
        bh = K.sb(ctx, "bh", [EXPERTS, 1, 2 * FE], F32R)
        bl = K.sb(ctx, "bl", [EXPERTS, 1, 2 * FE], F32R)
        load(K, [(b[:, 0, :], b_gu)])
        split(K, b, bh, bl)
        with stage(nc, "stored") as (block, stored):
            @block.sync
            def _(sp):
                sp.dma_start(parts[:, 0, :], bh[:, 0, :].bitcast(F32)).then_inc(stored, 16)
                sp.dma_start(parts[:, 1, :], bl[:, 0, :].bitcast(F32)).then_inc(stored, 16)
                sp.wait_ge(stored, 32)


def experts(K, pos, gpart, xh, xl, w, bias, pos_rows, out):
    nc = K.nc
    with ExitStack() as ctx:
        raw = K.sb(ctx, "raw", [P, RAW, CW])
        wh = K.sb(ctx, "wh", [P, PARTS, CW], F32R)
        wl = K.sb(ctx, "wl", [P, PARTS, CW], F32R)
        Xh = K.sb(ctx, "Xh", [P, DT, SLOTS], F32R)
        Xl = K.sb(ctx, "Xl", [P, DT, SLOTS], F32R)
        sel = K.sb(ctx, "sel", [P, NT, SLOTS], F32R)
        selt = K.sb(ctx, "selt", [P, S], F32R)
        prow = K.sb(ctx, "prow", [P, S])
        brow = K.sb(ctx, "brow", [2, 2 * FE], F32R)
        ones = K.sb(ctx, "ones2", [2, P], F32R)
        rl = K.sb(ctx, "rl", [P, 256])
        sg = K.sb(ctx, "sg", [P, 256])
        vc = K.sb(ctx, "vc", [P, 256])
        hb = K.sb(ctx, "hb", [P, 2, 256])
        top = K.sb(ctx, "top7", [P, 2])
        hh = K.sb(ctx, "hh", [P, FE // P, SLOTS], F32R)
        hl = K.sb(ctx, "hl", [P, FE // P, SLOTS], F32R)
        yh = K.sb(ctx, "yh", [P, D], F32R)
        yl = K.sb(ctx, "yl", [P, D], F32R)
        gneg = K.sb(ctx, "gneg", [P, 1])
        pu = K.ps(ctx, "pu", [P, 2, 512])
        pr = K.ps(ctx, "pr", [P, 2, 512])
        px = K.ps(ctx, "px", [P, 512])
        pt = K.ps(ctx, "pt", [P, 256])
        pd = K.ps(ctx, "pd", [P, 2, 512])
        with stage(nc, *[f"loaded{r}" for r in range(RAW)], "small_in", "w_high", "w_low", "used", "relu", "sigmoid",
                   "h_ready", "own", "turned", "t_high", "t_low", "y_high", "y_ready", "sel_ready", "selt_ready",
                   "g_filled", "g_copied", "s_filled", "s_added", "gate_in", "gate_ready", "ones_ready") as (block, *sems):
            loaded = sems[:RAW]
            (small_in, w_high, w_low, used, relu, sigmoid, h_ready, own, turned, t_high, t_low, y_high, y_ready, sel_ready,
             selt_ready, g_filled, g_copied, s_filled, s_added, gate_in, gate_ready, ones_ready) = sems[RAW:]

            def halves(m):
                return (m % 2, m // 2) if m < 8 else ((m - 8) // 2, m % 2)

            @block.sync
            def _(sp):
                def expert(e, first):
                    for m in range(CHUNKS):
                        if not (first and m < RAW):
                            sp.wait_ge(w_low, e * CHUNKS + (m - RAW + 1))
                        sp.dma_start(raw[:, m % RAW, :], w[bass.ds(e, 1), m, :, :].rearrange("a p n -> (a p) n")).then_inc(loaded[m % RAW], 16)

                expert(0, True)
                with sp.Fori(1, EXPERTS) as e:
                    expert(e, False)

            @block.gpsimd
            def _(pool):
                def rows_of(e):
                    pool.dma_start(prow[:, :], pos_rows[bass.ds(e, 1), :].to_broadcast([P, S])).then_inc(small_in, 16)
                    pool.dma_start(brow[:, :].bitcast(F32), bias[bass.ds(e, 1), :, :].rearrange("a b n -> (a b) n")).then_inc(small_in, 16)

                rows_of(0)
                with pool.Fori(1, EXPERTS) as e:
                    pool.wait_ge(used, (e - 1) * CHUNKS + 8)
                    pool.wait_ge(selt_ready, e)
                    rows_of(e)

            @block.tensor
            def _(pe):
                def gather(e, n, first):
                    if n == 0:
                        pe.wait_ge(sel_ready, e + 1)
                        if not first:
                            pe.wait_ge(gate_ready, e)
                    else:
                        pe.wait_ge(g_copied, e * 4 + n)
                    part = xl if n % 2 else xh
                    for kk in range(4):
                        k = 4 * (n // 2) + kk
                        for j in range(NT):
                            mm = nc.tensor.matmul(px[:, kk * SLOTS:(kk + 1) * SLOTS], part[:, j, k * P:(k + 1) * P], sel[:, j, :],
                                                  start=(j == 0), stop=(j == NT - 1))
                    mm.then_inc(g_filled, 1)

                def slot_gates(e):
                    for j in range(NT):
                        mm = nc.tensor.matmul(px[:, 0:2], sel[:, j, :], gpart[:, j, bass.ds(e, 1), :].rearrange("p a b -> p (a b)"),
                                              start=(j == 0), stop=(j == NT - 1))
                    mm.then_inc(gate_in, 1)

                def give_back(e, t):
                    if t == 0:
                        pe.wait_ge(y_ready, e * 2 + 2)
                        pe.wait_ge(selt_ready, e + 1)
                    pe.wait_ge(s_added, e * 8 + (t + 1))
                    for part in (yh, yl):
                        mm = nc.tensor.matmul(pr[:, t % 2, :], part[:, t * P:(t + 1) * P], selt[:, :], start=(part is yh), stop=(part is yl))
                    mm.then_inc(s_filled, 1)

                def turn(e, c, first):
                    pe.wait_ge(h_ready, e * 4 + (c + 1))
                    if not (first and c == 0):
                        pe.wait_ge(t_low, e * 4 + c)
                    for i in (0, 1):
                        mm = nc.tensor.transpose(pt[:, i * P:(i + 1) * P], hb[:, c % 2, i * P:(i + 1) * P], K.c("ident"))
                    mm.then_inc(turned, 1)

                def expert(e, first, last):
                    for m in range(CHUNKS):
                        kh, g = halves(m)
                        pe.wait_ge(w_low, e * CHUNKS + (m + 1))
                        if m < 8:
                            o, lh, ll = pu[:, g % 2, :], Xh, Xl
                            if kh == 0:
                                if g == 0:
                                    pe.wait_ge(small_in, e * 32 + 32)
                                    pe.wait_ge(g_copied, e * 4 + 2)
                                if not (first and g < 2):
                                    pe.wait_ge(h_ready, e * 4 + (g - 1))
                                nc.tensor.matmul(o, ones[:, :], brow[:, g * 512:(g + 1) * 512], start=True, stop=False)
                            elif g == 0:
                                pe.wait_ge(g_copied, e * 4 + 4)
                        else:
                            o, lh, ll = pd[:, g, :], hh, hl
                            pe.wait_ge(t_low, e * 4 + (4 if kh else 2))
                            if kh == 0 and not first:
                                pe.wait_ge(y_ready, e * 2 + (g - 1))
                        for kk in range(4):
                            k = 4 * kh + kk
                            c = slice(kk * 512, (kk + 1) * 512)
                            end = kh == 1 and kk == 3
                            nc.tensor.matmul(o, lh[:, k, :], wh[:, m % PARTS, c], start=(m >= 8 and kh == 0 and kk == 0), stop=False)
                            nc.tensor.matmul(o, lh[:, k, :], wl[:, m % PARTS, c], start=False, stop=False)
                            mm = nc.tensor.matmul(o, ll[:, k, :], wh[:, m % PARTS, c], start=False, stop=end)
                        mm.then_inc(used, 1)
                        if not first:
                            beside(e - 1, m + CHUNKS, False, False)
                        beside(e, m, first, last)

                def beside(e, m, first, last):
                    if m in (3, 5, 7, 8):
                        turn(e, 3 if m == 8 else (m - 3) // 2, first)
                    if m == 1:
                        slot_gates(e)
                    if not last and 8 <= m < 12:
                        gather(e + 1, m - 8, False)
                    if CHUNKS + RETURN <= m < CHUNKS + RETURN + DT:
                        give_back(e, m - CHUNKS - RETURN)

                pe.wait_ge(ones_ready, 3)
                for n in range(4):
                    gather(0, n, True)
                expert(0, True, False)
                with pe.Fori(1, EXPERTS - 1) as e:
                    expert(e, False, False)
                expert(EXPERTS - 1, False, True)
                for m in range(CHUNKS, 2 * CHUNKS):
                    beside(EXPERTS - 1, m, False, True)

            @block.scalar
            def _(act):
                def high_part(e, m, first):
                    act.wait_ge(loaded[m % RAW], e * (CHUNKS // RAW * 16) + (16 * (m // RAW) + 16))
                    if not (first and m < PARTS):
                        act.wait_ge(used, e * CHUNKS + (m - PARTS + 1))
                    nc.scalar.activation(wh[:, m % PARTS, :], raw[:, m % RAW, :], ACT.Copy).then_inc(w_high, 1)

                def weighted(e, d):
                    act.wait_ge(used, e * CHUNKS + (11 + d))
                    if d == 0:
                        act.wait_ge(gate_ready, e + 1)
                    nc.scalar.activation(yh[:, d * 512:(d + 1) * 512], pd[:, d, :], ACT.Copy, scale=gneg[:, 0:1]).then_inc(y_high, 1)

                def activate(e, g):
                    act.wait_ge(used, e * CHUNKS + (2 * g + 2))
                    nc.scalar.activation(rl[:, :], pu[:, g % 2, 0:256], ACT.Relu, scale=-1.0, bias=top[:, 0:1]).then_inc(relu, 1)
                    act.wait_ge(relu, e * 4 + (g + 1))
                    nc.scalar.activation(sg[:, :], rl[:, :], ACT.Sigmoid, scale=-SWIGLU_ALPHA, bias=top[:, 1:2]).then_inc(sigmoid, 1)

                def turned_high(e, c):
                    act.wait_ge(turned, e * 4 + (c + 1))
                    nc.scalar.activation(hh[:, 2 * c:2 * c + 2, :], pt[:, :].rearrange("p (a b) -> p a b", a=2), ACT.Copy).then_inc(t_high, 1)

                def gathered(e, n):
                    act.wait_ge(g_filled, e * 4 + (n + 1))
                    part = Xl if n % 2 else Xh
                    nc.scalar.activation(part[:, 4 * (n // 2):4 * (n // 2) + 4, :], px[:, :].rearrange("p (a b) -> p a b", a=4),
                                         ACT.Copy).then_inc(g_copied, 1)

                def expert(e, first, last):
                    for m in range(CHUNKS):
                        high_part(e, m, first)
                        if not first:
                            beside(e - 1, m + CHUNKS, False)
                        beside(e, m, last)

                def beside(e, m, last):
                    if m - AHEAD in (3, 5, 7, 8):
                        turned_high(e, 3 if m - AHEAD == 8 else (m - AHEAD - 3) // 2)
                    if m - AHEAD in (1, 3, 5, 7):
                        activate(e, (m - AHEAD - 1) // 2)
                    if not last and 8 <= m - AHEAD < 12:
                        gathered(e + 1, m - AHEAD - 8)
                    if m - AHEAD in (10, 11):
                        weighted(e, m - AHEAD - 10)

                act.wait_ge(ones_ready, 3)
                for n in range(4):
                    gathered(0, n)
                expert(0, True, False)
                with act.Fori(1, EXPERTS - 1) as e:
                    expert(e, False, False)
                expert(EXPERTS - 1, False, True)
                for m in range(CHUNKS, 2 * CHUNKS):
                    beside(EXPERTS - 1, m, True)

            @block.vector
            def _(dve):
                def low_part(e, m):
                    dve.wait_ge(w_high, e * CHUNKS + (m + 1))
                    nc.vector.tensor_tensor(wl[:, m % PARTS, :], raw[:, m % RAW, :], wh[:, m % PARTS, :], ALU.subtract).then_inc(w_low, 1)

                def weighted(e, d):
                    dve.wait_ge(y_high, e * 2 + (d + 1))
                    c = slice(d * 512, (d + 1) * 512)
                    nc.vector.scalar_tensor_tensor(yl[:, c], pd[:, d, :], gneg[:, 0:1], yh[:, c], ALU.mult, ALU.subtract).then_inc(y_ready, 1)

                def slot_gate(e, first):
                    dve.wait_ge(gate_in, e + 1)
                    if not first:
                        dve.wait_ge(y_ready, e * 2)
                    nc.vector.tensor_reduce(gneg[:, :], px[:, 0:2], AX.X, ALU.add, negate=True).then_inc(gate_ready, 1)

                def activate(e, g):
                    dve.wait_ge(relu, e * 4 + (g + 1))
                    nc.vector.tensor_scalar(vc[:, :], pu[:, g % 2, 256:512], SWIGLU_LIMIT, -SWIGLU_LIMIT, ALU.min, ALU.max).then_inc(own, 1)
                    dve.wait_ge(sigmoid, e * 4 + (g + 1))
                    nc.vector.scalar_tensor_tensor(sg[:, :], rl[:, :], SWIGLU_LIMIT, sg[:, :], ALU.subtract, ALU.mult).then_inc(own, 1)
                    dve.wait_ge(own, e * 8 + (2 * g + 2))
                    nc.vector.scalar_tensor_tensor(hb[:, g % 2, :], vc[:, :], 1.0, sg[:, :], ALU.add, ALU.mult).then_inc(h_ready, 1)

                def turned_low(e, c):
                    dve.wait_ge(t_high, e * 4 + (c + 1))
                    nc.vector.tensor_tensor(hl[:, 2 * c:2 * c + 2, :], pt[:, :].rearrange("p (a b) -> p a b", a=2),
                                            hh[:, 2 * c:2 * c + 2, :], ALU.subtract).then_inc(t_low, 1)

                def add_back(e, t):
                    dve.wait_ge(s_filled, e * 8 + (t + 1))
                    nc.vector.tensor_tensor(out[:, t, :], out[:, t, :], pr[:, t % 2, :], ALU.add).then_inc(s_added, 1)

                def select(e, first):
                    if not first:
                        dve.wait_ge(g_filled, e * 4)
                        dve.wait_ge(gate_in, e)
                    for j in range(NT):
                        ins = nc.vector.tensor_scalar(sel[:, j, :], K.c("iota"), pos[:, j, bass.ds(e, 1)], None, ALU.is_equal)
                    ins.then_inc(sel_ready, 1)

                def select_back(e, first):
                    dve.wait_ge(small_in, e * 32 + 32)
                    if not first:
                        dve.wait_ge(s_filled, e * 8)
                    nc.vector.tensor_scalar(selt[:, :], prow[:, :], K.const[:, CONST["slot"][0]:CONST["slot"][0] + 1], None,
                                            ALU.is_equal).then_inc(selt_ready, 1)

                def expert(e, first, last):
                    for m in range(CHUNKS):
                        low_part(e, m)
                        if not first:
                            beside(e - 1, m + CHUNKS, False, False)
                        beside(e, m, first, last)

                def beside(e, m, first, last):
                    if m - AHEAD in (1, 3, 5, 7):
                        activate(e, (m - AHEAD - 1) // 2)
                    if m - AHEAD in (3, 5, 7, 8):
                        turned_low(e, 3 if m - AHEAD == 8 else (m - AHEAD - 3) // 2)
                    if m - AHEAD in (10, 11):
                        weighted(e, m - AHEAD - 10)
                    if m - AHEAD == 1:
                        slot_gate(e, first)
                    if m == 7 and not last:
                        select(e + 1, False)
                    if m - AHEAD == RETURN + DT - 1:
                        select_back(e, first)
                    if 0 <= m - AHEAD - CHUNKS - RETURN < DT:
                        add_back(e, m - AHEAD - CHUNKS - RETURN)

                nc.vector.memset(top[:, 0:1], SWIGLU_LIMIT).then_inc(ones_ready, 1)
                nc.vector.memset(top[:, 1:2], SWIGLU_LIMIT * SWIGLU_ALPHA).then_inc(ones_ready, 1)
                nc.vector.tensor_copy(ones[:, :], K.c("ones", 2)).then_inc(ones_ready, 1)
                dve.sem_inc(s_added, 2)
                select(0, True)
                expert(0, True, False)
                with dve.Fori(1, EXPERTS - 1) as e:
                    expert(e, False, False)
                expert(EXPERTS - 1, False, True)
                for m in range(CHUNKS, 2 * CHUNKS):
                    beside(EXPERTS - 1, m, False, True)


def rest_of_experts(K, over, x_in, w, bias, late, out):
    nc = K.nc
    FJ = FE // P
    with ExitStack() as ctx:
        wt = K.sb(ctx, "wt", [P, CHUNKS, CW])
        gate = K.sb(ctx, "gate", [P, S])
        brow = K.sb(ctx, "brow", [1, 2 * FE])
        one_row = K.sb(ctx, "one_row", [1, S])
        x = K.sb(ctx, "x_kept", [P, DT, S])
        h = K.sb(ctx, "hact", [P, FJ, S])
        gt = K.sb(ctx, "gt", [P, 2, S])
        vl = K.sb(ctx, "vl", [P, 2, S])
        sg = K.sb(ctx, "sg", [P, 2, S])
        pg = K.ps(ctx, "pg", [P, 2, S])
        pv = K.ps(ctx, "pv", [P, 2, S])
        pd = K.ps(ctx, "pd", [P, 2, S])
        with stage(nc, "ones_ready", "x_loaded", "loaded", "up", "clipped", "sigmoid", "value", "glu", "down", "added") as (
                block, ones_ready, x_loaded, loaded, up, clipped, sigmoid, value, glu, down, added):
            @block.sync
            def _(sp):
                with sp.If(sp.value_load(over[0:1, 0:1]) > 0):
                    sp.dma_start(x[:, :, :], x_in).then_inc(x_loaded, 16)
                    with sp.Fori(0, EXPERTS) as e:
                        sp.wait_ge(added, e * DT + 2)
                        for m in range(CHUNKS):
                            sp.dma_start(wt[:, m, :], w[bass.ds(e, 1), m, :, :].rearrange("a p n -> (a p) n")).then_inc(loaded, 16)
                        sp.dma_start(gate[:, :], late[bass.ds(e, 1), :].to_broadcast([P, S])).then_inc(loaded, 16)
                        sp.dma_start(brow[:, :], bias[bass.ds(e, 1), :]).then_inc(loaded, 16)

            @block.tensor
            def _(pe):
                with pe.If(pe.value_load(over[0:1, 0:1]) > 0):
                    pe.wait_ge(ones_ready, 1)
                    pe.wait_ge(x_loaded, 16)
                    with pe.Fori(0, EXPERTS) as e:
                        pe.wait_ge(loaded, e * (16 * CHUNKS + 32) + (16 * CHUNKS + 32))
                        for j in range(FJ):
                            pe.wait_ge(glu, e * FJ + (j + 1))
                            for bank, half in ((pg, 0), (pv, 256)):
                                o = half + j % 2 * P
                                b = j // 2 * 512 + o
                                nc.tensor.matmul(bank[:, j % 2, :], brow[0:1, b:b + P], one_row[:, :], start=True, stop=False)
                                for k in range(DT):
                                    c = k % 4 * 512 + o
                                    mm = nc.tensor.matmul(bank[:, j % 2, :], wt[:, j // 2 * 2 + k // 4, c:c + P], x[:, k, :],
                                                          start=False, stop=(k == DT - 1))
                            mm.then_inc(up, 1)
                        pe.wait_ge(glu, e * FJ + (FJ + 2))
                        for t in range(DT):
                            pe.wait_ge(added, e * DT + (t + 1))
                            for k in range(FJ):
                                c = k % 4 * 512 + t % 4 * P
                                mm = nc.tensor.matmul(pd[:, t % 2, :], wt[:, 8 + k // 4 * 2 + t // 4, c:c + P], h[:, k, :],
                                                      start=(k == 0), stop=(k == FJ - 1))
                            mm.then_inc(down, 1)

            @block.scalar
            def _(act):
                with act.If(act.value_load(over[0:1, 0:1]) > 0):
                    with act.Fori(0, EXPERTS) as e:
                        for j in range(FJ):
                            act.wait_ge(clipped, e * FJ + (j + 1))
                            nc.scalar.activation(sg[:, j % 2, :], gt[:, j % 2, :], ACT.Sigmoid, scale=SWIGLU_ALPHA).then_inc(sigmoid, 1)

            @block.vector
            def _(dve):
                with dve.If(dve.value_load(over[0:1, 0:1]) > 0):
                    nc.vector.memset(one_row[:, :], 1.0).then_inc(ones_ready, 1)
                    dve.sem_inc(glu, 2)
                    dve.sem_inc(added, 2)
                    with dve.Fori(0, EXPERTS) as e:
                        dve.wait_ge(loaded, e * (16 * CHUNKS + 32) + (16 * CHUNKS + 32))
                        for j in range(FJ):
                            b = j % 2
                            dve.wait_ge(up, e * FJ + (j + 1))
                            nc.vector.tensor_scalar(gt[:, b, :], pg[:, b, :], SWIGLU_LIMIT, None, ALU.min).then_inc(clipped, 1)
                            nc.vector.tensor_scalar(vl[:, b, :], pv[:, b, :], SWIGLU_LIMIT, -SWIGLU_LIMIT, ALU.min, ALU.max).then_inc(value, 1)
                            dve.wait_ge(clipped, e * FJ + (j + 1))
                            dve.wait_ge(value, e * 3 * FJ + (3 * j + 1))
                            nc.vector.scalar_tensor_tensor(vl[:, b, :], vl[:, b, :], 1.0, gt[:, b, :], ALU.add, ALU.mult).then_inc(value, 1)
                            dve.wait_ge(value, e * 3 * FJ + (3 * j + 2))
                            nc.vector.tensor_tensor(vl[:, b, :], vl[:, b, :], gate[:, :], ALU.mult).then_inc(value, 1)
                            dve.wait_ge(value, e * 3 * FJ + (3 * j + 3))
                            dve.wait_ge(sigmoid, e * FJ + (j + 1))
                            nc.vector.tensor_tensor(h[:, j, :], vl[:, b, :], sg[:, b, :], ALU.mult).then_inc(glu, 1)
                        for t in range(DT):
                            dve.wait_ge(down, e * DT + (t + 1))
                            nc.vector.tensor_tensor(out[:, t, :], out[:, t, :], pd[:, t % 2, :], ALU.add).then_inc(added, 1)


def per_layer_embedding(K, h, w_gate, w_proj, p):
    nc = K.nc
    with ExitStack() as ctx:
        pp = K.sb(ctx, "pp", [P, PLE // P, S])
        g = K.sb(ctx, "g", [P, DT, S])
        e = K.sb(ctx, "e", [P, DT, S])
        load(K, [(pp[:, :, :], p)])
        with parts_of(K, h) as (high, low):
            project(K, w_gate, DT, DT, high, low, S, g)
        with parts_of(K, pp) as (high, low):
            project(K, w_proj, DT, PLE // P, high, low, S, e)
        with stage(nc, "gate", "own") as (block, gate, own):
            @block.scalar
            def _(act):
                for t in range(DT):
                    nc.scalar.activation(g[:, t, :], g[:, t, :], ACT.Sigmoid).then_inc(gate, 1)

            @block.vector
            def _(dve):
                step = Own(dve, own)
                for t in range(DT):
                    dve.wait_ge(gate, t + 1)
                    step.go(nc.vector.tensor_tensor(g[:, t, :], g[:, t, :], e[:, t, :], ALU.mult))
                step.all()
                step(nc.vector.tensor_tensor(h[:, :, :], h[:, :, :], g[:, :, :], ALU.add))


def tiles(x, n=DT):
    return [x[:, t, :] for t in range(n)]


def mixture(K, a, x):
    with ExitStack() as ctx:
        over = K.sb(ctx, "over", [1, 2], I32)
        with ExitStack() as c2:
            pos = K.sb(c2, "pos", [P, NT, EXPERTS])
            gpart = K.sb(c2, "gpart", [P, NT, EXPERTS, 2], F32R)
            xh = K.sb(c2, "xt_high", [P, NT, D], F32R)
            xl = K.sb(c2, "xt_low", [P, NT, D], F32R)
            with ExitStack() as c3:
                gates = K.sb(c3, "gates", [P, NT, EXPERTS])
                b_down = K.sb(c3, "b_down", [EXPERTS, D])
                rw = K.sb(c3, "rw", [P, DT, EXPERTS])
                rb = K.sb(c3, "rb", [1, EXPERTS])
                load(K, [(rw[:, :, :], a["router_w"]), (rb[:, :], a["router_b"]), (b_down[:, :], a["exp_b_down"])])
                router(K, x, rw, rb, gates)
                dispatch(K, x, gates, b_down, pos, gpart, xh, xl, over, a["expert_rows"], a["mixture_in"])
                split_biases(K, a["exp_b_gu"], a["bias_parts"])
            experts(K, pos, gpart, xh, xl, a["exp_w"], a["bias_parts"], a["expert_rows"][0], x)
        rest_of_experts(K, over, a["mixture_in"], a["exp_w"], a["exp_b_gu"], a["expert_rows"][1], x)


def first_block(K, a, x):
    nc = K.nc
    with ExitStack() as ctx:
        y = K.sb(ctx, "y", [P, DT, S])
        with ExitStack() as c2:
            U = K.sb(c2, "U", [P, U_TILES, S])
            gate_up = K.sb(c2, "gate_up", [P, P])
            lora = K.sb(c2, "lora", [P, 256])
            load(K, [(gate_up[ROW_GD:ROW_GD + 16, :], a["gla_gate_up"]), (lora[:, :], a["rwkv_lora"])])
            with parts_of(K, x) as (high, low):
                project(K, a["w_in"], U_TILES, DT, high, low, S, U)
            with ExitStack() as c3:
                conv = K.sb(c3, "conv", [P, 8, S])
                rows = K.sb(c3, "rows", [H, 5, S])
                cols = K.sb(c3, "gate_cols", [P, 3, NT, H])
                short_convs(K, U, conv)
                scalar_gates(K, U, rows, cols)
                ssd(K, U, conv, rows, cols, y[:, 0:2, :])
                mlstm(K, U, conv, rows, cols, y[:, 6:8, :])
            gla(K, U, gate_up, y[:, 4:6, :])
            rwkv(K, U, lora, y[:, 2:4, :])
        with parts_of(K, y) as (high, low):
            project(K, a["w_out"], DT, DT, high, low, S, x, residual=x, alpha=ALPHA1)
        normalise(K, [tiles(x)], [tiles(x)], K.c("mean1024"), 1e-5, True, lambda t: K.col("ln1_g", t),
                  bias=lambda t: K.col("ln1_b", t))
    mixture(K, a, x)
    per_layer_embedding(K, x, a["ple_gate_w"], a["ple_proj"], a["p"])
    normalise(K, [tiles(x)], [tiles(x)], K.c("mean1024"), 1e-5, True, lambda t: K.col("ln2_g", t),
              bias=lambda t: K.col("ln2_b", t))


DQ, DK, DV = 0, 4, 8
HQ, HFF, HFB, HI, HG = 0, 4, 8, 12, 16
DA_TILES, HG_TILES, MX_TILES = 12, 20, 4
MIX_TILES = 12
TWO_PI_HI = 6.28125
TWO_PI_LO = float(2 * np.pi - 6.28125)
ROUND = 1.5 * 2.0 ** 23


def rope_tables(K, positions, cs, sn):
    nc = K.nc
    with ExitStack() as ctx:
        pi = K.sb(ctx, "pi", [P, S], I32)
        ang = K.sb(ctx, "ang", [P, S])
        k = K.sb(ctx, "k", [P, S])
        with stage(nc, "loaded", "own", "reduced", "done") as (block, loaded, own, reduced, done):
            @block.sync
            def _(sp):
                sp.dma_start(pi[:, :], positions.to_broadcast([P, S])).then_inc(loaded, 16)

            @block.vector
            def _(dve):
                step = Own(dve, own)
                dve.wait_ge(loaded, 16)
                step(nc.vector.tensor_copy(ang[:, :], pi[:, :]))
                step(nc.vector.tensor_scalar(ang[:, :], ang[:, :], K.const[:, CONST["freq"][0]:CONST["freq"][0] + 1], None, ALU.mult))
                step(nc.vector.tensor_scalar(k[:, :], ang[:, :], float(1 / (2 * np.pi)), None, ALU.mult))
                step(nc.vector.tensor_scalar(k[:, :], k[:, :], ROUND, None, ALU.add))
                step(nc.vector.tensor_scalar(k[:, :], k[:, :], ROUND, None, ALU.subtract))
                step(nc.vector.scalar_tensor_tensor(ang[:, :], k[:, :], -TWO_PI_HI, ang[:, :], ALU.mult, ALU.add))
                step(nc.vector.scalar_tensor_tensor(ang[:, :], k[:, :], -TWO_PI_LO, ang[:, :], ALU.mult, ALU.add))
                step(nc.vector.tensor_scalar(ang[:, :], ang[:, :], 3.141592, -3.141592, ALU.min, ALU.max))
                step(nc.vector.scalar_tensor_tensor(k[:, :], ang[:, :], -1.0, ang[:, :], ALU.mult, ALU.max))
                nc.vector.tensor_scalar(k[:, :], k[:, :], -1.0, float(np.pi / 2), ALU.mult, ALU.add).then_inc(reduced, 1)

            @block.scalar
            def _(act):
                act.wait_ge(reduced, 1)
                nc.scalar.activation(sn[:, :], ang[:, :], ACT.Sin).then_inc(done, 1)
                nc.scalar.activation(cs[:, :], k[:, :], ACT.Sin).then_inc(done, 1)


def rope(K, U, n, cs, sn):
    nc = K.nc
    with ExitStack() as ctx:
        t = K.sb(ctx, "t", [P, 2, S])
        ps = K.ps(ctx, "ps", [P, 2, S])
        with stage(nc, "turned", "own", "done") as (block, turned, own, done):
            @block.tensor
            def _(pe):
                for i in range(n):
                    if i >= 2:
                        pe.wait_ge(done, i - 1)
                    nc.tensor.matmul(ps[:, i % 2, :], K.c("rot"), U[:, i, :], start=True, stop=True).then_inc(turned, 1)

            @block.vector
            def _(dve):
                step = Own(dve, own)
                for i in range(n):
                    dve.wait_ge(turned, i + 1)
                    step.go(nc.vector.tensor_tensor(t[:, i % 2, :], ps[:, i % 2, :], sn[:, :], ALU.mult))
                    step(nc.vector.tensor_tensor(U[:, i, :], U[:, i, :], cs[:, :], ALU.mult))
                    nc.vector.tensor_tensor(U[:, i, :], U[:, i, :], t[:, i % 2, :], ALU.add).then_inc(done, 1)


def softmax_attention(K, parts, query, key, n_key, value, scale, neglam, out):
    nc = K.nc
    KT = n_key // P
    steps = [(h, q) for h in range(H) for q in range(NT)]
    with ExitStack() as ctx:
        p = K.sb(ctx, "p", [P, 2, parts, n_key])
        at = K.sb(ctx, "at", [P, 2, KT, S])
        top = K.sb(ctx, "top", [P, 2, 2])
        total = K.sb(ctx, "total", [P, 2, 2])
        sc = K.ps(ctx, "sc", [P, 2, parts, 512])
        tr = K.ps(ctx, "tr", [P, 2, 512])
        po = K.ps(ctx, "po", [P, 2, 512])
        with stage(nc, "own", "scored", "maximum", "exps", "mixed", "turned", "gathered", "summed", "stored") as (
                block, own, scored, maximum, exps, mixed, turned, gathered, summed, stored):
            @block.tensor
            def _(pe):
                def scores(n):
                    h, q = steps[n]
                    if n >= 2:
                        pe.wait_ge(exps, parts * (n - 1))
                    for c in range(parts):
                        mm = nc.tensor.matmul(sc[:, n % 2, c, 0:n_key], query(h, c)[:, q * P:(q + 1) * P], key(h, c),
                                              start=True, stop=True)
                    mm.then_inc(scored, 1)

                scores(0)
                scores(1)
                for n, (h, q) in enumerate(steps):
                    if n + 2 < len(steps):
                        scores(n + 2)
                    pe.wait_ge(mixed, n + 1)
                    if n >= 2:
                        pe.wait_ge(gathered, n - 1)
                    for t in range(KT):
                        mm = nc.tensor.transpose(tr[:, n % 2, t * P:(t + 1) * P], p[:, n % 2, 0, t * P:(t + 1) * P], K.c("ident"))
                    mm.then_inc(turned, 1)
                    if q == NT - 1:
                        pe.wait_ge(gathered, n + 1)
                        if h >= 2:
                            pe.wait_ge(stored, h - 1)
                        for t in range(KT):
                            mm = nc.tensor.matmul(po[:, h % 2, :], value(h, t), at[:, h % 2, t, :], start=(t == 0), stop=(t == KT - 1))
                        mm.then_inc(summed, 1)

            @block.scalar
            def _(act):
                def gather(n):
                    h, q = steps[n]
                    act.wait_ge(turned, n + 1)
                    if h >= 2 and q == 0:
                        act.wait_ge(summed, h - 1)
                    nc.scalar.activation(at[:, h % 2, :, q * P:(q + 1) * P], tr[:, n % 2, 0:KT * P].rearrange("p (t q) -> p t q", q=P),
                                         ACT.Copy).then_inc(gathered, 1)

                def store(h):
                    act.wait_ge(summed, h + 1)
                    nc.scalar.activation(out(h), po[:, h % 2, :], ACT.Copy).then_inc(stored, 1)

                for n, (h, q) in enumerate(steps):
                    act.wait_ge(maximum, n + 1)
                    if n >= 2:
                        act.wait_ge(turned, n - 1)
                    for c in range(parts):
                        nc.scalar.activation(p[:, n % 2, c, :], sc[:, n % 2, c, 0:n_key], ACT.Exp, bias=top[:, n % 2, c:c + 1],
                                             scale=scale, accum_out=total[:, n % 2, c:c + 1]).then_inc(exps, 1)
                    if n:
                        gather(n - 1)
                    if q == 1 and h:
                        store(h - 1)
                gather(len(steps) - 1)
                store(H - 1)

            @block.vector
            def _(dve):
                step = Own(dve, own)

                def maxima(n):
                    dve.wait_ge(scored, n + 1)
                    if n >= 2:
                        dve.wait_ge(exps, parts * (n - 1))
                    step(nc.vector.tensor_reduce(top[:, n % 2, 0:parts], sc[:, n % 2, :, 0:n_key], AX.X, ALU.max, negate=True))
                    nc.vector.tensor_scalar(top[:, n % 2, 0:parts], top[:, n % 2, 0:parts], scale, None, ALU.mult).then_inc(maximum, 1)

                maxima(0)
                for n in range(len(steps)):
                    if n + 1 < len(steps):
                        maxima(n + 1)
                    dve.wait_ge(exps, parts * (n + 1))
                    step(nc.vector.reciprocal(total[:, n % 2, 0:parts], total[:, n % 2, 0:parts]))
                    a, b = p[:, n % 2, 0, :], p[:, n % 2, parts - 1, :]
                    if parts == 2:
                        step.go(nc.vector.tensor_scalar(total[:, n % 2, 1:2], total[:, n % 2, 1:2], neglam[:, 0:1], None, ALU.mult))
                        step(nc.vector.tensor_scalar(a, a, total[:, n % 2, 0:1], None, ALU.mult))
                        nc.vector.scalar_tensor_tensor(a, b, total[:, n % 2, 1:2], a, ALU.mult, ALU.add).then_inc(mixed, 1)
                    else:
                        nc.vector.tensor_scalar(a, a, total[:, n % 2, 0:1], None, ALU.mult).then_inc(mixed, 1)


def differential(K, layer, parts, w, cs, sn, y):
    nc = K.nc
    lam_init = 0.8 - 0.6 * float(np.exp(-0.3 * layer))
    with ExitStack() as ctx:
        U = K.sb(ctx, "Uda", [P, DA_TILES, S])
        project(K, w, DA_TILES, DT, *parts, S, U)
        vt = K.sb(ctx, "vt", [P, NT, H * P])
        neglam = K.sb(ctx, "neglam", [P, 2])
        pr = K.sb(ctx, "pr", [64, 2])
        with ExitStack() as c2:
            ps = K.ps(c2, "ps", [P, 2])
            with stage(nc, "own", "product", "summed", "exps") as (block, own, product, summed, exps):
                lf = K.col("da_lambda_2", 4 * layer, 64, 4).rearrange("p (a b) -> p a b", b=2)

                @block.vector
                def _(dve):
                    step = Own(dve, own)
                    nc.vector.tensor_tensor(pr[:, :], lf[:, :, 0], lf[:, :, 1], ALU.mult).then_inc(product, 1)
                    dve.wait_ge(exps, 1)
                    step(nc.vector.tensor_tensor(neglam[:, 0:1], neglam[:, 1:2], neglam[:, 0:1], ALU.subtract))
                    step(nc.vector.tensor_scalar(neglam[:, 0:1], neglam[:, 0:1], lam_init, None, ALU.subtract))

                @block.tensor
                def _(pe):
                    pe.wait_ge(product, 1)
                    nc.tensor.matmul(ps[:, :], K.c("ones", 64), pr[:, :], start=True, stop=True).then_inc(summed, 1)

                @block.scalar
                def _(act):
                    act.wait_ge(summed, 1)
                    nc.scalar.activation(neglam[:, :], ps[:, :], ACT.Exp).then_inc(exps, 1)
        rope(K, U, DV, cs, sn)
        transposes(K, [(U[:, DV + t, :], vt[:, :, t * P:(t + 1) * P]) for t in range(H)])
        softmax_attention(K, 2, lambda h, c: U[64 * c:64 * c + 64, DQ + h, :], lambda h, c: U[64 * c:64 * c + 64, DK + h, :],
                          S, lambda h, t: vt[:, t, h * P:(h + 1) * P], 0.125, neglam, lambda h: y[h])
    normalise(K, [[t] for t in y], [[t] for t in y], K.c("mean128"), 1e-6, False, lambda t: K.col("da_norm_g_2", layer),
              scale=1.0 - lam_init)


def memory(K, parts, w, w_kv, mem, y):
    with ExitStack() as ctx:
        U = K.sb(ctx, "Umx", [P, MX_TILES, S])
        kv = K.sb(ctx, "kv", [P, 2 * H, MEM])
        vt = K.sb(ctx, "vt", [P, MEM // P, H * P])
        project(K, w, MX_TILES, DT, *parts, S, U)
        with ExitStack() as c2:
            mm = K.sb(c2, "mem", [P, DT, MEM])
            load(K, [(mm[:, :, :], mem)])
            with parts_of(K, mm, MEM) as (high, low):
                project(K, w_kv, 2 * H, DT, high, low, MEM, kv)
        transposes(K, [(kv[:, H + t, :], vt[:, :, t * P:(t + 1) * P]) for t in range(H)])
        softmax_attention(K, 1, lambda h, c: U[:, h, :], lambda h, c: kv[:, h, :], MEM,
                          lambda h, t: vt[:, t, h * P:(h + 1) * P], P ** -0.5, None, lambda h: y[h])


def hgrn_direction(K, q, z, lb, back, vt, out, add):
    nc = K.nc
    order = list(range(NT - 1, -1, -1)) if back else list(range(NT))
    with ExitStack() as ctx:
        b = K.sb(ctx, "b", [P, H, S])
        k = K.sb(ctx, "k", [P, H, S])
        e = K.sb(ctx, "e", [P, H, S])
        qe = K.sb(ctx, "qe", [P, H, S])
        ke = K.sb(ctx, "ke", [P, H, S])
        att = K.sb(ctx, "att", [P, NT, H, P])
        one = K.sb(ctx, "one", [P, P])
        with stage(nc, "own", "sigmoid", "ready", "logs", "low_in") as (block, own, sigmoid, ready, logs, low_in):
            @block.scalar
            def _(act):
                nc.scalar.activation(e[:, :, :], z, ACT.Sigmoid).then_inc(sigmoid, 1)
                act.wait_ge(ready, 1)
                nc.scalar.activation(qe[:, :, :], qe[:, :, :], ACT.Ln).then_inc(logs, 1)
                nc.scalar.activation(ke[:, :, :], ke[:, :, :], ACT.Ln, scale=2.0 ** 60).then_inc(logs, 1)

            @block.vector
            def _(dve):
                step = Own(dve, own)
                step.go(nc.vector.memset(one[:, :], 1.0))
                step.go(nc.vector.memset(att[:, :, :, :], 0.0))
                dve.wait_ge(sigmoid, 1)
                if lb is not None:
                    step.all()
                    step(nc.vector.tensor_scalar(k[:, 0, 0:H], lb, -1.0, 1.0, ALU.mult, ALU.add))
                    for h in range(H):
                        step.go(nc.vector.tensor_scalar(e[:, h, :], e[:, h, :], k[:, 0, h:h + 1], lb[:, h:h + 1], ALU.mult, ALU.add))
                step.all()
                step(nc.vector.tensor_scalar(e[:, :, :], e[:, :, :], 1e-20, None, ALU.max))
                step.go(nc.vector.tensor_scalar(k[:, :, :], e[:, :, :], -1.0, 1.0, ALU.mult, ALU.add))
                step.go(nc.vector.tensor_scalar(qe[:, :, :], e[:, :, :], 2.0 ** -60, None, ALU.max))
                nc.vector.tensor_scalar(ke[:, :, :], e[:, :, :], 2.0 ** -60, None, ALU.min).then_inc(ready, 1)
                step.all()
                dve.wait_ge(logs, 2)
                step(nc.vector.tensor_tensor(e[:, :, :], qe[:, :, :], ke[:, :, :], ALU.add))
                for h in range(H):
                    for c in range(NT):
                        to, at = b[:, h, c * P:(c + 1) * P], e[:, h, c * P:(c + 1) * P]
                        if back:
                            to, at = to[:, ::-1], at[:, ::-1]
                        step.go(nc.vector.tensor_tensor_scan(to, one[:, :], at, 0.0, ALU.mult, ALU.add))
                step.all()
        with ExitStack() as c2:
            ps = K.ps(c2, "ps", [P, 4, H, P])
            mask = "bwd" if back else "fwd"
            rounds = [None] + list(range(len(HALVES)))
            with stage(nc, "own", "offset", "size", "decay", "decayed", "product", "kept") as (
                    block, own, offset, size, decay, decayed, product, kept):
                @block.tensor
                def _(pe):
                    for i, lv in enumerate(rounds):
                        if i:
                            pe.wait_ge(decayed, 2 * i)
                        for c in range(NT):
                            n = i * NT + c
                            if n >= 4:
                                pe.wait_ge(kept, n - 3)
                            for h in range(H):
                                left, right = (k, q) if lv is None else (ke, qe)
                                mm = nc.tensor.matmul(ps[:, c, h, :], left[:, h, c * P:(c + 1) * P], right[:, h, c * P:(c + 1) * P],
                                                      start=True, stop=True)
                            mm.then_inc(product, 1)

                @block.scalar
                def _(act):
                    for i in range(len(HALVES)):
                        act.wait_ge(offset, i + 1)
                        nc.scalar.activation(e[:, :, :], e[:, :, :], ACT.Abs).then_inc(size, 1)
                        act.wait_ge(size, i + 1)
                        nc.scalar.activation(e[:, :, :], e[:, :, :], ACT.Exp, scale=-1.0).then_inc(decay, 1)

                @block.vector
                def _(dve):
                    def offsets(lv):
                        half = HALVES[lv]
                        pivot = half if back else half - 1
                        bb = b[:, :, :].rearrange("p h (n m) -> p (h n) m", m=2 * half)
                        ee = e[:, :, :].rearrange("p h (n m) -> p (h n) m", m=2 * half)
                        nc.vector.tensor_tensor(ee, bb, bb[:, :, pivot:pivot + 1].to_broadcast([P, H * S // (2 * half), 2 * half]),
                                                ALU.subtract).then_inc(offset, 1)

                    for i, lv in enumerate(rounds):
                        if lv is not None:
                            dve.wait_ge(decay, i)
                            dve.wait_ge(product, i * NT)
                            nc.vector.tensor_tensor(qe[:, :, :], q, e[:, :, :], ALU.mult).then_inc(decayed, 1)
                            nc.vector.tensor_tensor(ke[:, :, :], k[:, :, :], e[:, :, :], ALU.mult).then_inc(decayed, 1)
                            m = K.c(mask, P, lv)
                            dve.wait_ge(decayed, 2 * i)
                        else:
                            m = K.c("ident")
                        if i < len(HALVES):
                            offsets(rounds[i + 1])
                        m = m.bitcast(I32).unsqueeze(1).to_broadcast([P, H, P])
                        for c in range(NT):
                            dve.wait_ge(product, i * NT + c + 1)
                            nc.vector.copy_predicated(att[:, c, :, :], m, ps[:, c, :, :]).then_inc(kept, 1)
                        dve.wait_ge(kept, (i + 1) * NT)
        ends = K.sb(ctx, "ends", [P, H, NT])
        end = 0 if back else P - 1
        with stage(nc, "own", "offset", "decay") as (block, own, offset, decay):
            @block.vector
            def _(dve):
                step = Own(dve, own)
                bb = b[:, :, :].rearrange("p h (n m) -> p (h n) m", m=P)
                step.go(nc.vector.tensor_copy(ends[:, :, :].rearrange("p h n -> p (h n)").unsqueeze(2), bb[:, :, end:end + 1]))
                nc.vector.tensor_tensor(e[:, :, :].rearrange("p h (n m) -> p (h n) m", m=P),
                                        bb[:, :, end:end + 1].to_broadcast([P, H * NT, P]), bb, ALU.subtract).then_inc(offset, 1)
                step.all()
                dve.wait_ge(decay, 3)
                step.go(nc.vector.tensor_tensor(qe[:, :, :], q, qe[:, :, :], ALU.mult))
                step.go(nc.vector.tensor_tensor(ke[:, :, :], k[:, :, :], e[:, :, :], ALU.mult))
                step.all()

            @block.scalar
            def _(act):
                nc.scalar.activation(qe[:, :, :], b[:, :, :], ACT.Exp).then_inc(decay, 1)
                act.wait_ge(offset, 1)
                nc.scalar.activation(e[:, :, :], e[:, :, :], ACT.Exp).then_inc(decay, 1)
                nc.scalar.activation(ends[:, :, :], ends[:, :, :], ACT.Exp).then_inc(decay, 1)
        kt = e[:, :, :].rearrange("p h (n m) -> p n h m", m=P)
        transposes(K, [(ke[:, h, :], kt[:, :, h, :]) for h in range(H)])
        state = k
        with ExitStack() as c2:
            po = K.ps(c2, "po", [P, H, S])
            kv = K.ps(c2, "kv", [P, 2, H, P])
            with stage(nc, "own", "contrib", "state_ready", "chunk_done") as (block, own, contrib, state_ready, chunk_done):
                @block.tensor
                def _(pe):
                    for i, c in enumerate(order):
                        for h in range(H):
                            mm = nc.tensor.matmul(kv[:, i % 2, h, :], kt[:, c, h, :], vt[:, c, h * P:(h + 1) * P], start=True, stop=True)
                        mm.then_inc(contrib, 1)
                        if i:
                            pe.wait_ge(state_ready, i)
                        for h in range(H):
                            o = po[:, h, c * P:(c + 1) * P]
                            if i:
                                nc.tensor.matmul(o, state[:, h, 0:P], qe[:, h, c * P:(c + 1) * P], start=True, stop=False)
                            mm = nc.tensor.matmul(o, vt[:, c, h * P:(h + 1) * P], att[:, c, h, :], start=(i == 0), stop=True)
                        mm.then_inc(chunk_done, 1)

                @block.vector
                def _(dve):
                    step = Own(dve, own)
                    for i, c in enumerate(order[:-1]):
                        dve.wait_ge(contrib, i + 1)
                        if i:
                            dve.wait_ge(chunk_done, i + 1)
                            for h in range(H):
                                step.go(nc.vector.tensor_scalar(state[:, h, 0:P], state[:, h, 0:P], ends[:, h, c:c + 1], None, ALU.mult))
                            step.all()
                            nc.vector.tensor_tensor(state[:, :, 0:P], state[:, :, 0:P], kv[:, i % 2, :, :], ALU.add).then_inc(state_ready, 1)
                        else:
                            nc.vector.tensor_copy(state[:, :, 0:P], kv[:, 0, :, :]).then_inc(state_ready, 1)
                        dve.wait_ge(state_ready, i + 1)
                    dve.wait_ge(chunk_done, NT)
                    if add:
                        step(nc.vector.tensor_tensor(out, out, po[:, :, :], ALU.add))
                    else:
                        step(nc.vector.tensor_copy(out, po[:, :, :]))


def hgrn(K, layer, parts, w, y):
    nc = K.nc
    with ExitStack() as ctx:
        U = K.sb(ctx, "Uhg", [P, HG_TILES, S])
        lb = K.sb(ctx, "lb", [P, 2, H])
        project(K, w, HG_TILES, DT, *parts, S, U)
        vt = K.sb(ctx, "vt", [P, NT, H * P])
        transposes(K, [(U[:, HI + t, :], vt[:, :, t * P:(t + 1) * P]) for t in range(H)])
        with stage(nc, "own", "silu", "diff") as (block, own, silu, diff):
            @block.vector
            def _(dve):
                for i, name in enumerate(("hg_lb_fwd_2", "hg_lb_bwd_2")):
                    nc.vector.tensor_tensor(lb[:, i, :], K.col(name, H, P, H), K.col(name, 0, P, H), ALU.subtract).then_inc(diff, 1)

            @block.scalar
            def _(act):
                nc.scalar.activation(U[:, HQ:HQ + H, :], U[:, HQ:HQ + H, :], ACT.Silu).then_inc(silu, 1)
                nc.scalar.activation(U[:, HG:HG + H, :], U[:, HG:HG + H, :], ACT.Silu).then_inc(silu, 1)
                act.wait_ge(diff, 2)
                nc.scalar.activation(lb[:, :, :], lb[:, :, :], ACT.Sigmoid).then_inc(silu, 1)
        for i, back in enumerate((False, True)):
            z = U[:, (HFB if back else HFF):(HFB if back else HFF) + H, :]
            hgrn_direction(K, U[:, HQ:HQ + H, :], z, lb[:, i, :] if layer else None, back, vt, y, back)
        normalise(K, [[y[:, h, :]] for h in range(H)], [[y[:, h, :]] for h in range(H)], K.c("mean128"), 1e-6, False,
                  lambda t: K.col("hg_norm_g_2", layer), gate=lambda t: U[:, HG + t, :])


def conv_up(K, layer, high, low, w, out_high, out_low):
    nc = K.nc
    wcol, bcol = COLS["conv_w_2"][0] + 3 * 2 * FT * layer, COLS["conv_b_2"][0] + 2 * FT * layer
    PAIRS = FT // 2
    HALF = DT * P
    with ExitStack() as ctx:
        raw = K.sb(ctx, "raw", [P, 2 * HALF])
        wh = K.sb(ctx, "wh", [P, 2, HALF], F32R)
        wl = K.sb(ctx, "wl", [P, 2, HALF], F32R)
        cv = K.sb(ctx, "cv", [P, 2, S])
        sg = K.sb(ctx, "sg", [P, S])
        ps = K.ps(ctx, "ps", [P, 2, 2, S])
        with stage(nc, "loaded", "high_ready", "low_ready", "product", "centre", "sides", "silu", "full", "done", "done_low") as (
                block, loaded, high_ready, low_ready, product, centre, sides, silu, full, done, done_low):
            @block.sync
            def _(sp):
                sp.dma_start(raw[:, :], w[0]).then_inc(loaded, 16)
                with sp.Fori(1, FT) as n:
                    sp.wait_ge(low_ready, n * 2)
                    sp.dma_start(raw[:, :], w[bass.ds(n, 1), :, :].rearrange("a p k -> (a p) k")).then_inc(loaded, 16)

            @block.tensor
            def _(pe):
                def pairs(i, first):
                    for s in (0, 1):
                        if not first:
                            pe.wait_ge(sides, i * 8 + (4 * s - 4))
                        for g in (0, 1):
                            pe.wait_ge(low_ready, i * 4 + (2 * s + g + 1))
                            for k in range(DT):
                                c = slice(k * P, (k + 1) * P)
                                nc.tensor.matmul(ps[:, s, g, :], wh[:, g, c], high[:, k, :], start=(k == 0), stop=False)
                                nc.tensor.matmul(ps[:, s, g, :], wh[:, g, c], low[:, k, :], start=False, stop=False)
                                mm = nc.tensor.matmul(ps[:, s, g, :], wl[:, g, c], high[:, k, :], start=False, stop=(k == DT - 1))
                            mm.then_inc(product, 1)

                pairs(0, True)
                with pe.Fori(1, PAIRS) as i:
                    pairs(i, False)

            @block.scalar
            def _(act):
                def high_parts(n, first=False):
                    act.wait_ge(loaded, n * 16 + 16)
                    for g in (0, 1):
                        if not first:
                            act.wait_ge(product, n * 2 + (g - 1))
                        nc.scalar.activation(wh[:, g, :], raw[:, g * HALF:(g + 1) * HALF], ACT.Copy).then_inc(high_ready, 1)

                def finish(n, s):
                    for g in (0, 1):
                        act.wait_ge(product, n * 2 + (g + 1))
                        nc.scalar.activation(cv[:, g, :], ps[:, s, g, :], ACT.Identity,
                                             bias=K.cols[:, bass.ds(n + (bcol + FT * g), 1)],
                                             scale=K.cols[:, bass.ds(n + (wcol + 2 * FT + FT * g), 1)]).then_inc(centre, 1)
                    act.wait_ge(sides, n * 4 + 4)
                    nc.scalar.activation(sg[:, :], cv[:, 0, :], ACT.Silu).then_inc(silu, 1)
                    act.wait_ge(full, n + 1)
                    nc.scalar.activation(out_high[:, bass.ds(n, 1), :], sg[:, :].unsqueeze(1), ACT.Copy).then_inc(done, 1)

                high_parts(0, True)
                high_parts(1)
                finish(0, 0)
                with act.Fori(1, PAIRS) as i:
                    high_parts(i * 2)
                    finish(i * 2 - 1, 1)
                    high_parts(i * 2 + 1)
                    finish(i * 2, 0)
                finish(FT - 1, 1)

            @block.vector
            def _(dve):
                def low_parts(n):
                    for g in (0, 1):
                        dve.wait_ge(high_ready, n * 2 + (g + 1))
                        nc.vector.tensor_tensor(wl[:, g, :], raw[:, g * HALF:(g + 1) * HALF], wh[:, g, :], ALU.subtract).then_inc(low_ready, 1)

                def finish(n, s):
                    for g in (0, 1):
                        dve.wait_ge(centre, n * 2 + (g + 1))
                        nc.vector.scalar_tensor_tensor(cv[:, g, 1:S], ps[:, s, g, 0:S - 1], K.cols[:, bass.ds(n + (wcol + FT * g), 1)],
                                                       cv[:, g, 1:S], ALU.mult, ALU.add).then_inc(sides, 1)
                    for g in (0, 1):
                        dve.wait_ge(sides, n * 4 + (g + 1))
                        nc.vector.scalar_tensor_tensor(cv[:, g, 0:S - 1], ps[:, s, g, 1:S],
                                                       K.cols[:, bass.ds(n + (wcol + 4 * FT + FT * g), 1)],
                                                       cv[:, g, 0:S - 1], ALU.mult, ALU.add).then_inc(sides, 1)
                    dve.wait_ge(sides, n * 4 + 4)
                    dve.wait_ge(silu, n + 1)
                    nc.vector.tensor_tensor(sg[:, :], cv[:, 1, :], sg[:, :], ALU.mult).then_inc(full, 1)
                    dve.wait_ge(full, n + 1)
                    dve.wait_ge(done, n + 1)
                    nc.vector.tensor_tensor(out_low[:, bass.ds(n, 1), :], sg[:, :].unsqueeze(1), out_high[:, bass.ds(n, 1), :],
                                            ALU.subtract).then_inc(done_low, 1)
                    dve.wait_ge(done_low, n + 1)

                low_parts(0)
                low_parts(1)
                finish(0, 0)
                with dve.Fori(1, PAIRS) as i:
                    low_parts(i * 2)
                    finish(i * 2 - 1, 1)
                    low_parts(i * 2 + 1)
                    finish(i * 2, 0)
                finish(FT - 1, 1)


def second_layer(K, a, layer, x, cs, sn):
    with ExitStack() as ctx:
        y = K.sb(ctx, "mix", [P, MIX_TILES, S])
        t = tiles(y, MIX_TILES)
        w = a["w_in_2"][layer]
        with parts_of(K, x) as parts:
            differential(K, layer, parts, w[0:12], cs, sn, t[0:4])
            memory(K, parts, w[32:36], a["w_mem_kv_2"][layer], a["mem_2"], t[8:12])
            hgrn(K, layer, parts, w[12:32], y[:, 4:8, :])
        with parts_of(K, y) as (high, low):
            project(K, a["w_out_2"][layer], DT, MIX_TILES, high, low, S, x, residual=x, alpha=ALPHA2)
    normalise(K, [tiles(x)], [tiles(x)], K.c("mean1024"), 1e-5, True, lambda t: K.col("ln1_g_2", 8 * layer + t),
              bias=lambda t: K.col("ln1_b_2", 8 * layer + t))
    with ExitStack() as ctx:
        hh = K.sb(ctx, "h_high", [P, FT, S], F32R)
        hl = K.sb(ctx, "h_low", [P, FT, S], F32R)
        with parts_of(K, x) as (high, low):
            conv_up(K, layer, high, low, a["w_up_2"][layer], hh, hl)
        project(K, a["w_down_2"][layer], DT, FT, hh, hl, S, x, residual=x, alpha=ALPHA2, ring=2)
    normalise(K, [tiles(x)], [tiles(x)], K.c("mean1024"), 1e-5, True, lambda t: K.col("ln2_g_2", 8 * layer + t),
              bias=lambda t: K.col("ln2_b_2", 8 * layer + t))


def second_block(K, a, x):
    with ExitStack() as ctx:
        cs = K.sb(ctx, "cs", [P, S])
        sn = K.sb(ctx, "sn", [P, S])
        rope_tables(K, a["positions_2"], cs, sn)
        normalise(K, [tiles(x)], [tiles(x)], K.c("mean1024"), 1e-5, True, lambda t: K.col("ln_in_g_2", t),
                  bias=lambda t: K.col("ln_in_b_2", t))
        for layer in (0, 1):
            second_layer(K, a, layer, x, cs, sn)


def pack_experts(gu, down):
    up = gu.reshape(EXPERTS, 2, 4, P, 2, 4, 256).transpose(0, 5, 1, 3, 2, 4, 6)
    dn = down.reshape(EXPERTS, 2, 4, P, 2, 512).transpose(0, 1, 4, 3, 2, 5)
    w = np.empty((EXPERTS, CHUNKS, P, CW), gu.dtype)
    w[:, 0:8] = up.reshape(EXPERTS, 8, P, CW)
    w[:, 8:12] = dn.reshape(EXPERTS, 4, P, CW)
    return w


def lay_out(i):
    i = {k: np.asarray(v) for k, v in i.items()}
    rw = i["router_w"][0]
    return {
        "const": constants(), "cols": pack_columns(i), "x": fm(i["x"][0]), "p": fm(i["p"][0, 0]),
        "w_in": pack_w_in(i["w_in"][0]), "w_out": tiles_of(i["w_out"][0]),
        "gla_gate_up": i["gla_gate_up"][0],
        "rwkv_lora": np.concatenate([i["rwkv_w_up"][0], i["rwkv_a_up"][0], i["rwkv_g_up"][0]], 0),
        "router_w": np.ascontiguousarray(rw.reshape(DT, P, EXPERTS).transpose(1, 0, 2)), "router_b": i["router_b"],
        "exp_w": pack_experts(i["exp_w_gu"][0], i["exp_w_down"][0]),
        "exp_b_gu": np.ascontiguousarray(i["exp_b_gu"][0].reshape(EXPERTS, 2, 4, 256).transpose(0, 2, 1, 3)).reshape(EXPERTS, 2 * FE),
        "exp_b_down": i["exp_b_down"][0],
        "ple_gate_w": tiles_of(i["ple_gate_w"][0]), "ple_proj": tiles_of(i["ple_proj"][0]),
        "mem_2": fm(i["mem_2"][0]), "positions_2": i["positions_2"],
        "w_in_2": np.stack([tiles_of(w) for w in i["w_in_2"]]),
        "w_mem_kv_2": np.stack([tiles_of(w) for w in i["w_mem_kv_2"]]),
        "w_out_2": np.stack([tiles_of(w) for w in i["w_out_2"]]),
        "w_up_2": np.ascontiguousarray(i["w_up_2"].reshape(2, DT, P, 2, FT, P).transpose(0, 4, 2, 3, 1, 5)).reshape(2, FT, P, 2 * D),
        "w_down_2": np.stack([tiles_of(w) for w in i["w_down_2"]]),
    }


def scratch(nc, a):
    a["expert_rows"] = nc.dram_tensor("expert_rows", (2, EXPERTS, S), F32, kind="Internal").ap()
    a["bias_parts"] = nc.dram_tensor("bias_parts", (EXPERTS, 2, 2 * FE), F32, kind="Internal").ap()
    a["mixture_in"] = nc.dram_tensor("mixture_in", (P, DT, S), F32, kind="Internal").ap()


def build(nc, a, out):
    scratch(nc, a)
    with ExitStack() as ctx:
        const = ctx.enter_context(nc.sbuf_tensor("const", [P, CONST_W], F32))
        cols = ctx.enter_context(nc.sbuf_tensor("cols", [P, COLS_W], F32))
        x = ctx.enter_context(nc.sbuf_tensor("x", [P, DT, S], F32))
        K = Kit(nc, const, cols)
        load(K, [(const[:, :], a["const"]), (cols[:, :], a["cols"]), (x[:, :, :], a["x"])])
        first_block(K, a, x)
        second_block(K, a, x)
        with stage(nc, "stored") as (block, stored):
            @block.sync
            def _(sp):
                sp.dma_start(out, x[:, :, :]).then_inc(stored, 16)
                sp.wait_ge(stored, 16)


def kernel(**inputs):
    import concourse.bacc as bacc
    from concourse.bass_utils import run_bass_kernel_spmd

    arrays = lay_out(inputs)
    nc = bacc.Bacc("TRN2", target_bir_lowering=False, num_devices=1)
    a = {n: nc.dram_tensor(f"in_{n}", v.shape, mybir.dt.from_np(v.dtype), kind="ExternalInput").ap() for n, v in arrays.items()}
    out = nc.dram_tensor("out", (P, DT, S), F32, kind="ExternalOutput").ap()
    build(nc, a, out)
    r = run_bass_kernel_spmd(nc, [{f"in_{n}": v for n, v in arrays.items()}], core_ids=[0])
    y = r.results[0]["out"]
    return np.ascontiguousarray(np.asarray(y).transpose(2, 1, 0)).reshape(1, S, D)
```
